# Optimizing a Trainium2 kernel written in Bass

```python
import math
import jax, jax.numpy as jnp
from jax import lax
import numpy as np

D_MODEL = 1024
BATCH = 1
SEQ = 512
DEPTH = 2
DEC_BATCH = 8
DEC_SEQ = 16
PAST_LEN = 256

CHUNK = 64
QBLOCK = 128
D_PLE = 256
D_FF = 2816
EPS = 1e-6
N_NORMS = 8
N_EVEN = (DEPTH + 1) // 2
N_ODD = DEPTH // 2

SB_HEADS = 8
SB_HD = 64
DF_HEADS = 4
DF_HD = 64
DF_ROT = DF_HD // 4
ROPE_THETA = 500000.0
MLA_HEADS = 16
MLA_NOPE = 64
MLA_ROPE = 32
MLA_VD = 64
Q_LORA = 384
KV_LORA = 256
MLA_THETA = 10000.0

SB_W = SB_HEADS * SB_HD
DF_QK_W = DF_HEADS * 2 * DF_HD
DF_V_W = DF_HEADS * 2 * DF_HD
AB_IN = 3 * SB_W + 2 * DF_QK_W + DF_V_W
AB_OUT = SB_W + DF_V_W
MLA_QD = MLA_NOPE + MLA_ROPE
MLA_IN = Q_LORA + KV_LORA + MLA_ROPE

kernel_name = 'stickbreak_diff_mla_macaron_stream'

def _rms(x, g):
    x32 = x.astype(jnp.float32)
    y = x32 * lax.rsqrt(jnp.mean(x32 * x32, axis=-1, keepdims=True) + EPS)
    return (y * g.astype(jnp.float32)).astype(x.dtype)

def _rope(x, pos, rot, theta):
    half = rot // 2
    inv = jnp.float32(theta) ** (-(jnp.arange(half, dtype=jnp.float32) * (2.0 / rot)))
    ang = pos.astype(jnp.float32)[:, None] * inv[None, :]
    shape = (1, pos.shape[0]) + (1,) * (x.ndim - 3) + (half,)
    cos = jnp.cos(ang).reshape(shape)
    sin = jnp.sin(ang).reshape(shape)
    xf = x.astype(jnp.float32)
    x1 = xf[..., :half]
    x2 = xf[..., half:rot]
    out = jnp.concatenate([x1 * cos - x2 * sin, x2 * cos + x1 * sin, xf[..., rot:]], axis=-1)
    return out.astype(x.dtype)

def _swiglu(x, w_gu, w_dn):
    g, u = jnp.split(x @ w_gu, 2, axis=-1)
    return (jax.nn.silu(g) * u) @ w_dn

def _sweep(block_fn, q_pos, *qs):
    T = q_pos.shape[0]
    qb = QBLOCK if T % QBLOCK == 0 else T
    nb = T // qb

    def split(a):
        return jnp.moveaxis(a.reshape((a.shape[0], nb, qb) + a.shape[2:]), 1, 0)

    out = lax.map(lambda args: block_fn(*args), (q_pos.reshape(nb, qb),) + tuple(split(a) for a in qs))
    out = jnp.moveaxis(out, 0, 1)
    return out.reshape((out.shape[0], T) + out.shape[3:])

def _chunk_visible(pb, k_pos):
    return (k_pos[None, :] // CHUNK) <= (pb[:, None] // CHUNK)

def _stick_breaking(q, k, v, q_pos, k_pos):
    scale = SB_HD ** -0.5

    def block(pb, qb_):
        z = jnp.einsum('bqhd,bkhd->bhqk', qb_, k).astype(jnp.float32) * scale
        earlier = k_pos[None, :] < pb[:, None]
        log_fail = jnp.where(earlier, jax.nn.log_sigmoid(-z), 0.0)
        between = lax.cumsum(log_fail, axis=3, reverse=True) - log_fail
        w = jnp.where(earlier, jnp.exp(jax.nn.log_sigmoid(z) + between), 0.0)
        return jnp.einsum('bhqk,bkhd->bqhd', w.astype(v.dtype), v)

    return _sweep(block, q_pos, q)

def _diff_attn(q, k, v, q_pos, k_pos, lam):
    scale = DF_HD ** -0.5

    def block(pb, qb_):
        s = jnp.einsum('bqhcd,bkhcd->bhcqk', qb_, k).astype(jnp.float32) * scale
        vis = _chunk_visible(pb, k_pos)
        pr = jax.nn.softmax(jnp.where(vis, s, -jnp.inf), axis=-1)
        w = pr[:, :, 0] - lam * pr[:, :, 1]
        return jnp.einsum('bhqk,bkhe->bqhe', w.astype(v.dtype), v)

    return _sweep(block, q_pos, q)

def _mla_attn(q_nope, q_rope, k_nope, k_rope, v, q_pos, k_pos):
    scale = MLA_QD ** -0.5

    def block(pb, qn, qr):
        s = (jnp.einsum('bqhd,bkhd->bhqk', qn, k_nope).astype(jnp.float32)
             + jnp.einsum('bqhr,bkr->bhqk', qr, k_rope).astype(jnp.float32)) * scale
        pr = jax.nn.softmax(jnp.where(_chunk_visible(pb, k_pos), s, -jnp.inf), axis=-1)
        return jnp.einsum('bhqk,bkhd->bqhd', pr.astype(v.dtype), v)

    return _sweep(block, q_pos, q_nope, q_rope)

def _mixer_ab(h, start, layer, w_in, w_out, lam_vecs, subln, cache):
    B, T, _ = h.shape
    pos = start + jnp.arange(T)
    k_pos = jnp.arange(start + T)
    proj = h @ w_in
    cuts = [SB_W, 2 * SB_W, 3 * SB_W, 3 * SB_W + DF_QK_W, 3 * SB_W + 2 * DF_QK_W]
    sb_q, sb_k, sb_v, df_q, df_k, df_v = jnp.split(proj, cuts, axis=-1)
    sb_q = sb_q.reshape(B, T, SB_HEADS, SB_HD)
    sb_k = sb_k.reshape(B, T, SB_HEADS, SB_HD)
    sb_v = sb_v.reshape(B, T, SB_HEADS, SB_HD)
    df_q = _rope(df_q.reshape(B, T, DF_HEADS, 2, DF_HD), pos, DF_ROT, ROPE_THETA)
    df_k = _rope(df_k.reshape(B, T, DF_HEADS, 2, DF_HD), pos, DF_ROT, ROPE_THETA)
    df_v = df_v.reshape(B, T, DF_HEADS, 2 * DF_HD)
    new = (sb_k, sb_v, df_k, df_v)
    if cache is None:
        ks = new
    else:
        ks = tuple(jnp.concatenate([c, n], axis=1) for c, n in zip(cache, new))
    sb_out = _stick_breaking(sb_q, ks[0], ks[1], pos, k_pos)
    lam_init = 0.8 - 0.6 * math.exp(-0.3 * layer)
    lv = lam_vecs.astype(jnp.float32)
    lam = jnp.exp(jnp.dot(lv[0], lv[1])) - jnp.exp(jnp.dot(lv[2], lv[3])) + lam_init
    df_out = _diff_attn(df_q, ks[2], ks[3], pos, k_pos, lam)
    df_out = _rms(df_out, subln) * (1.0 - lam_init)
    merged = jnp.concatenate([sb_out.reshape(B, T, SB_W), df_out.reshape(B, T, DF_V_W)], axis=-1)
    return merged @ w_out, new

def _mixer_mla(h, start, w_in, q_norm, kv_norm, w_uq, w_uk, w_uv, w_out, cache):
    B, T, _ = h.shape
    pos = start + jnp.arange(T)
    k_pos = jnp.arange(start + T)
    c_q, c_kv, k_r = jnp.split(h @ w_in, [Q_LORA, Q_LORA + KV_LORA], axis=-1)
    c_q = _rms(c_q, q_norm)
    c_kv = _rms(c_kv, kv_norm)
    q = (c_q @ w_uq).reshape(B, T, MLA_HEADS, MLA_QD)
    q_nope = q[..., :MLA_NOPE]
    q_rope = _rope(q[..., MLA_NOPE:], pos, MLA_ROPE, MLA_THETA)
    k_r = _rope(k_r, pos, MLA_ROPE, MLA_THETA)
    new = (c_kv, k_r)
    if cache is None:
        lat, kr = new
    else:
        lat = jnp.concatenate([cache[0], c_kv], axis=1)
        kr = jnp.concatenate([cache[1], k_r], axis=1)
    Tk = lat.shape[1]
    k_nope = (lat @ w_uk).reshape(B, Tk, MLA_HEADS, MLA_NOPE)
    v = (lat @ w_uv).reshape(B, Tk, MLA_HEADS, MLA_VD)
    out = _mla_attn(q_nope, q_rope, k_nope, kr, v, pos, k_pos)
    return out.reshape(B, T, MLA_HEADS * MLA_VD) @ w_out, new

def _trunk(x, p, start, caches, W):
    ab_rows, mla_rows = [], []
    for i in range(DEPTH):
        g = W['norms'][i]
        x = x + 0.5 * _rms(_swiglu(_rms(x, g[0]), W['ffn1_gu'][i], W['ffn1_dn'][i]), g[1])
        h = _rms(x, g[2])
        j = i // 2
        if i % 2 == 0:
            c = None if caches is None else tuple(a[j] for a in caches[:4])
            m, rows = _mixer_ab(h, start, i, W['ab_in'][j], W['ab_out'][j], W['df_lambda'][j], W['df_subln'][j], c)
            ab_rows.append(rows)
        else:
            c = None if caches is None else tuple(a[j] for a in caches[4:])
            m, rows = _mixer_mla(h, start, W['mla_in'][j], W['mla_q_norm'][j], W['mla_kv_norm'][j],
                                 W['mla_uq'][j], W['mla_uk'][j], W['mla_uv'][j], W['mla_out'][j], c)
            mla_rows.append(rows)
        x = x + _rms(m, g[3])
        x = x + 0.5 * _rms(_swiglu(_rms(x, g[4]), W['ffn2_gu'][i], W['ffn2_dn'][i]), g[5])
        gate = jax.nn.sigmoid(_rms(x, g[6]) @ W['ple_gate'][i])
        x = x + _rms(gate * (p[i] @ W['ple_in'][i]), g[7])
    sb_k, sb_v, df_k, df_v = [jnp.stack(r, axis=0) for r in zip(*ab_rows)]
    lat, kr = [jnp.stack(r, axis=0) for r in zip(*mla_rows)]
    return x, sb_k, sb_v, df_k, df_v, lat, kr

def setup_inputs(seed: int = 0) -> dict:
    key = jax.random.key(seed)
    ks = jax.random.split(key, 32)
    f32 = jnp.float32

    def w(k, shape, fan_in):
        return jax.random.normal(k, shape, f32) * (fan_in ** -0.5)

    def gain(k, shape):
        return 1.0 + 0.05 * jax.random.normal(k, shape, f32)

    return {
        'x_prompt': jax.random.normal(ks[0], (BATCH, SEQ, D_MODEL), f32),
        'x_sample': jax.random.normal(ks[1], (DEC_BATCH, DEC_SEQ, D_MODEL), f32),
        'p_prompt': jax.random.normal(ks[2], (DEPTH, BATCH, SEQ, D_PLE), f32),
        'p_sample': jax.random.normal(ks[3], (DEPTH, DEC_BATCH, DEC_SEQ, D_PLE), f32),
        'cache_sb_k': jax.random.normal(ks[4], (N_EVEN, DEC_BATCH, PAST_LEN, SB_HEADS, SB_HD), f32),
        'cache_sb_v': jax.random.normal(ks[5], (N_EVEN, DEC_BATCH, PAST_LEN, SB_HEADS, SB_HD), f32),
        'cache_df_k': jax.random.normal(ks[6], (N_EVEN, DEC_BATCH, PAST_LEN, DF_HEADS, 2, DF_HD), f32),
        'cache_df_v': jax.random.normal(ks[7], (N_EVEN, DEC_BATCH, PAST_LEN, DF_HEADS, 2 * DF_HD), f32),
        'cache_mla_latent': jax.random.normal(ks[8], (N_ODD, DEC_BATCH, PAST_LEN, KV_LORA), f32),
        'cache_mla_krope': jax.random.normal(ks[9], (N_ODD, DEC_BATCH, PAST_LEN, MLA_ROPE), f32),
        'norms': gain(ks[10], (DEPTH, N_NORMS, D_MODEL)),
        'ffn1_gu': w(ks[11], (DEPTH, D_MODEL, 2 * D_FF), D_MODEL),
        'ffn1_dn': w(ks[12], (DEPTH, D_FF, D_MODEL), D_FF),
        'ffn2_gu': w(ks[13], (DEPTH, D_MODEL, 2 * D_FF), D_MODEL),
        'ffn2_dn': w(ks[14], (DEPTH, D_FF, D_MODEL), D_FF),
        'ple_in': w(ks[15], (DEPTH, D_PLE, D_MODEL), D_PLE),
        'ple_gate': w(ks[16], (DEPTH, D_MODEL, D_MODEL), D_MODEL),
        'ab_in': w(ks[17], (N_EVEN, D_MODEL, AB_IN), D_MODEL),
        'ab_out': w(ks[18], (N_EVEN, AB_OUT, D_MODEL), AB_OUT),
        'df_lambda': 0.1 * jax.random.normal(ks[19], (N_EVEN, 4, DF_HD), f32),
        'df_subln': gain(ks[20], (N_EVEN, 2 * DF_HD)),
        'mla_in': w(ks[21], (N_ODD, D_MODEL, MLA_IN), D_MODEL),
        'mla_q_norm': gain(ks[22], (N_ODD, Q_LORA)),
        'mla_kv_norm': gain(ks[23], (N_ODD, KV_LORA)),
        'mla_uq': w(ks[24], (N_ODD, Q_LORA, MLA_HEADS * MLA_QD), Q_LORA),
        'mla_uk': w(ks[25], (N_ODD, KV_LORA, MLA_HEADS * MLA_NOPE), KV_LORA),
        'mla_uv': w(ks[26], (N_ODD, KV_LORA, MLA_HEADS * MLA_VD), KV_LORA),
        'mla_out': w(ks[27], (N_ODD, MLA_HEADS * MLA_VD, D_MODEL), MLA_HEADS * MLA_VD),
    }

def reference(x_prompt, x_sample, p_prompt, p_sample, cache_sb_k, cache_sb_v, cache_df_k, cache_df_v,
              cache_mla_latent, cache_mla_krope, norms, ffn1_gu, ffn1_dn, ffn2_gu, ffn2_dn, ple_in, ple_gate,
              ab_in, ab_out, df_lambda, df_subln, mla_in, mla_q_norm, mla_kv_norm, mla_uq, mla_uk, mla_uv, mla_out):
    W = dict(norms=norms, ffn1_gu=ffn1_gu, ffn1_dn=ffn1_dn, ffn2_gu=ffn2_gu, ffn2_dn=ffn2_dn,
             ple_in=ple_in, ple_gate=ple_gate, ab_in=ab_in, ab_out=ab_out, df_lambda=df_lambda,
             df_subln=df_subln, mla_in=mla_in, mla_q_norm=mla_q_norm, mla_kv_norm=mla_kv_norm,
             mla_uq=mla_uq, mla_uk=mla_uk, mla_uv=mla_uv, mla_out=mla_out)
    (y_prompt, sb_k_p, sb_v_p, df_k_p, df_v_p, lat_p, kr_p) = _trunk(x_prompt, p_prompt, 0, None, W)
    caches = (cache_sb_k, cache_sb_v, cache_df_k, cache_df_v, cache_mla_latent, cache_mla_krope)
    past = cache_sb_k.shape[2]
    (y_sample, sb_k_s, sb_v_s, df_k_s, df_v_s, lat_s, kr_s) = _trunk(x_sample, p_sample, past, caches, W)
    return (y_prompt, y_sample, sb_k_p, sb_v_p, df_k_p, df_v_p, lat_p, kr_p,
            sb_k_s, sb_v_s, df_k_s, df_v_s, lat_s, kr_s)


_drawn_inputs = setup_inputs


def setup_inputs(seed=0):
    import zlib

    import numpy as np

    out = dict(_drawn_inputs(seed))
    spreads = {}
    factors = {}
    for name, (base, spread) in spreads.items():
        noise = np.random.default_rng([zlib.crc32(name.encode()), seed]).standard_normal(out[name].shape)
        drawn = base * np.exp(spread * noise) if base else spread * noise
        out[name] = __import__('jax').numpy.asarray(drawn.astype(out[name].dtype))
    for name, factor in factors.items():
        out[name] = (out[name] * factor).astype(out[name].dtype)
    return out
```

```python
from contextlib import ExitStack
import math

import numpy as np

import concourse.bass as bass
from concourse import mybir

F32 = mybir.dt.float32
F32R = mybir.dt.float32r
ALU = mybir.AluOpType
ACT = mybir.ActivationFunctionType
AX_X = mybir.AxisListType.X

P = 128
D = 1024
KD = D // P
PROMPT = 512
DEC_B, DEC_T = 8, 16
PAST = 256
TILES = PROMPT // P + DEC_B * DEC_T // P
PT = PROMPT // P
TOK = TILES * P
DEPTH = 2
D_FF = 2816
D_PLE = 256
EPS = 1e-6
N_NORMS = 8
HALF = 512

FB = D_FF // P // 2
GA = 3 * P
GB = TOK - GA
GU_PIECES = 4
CH = FB

SB_HEADS, HD = 8, 64
DF_HEADS = 4
DF_ROT = HD // 4
SB_W = SB_HEADS * HD
ROPE_THETA = 500000.0
MLA_HEADS, NOPE, ROPE, VD = 16, 64, 32, 64
QD = NOPE + ROPE
Q_LORA, KV_LORA = 384, 256
MLA_THETA = 10000.0
MLA_IN = Q_LORA + KV_LORA + ROPE
Z_MOST = 20.0
BIG = float(2.0 ** 100)


def const_map():
    widths = [("neg_tri", P), ("neg_ones", P), ("diag", P), ("batch_tri", P), ("cos_d", TILES * DF_ROT // 2),
              ("sin_d", TILES * DF_ROT // 2), ("comp0", 1), ("comp1", 1), ("merge", DF_HEADS * DEC_T), ("row_mask", P), ("col_mask", P),
              ("batch_mask", P), ("cos_m", TILES * ROPE // 2), ("sin_m", TILES * ROPE // 2)]
    out, n = {}, 0
    for name, w in widths:
        out[name] = (n, w)
        n += w
    out["end"] = n
    return out


CONSTS = const_map()


def positions():
    return np.concatenate([np.arange(PROMPT), np.tile(PAST + np.arange(DEC_T), DEC_B)]).astype(np.float32)


def rope_table(rot, theta):
    half = rot // 2
    inv = np.float32(theta) ** (-(np.arange(half, dtype=np.float32) * np.float32(2.0 / rot)))
    ang = positions()[:, None] * inv.astype(np.float32)[None, :]
    lay = lambda a: a.reshape(TILES, P, half).transpose(1, 0, 2).reshape(P, TILES * half).astype(np.float32)
    return lay(np.cos(ang)), lay(np.sin(ang))


def const_table():
    t = np.zeros((P, CONSTS["end"]), np.float32)

    def put(name, value, rows=P):
        a, n = CONSTS[name]
        t[0:rows, a:a + n] = value

    k, q = np.arange(P)[:, None], np.arange(P)[None, :]
    put("neg_tri", -(k >= q).astype(np.float32))
    put("neg_ones", -1.0)
    put("diag", k < q)
    put("batch_tri", (k // DEC_T == q // DEC_T) & (k % DEC_T < q % DEC_T))
    cos, sin = rope_table(DF_ROT, ROPE_THETA)
    put("cos_d", cos)
    put("sin_d", sin)
    cos, sin = rope_table(ROPE, MLA_THETA)
    put("cos_m", cos)
    put("sin_m", sin)
    put("comp0", (k // DEC_T) % 2 == 0)
    put("comp1", (k // DEC_T) % 2 == 1)
    ht = np.arange(DF_HEADS * DEC_T)[None, :]
    put("merge", (k // (2 * DEC_T) == ht // DEC_T) & (k % DEC_T == ht % DEC_T))
    put("row_mask", np.where(q < P // 2, -BIG, 0.0), 1)
    put("col_mask", q >= P // 2, 1)
    put("batch_mask", np.where(np.arange(DEC_B)[:, None] == q // DEC_T, 0.0, -BIG), DEC_B)
    return t


def encoder(nc, io):
    ctx = ExitStack()
    with ctx:
        def sem(name):
            return ctx.enter_context(nc.semaphore(name))

        base0 = (nc.sbuf_base + 31) // 32 * 32
        cursor = [base0]

        def region(nbytes):
            start = cursor[0]
            cursor[0] += (nbytes + 31) // 32 * 32
            return start

        def place(name, shape, dt, offset):
            return nc.alloc_sbuf_tensor_at(name, shape, dt, offset=offset)

        X = place("x_rows", [P, TILES, D], F32, region(TILES * D * 4))
        r_xt = region(2 * KD * TOK * 4)
        XT = [place("xt_hi", [P, KD, TOK], F32R, r_xt), place("xt_lo", [P, KD, TOK], F32R, r_xt + KD * TOK * 4)]
        r_y = region(TILES * D * 4)
        Y = place("y_rows", [P, TILES, D], F32, r_y)
        r_h = region(2 * FB * TOK * 4)
        HT = [place("ht_hi", [P, FB, TOK], F32R, r_h), place("ht_lo", [P, FB, TOK], F32R, r_h + FB * TOK * 4)]
        r_gu = region(2 * GU_PIECES * HALF * 4)
        gu_raw = place("gu_raw", [P, GU_PIECES, 4, P], F32, r_gu)
        gu_lo = place("gu_lo", [P, GU_PIECES, 4, P], F32R, r_gu)
        gu_hi = place("gu_hi", [P, GU_PIECES, 4, P], F32R, r_gu + GU_PIECES * HALF * 4)
        r_ch = region(2 * CH * HALF * 4)
        ch_raw = place("ch_raw", [P, CH, HALF], F32, r_ch)
        ch_lo = place("ch_lo", [P, CH, HALF], F32R, r_ch)
        ch_hi = place("ch_hi", [P, CH, HALF], F32R, r_ch + CH * HALF * 4)
        g_post = place("g_post", [P, D], F32, region(D * 4))
        g_pre = place("g_pre", [P, D], F32, region(D * 4))
        SG = place("silu_gate", [P, TOK], F32, region(TOK * 4))
        ident = place("ident", [P, P], F32, region(P * 4))
        ssq = place("ssq", [P, TILES, 4], F32, region(TILES * 4 * 4))
        rs = place("rs", [P, TILES, 2], F32, region(TILES * 2 * 4))
        minus_half = place("minus_half", [P, 1], F32, region(4))
        one = place("one", [P, 1], F32, region(4))
        eps_col = place("eps_col", [P, 1], F32, region(4))
        at_cols = place("at_cols", [P, 4, 4], F32, region(64))
        assert cursor[0] <= nc.sbuf_usable_end, (cursor[0], nc.sbuf_usable_end)

        p_raw = place("p_raw", [P, TILES, D_PLE], F32, r_h)
        PTT = [place(f"pt_{w}", [P, D_PLE // P, TOK], F32R, r_h + 5120 * (i + 1)) for i, w in enumerate(("hi", "lo"))]
        GT = place("gate", [P, 2, HALF], F32, r_h + 3 * 5120)

        def at_y(name, shape, offset):
            return place(name, shape, F32, r_y + offset)

        OT = place("mixed", [P, KD, TOK], F32, r_xt + KD * TOK * 4)
        rows_in = at_y("rows_in", [P, TILES, HALF], 0)
        QKV = {n: at_y(n, [P, 4, TOK] if n[3] != "v" else [P, TILES, HALF], 10240 * (i + 1))
               for i, n in enumerate(("sb_q", "sb_k", "sb_v", "df_q", "df_k", "df_v"))}
        k_raw = at_y("k_raw", [P, 2, 2, HALF], 71680)
        v_raw = at_y("v_raw", [P, 2, 2, HALF], 79872)
        consts = at_y("consts", [P, CONSTS["end"]], 88064)
        assert 88064 + 4 * CONSTS["end"] <= r_ch - r_y
        kt = place("kt", [P, 2, 4, PAST], F32, g_post.manual_sbuf_range[0])
        rope_tmp = place("rope_tmp", [P, 4, 128], F32, SG.manual_sbuf_range[0])
        sp_buf = place("sp_buf", [P, 2, 1280], F32, r_xt)
        e_buf = place("e_buf", [P, 2, HALF], F32, r_xt + 10240)
        w_buf = place("w_buf", [P, 2, HALF], F32, r_xt + 14336)
        p_buf = place("p_buf", [P, 2, HALF], F32, r_xt)
        pt_buf = place("pt_buf", [P, 2, HALF], F32, r_xt + 4096)
        qbd = {n: at_y("qbd_" + n, [P, 4, DEC_B, 2, DEC_T], 4096 * i) for i, n in enumerate(("sb_q", "df_q"))}
        lam_rows = place("lam_rows", [P, 4, HD], F32, r_xt + 18432)
        lam_cols = place("lam_cols", [P, 8], F32, r_xt + 19456)
        subln_tmp = place("subln_tmp", [P, 2, TOK], F32, r_xt + 12288)

        c_in = at_y("c_in", [P, TILES, MLA_IN], 0)
        V = at_y("mla_v", [P, PT, MLA_HEADS * VD], 0)
        OLT = at_y("out_latent_t", [P, DEC_B, 2, 2, P], 0)
        CQT = [place(f"cq_t_{w}", [P, Q_LORA // P, TOK], F32R, r_y + 16384 + 7680 * i) for i, w in enumerate(("hi", "lo"))]
        q_lat_t = at_y("q_latent_t", [P, 2, DEC_B, MLA_HEADS, DEC_T], 16384)
        lat_t = at_y("latent_t", [P, 2, TOK], 32768)
        kr_t = at_y("krope_t", [P, TOK], 37888)
        lat_new = at_y("latent_new", [P, KV_LORA], 40448)
        W_uk = at_y("w_uk", [P, 2, MLA_HEADS * NOPE], 41472)
        at_q = 49664
        q_t = at_y("q_t", [P, MLA_HEADS, TOK], at_q)
        W_uv = [at_y(f"w_uv{i}", [P, 2, MLA_HEADS * VD], at_q) for i in range(2)]
        sq_tmp = at_y("sq_tmp", [P, 2, Q_LORA], at_q + 8192)
        lat_raw = at_y("lat_raw", [P, 3, 2, KV_LORA], at_q + 8192)
        kr_raw = at_y("kr_raw", [P, 3, 2, ROPE], at_q + 14336)
        lat_bt = at_y("lat_bt", [P, 2, 2, PAST], at_q + 15360)
        kr_bt = at_y("kr_bt", [P, 2, PAST], at_q + 19456)
        m_first, m_end = CONSTS["row_mask"][0], CONSTS["end"]
        m_consts = at_y("m_consts", [P, m_end - m_first], 90624)
        assert at_q + 4 * MLA_HEADS * TOK <= 90624 and 90624 + 4 * (m_end - m_first) <= r_ch - r_y
        q_rows = place("q_rows", [P, TILES, 4 * QD], F32, r_xt)
        k_t = place("k_t", [P, 2, PROMPT], F32, r_xt + 8192)
        qr_t = place("q_rope_t", [P, DEC_B, MLA_HEADS, DEC_T], F32, r_xt + 12288)
        g0 = g_post.manual_sbuf_range[0]
        mg_q = place("mg_q", [P, Q_LORA], F32, g0)
        mg_kv = place("mg_kv", [P, KV_LORA], F32, g0 + 4 * Q_LORA)
        w_ukt = place("w_ukt", [P, 2, 2 * P], F32, g0 + 2560)
        mc = place("mc_cols", [P, 2, TILES, 2], F32, g0 + 4608)

        def const(name, rows=P):
            a, n = CONSTS[name]
            return consts[0:rows, a:a + n]

        def mconst(name, rows=P):
            a, n = CONSTS[name]
            return m_consts[0:rows, a - m_first:a - m_first + n]

        PS = ctx.enter_context(nc.psum_tensor("ps", [P, 8, HALF], F32))
        Y_BANK = [0, 4, 5, 6, 7]
        TR_BANK = [(1, 2), (3, 7)]
        GATE_A, GATE_B, UP_A, UP_B = 4, 5, 6, 7

        x_in = [sem(f"x_in{t}") for t in range(TILES)]
        gains_in = sem("gains_in")
        const_ok = sem("const_ok")
        gu_landed = [sem(f"gu_landed{s}") for s in range(GU_PIECES)]
        gu_hi_ok, gu_lo_ok, gu_used = sem("gu_hi_ok"), sem("gu_lo_ok"), sem("gu_used")
        ch_landed = [sem(f"ch_landed{c}") for c in range(CH)]
        ch_hi_ok, ch_lo_ok, ch_used = sem("ch_hi_ok"), sem("ch_lo_ok"), sem("ch_used")
        y_mm, y_out, y_zero = sem("y_mm"), sem("y_out"), sem("y_zero")
        gate_mm, up_mm = sem("gate_mm"), sem("up_mm")
        silu_ok, h_mul, h_hi_ok, sg_free = sem("silu_ok"), sem("h_mul"), sem("h_hi_ok"), sem("sg_free")
        ss1_ok, ss2_ok = sem("ss1_ok"), sem("ss2_ok")
        eps_ok, rs1_ok, rs2_ok = sem("eps_ok"), sem("rs1_ok"), sem("rs2_ok")
        post_ok, x_ok, xn_ok = sem("post_ok"), sem("x_ok"), sem("xn_ok")
        tr_ok, xt_hi_ok, xt_lo_ok = sem("tr_ok"), sem("xt_hi_ok"), sem("xt_lo_ok")
        ple = {k: sem(f"ple_{k}") for k in ("in", "tr", "hi", "lo", "gate", "pin")}
        out_done = sem("out_done")
        consts_in = sem("consts_in")
        st_ok, rope_part, rope_ok, st_tr, st_cp = (sem(n) for n in ("st_ok", "rope_part", "rope_ok", "st_tr", "st_cp"))
        st_out = {n: sem("st_out_" + n) for n in ("sb_k", "sb_v", "df_k", "df_v", "lat", "kr")}
        kraw_in = [sem(f"kraw_in{b}") for b in range(2)]
        vraw_in = [sem(f"vraw_in{b}") for b in range(2)]
        kt_tr, kt_ok = sem("kt_tr"), sem("kt_ok")
        sb_z, sb_min, sb_exp, sb_ln, sb_sp, sb_spm, sb_acc, sb_w, sb_wm, sb_pv = (
            sem("sb_" + n) for n in ("z", "min", "exp", "ln", "sp", "spm", "acc", "w", "wm", "pv"))
        at_s, at_max, at_exp, at_r, at_p, at_t, at_pt, at_pv, o_out = (
            sem(n) for n in ("at_s", "at_max", "at_exp", "at_r", "at_p", "at_t", "at_pt", "at_pv", "o_out"))
        lam_in, lam_step, qbd_ok = sem("lam_in"), sem("lam_step"), sem("qbd_ok")
        sub_sq, sub_mm, sub_ln, sub_rs, sub_ok = (sem("sub_" + n) for n in ("sq", "mm", "ln", "rs", "ok"))
        ot_hi, ot_lo = sem("ot_hi"), sem("ot_lo")
        mg_in, mw_in, muv_in = sem("mg_in"), sem("mw_in"), [sem(f"muv_in{i}") for i in range(2)]
        mc_ss, mc_eps, mc_rs, mc_n, mc_tr, mc_hi, mc_lo, mc_lat = (
            sem("mc_" + n) for n in ("ss", "eps", "rs", "n", "tr", "hi", "lo", "lat"))
        v_mm, v_ok, mq_tr, mq_cp, qr_cp, krt_cp, wt_tr, wt_cp, ql_mm, ql_cp, uo_mm, uo_ok, new_cp = (
            sem(n) for n in ("v_mm", "v_ok", "mq_tr", "mq_cp", "qr_cp", "krt_cp", "wt_tr", "wt_cp", "ql_mm", "ql_cp",
                             "uo_mm", "uo_ok", "new_cp"))
        lat_in = [sem(f"lat_in{b}") for b in range(3)]

        passes = []

        def new_pass(K, src):
            passes.append({"i": len(passes), "K": K, "n": src.shape[1] if src is not None else HALF, "src": src,
                           "uses": [sum(q["K"] > c for q in passes) for c in range(CH)]})
            return passes[-1]

        def col_half(w, h):
            return w[:, h * HALF:(h + 1) * HALF]

        stages = [{"kind": "start", "passes": []}]
        for kind, layer, which in io["plan"]:
            st = {"kind": kind, "layer": layer}
            if kind == "ffn":
                st["n"] = sum(q["kind"] == "ffn" for q in stages)
                st["gu"], st["dn"] = io[f"ffn{which}_gu"][layer], io[f"ffn{which}_dn"][layer]
                st["passes"] = [new_pass(FB, None) for _ in range(4)]
                st["g"], st["c"] = (1 if which == 1 else 5), 0.5
            elif kind == "ple":
                st["n"] = sum(q["kind"] == "ple" for q in stages)
                st["passes"] = [new_pass(D_PLE // P, col_half(io["ple_in"][layer], h)) for h in range(2)]
                st["passes"] += [new_pass(KD, col_half(io["ple_gate"][layer], h)) for h in range(2)]
                st["g"], st["c"] = 7, 1.0
            elif kind == "ab":
                st["passes"] = [new_pass(KD, col_half(io["ab_in"][0], h)) for h in range(6)]
                st["passes"] += [new_pass(KD, col_half(io["ab_out"][0], h)) for h in range(2)]
                st["g"], st["c"] = 3, 1.0
            elif kind == "mla":
                w = io["mla_in"][0]
                st["passes"] = [new_pass(KD, w[:, 0:HALF]), new_pass(KD, w[:, HALF:MLA_IN])]
                st["passes"] += [new_pass(Q_LORA // P, io["mla_uq"][0][:, g * 4 * QD:(g + 1) * 4 * QD])
                                 for g in range(MLA_HEADS // 4)]
                st["passes"] += [new_pass(KD, col_half(io["mla_out"][0], h)) for h in range(2)]
                st["g"], st["c"] = 3, 1.0
            stages.append(st)
        for k, st in enumerate(stages):
            st["zero_y"] = k + 1 < len(stages) and stages[k + 1]["kind"] in ("ffn", "ple")
            st["k"] = k
            if k > 0:
                st["post"] = io["norms"][st["layer"], st["g"]]
                nxt = (st["layer"], st["g"] + 1) if st["g"] < 7 else (st["layer"] + 1, 0)
            else:
                nxt = (io["plan"][0][1], {"ffn": 0, "ple": 6, "ab": 2, "mla": 2}[io["plan"][0][0]])
                if io["plan"][0][0] == "ffn" and io["plan"][0][2] == 2:
                    nxt = (nxt[0], 4)
            st["pre"] = None if k == len(stages) - 1 else io["norms"][nxt[0], nxt[1]]
            st["last"] = st["passes"][-1]["i"] if st["passes"] else None

        def ple_evict(b, part):
            if b < 2:
                return PTT[part][:, b, 0:PROMPT], PS[:, 5 + b, :]
            return PTT[part][:, :, PROMPT:TOK], PS[:, 7, 0:2 * P].rearrange("p (b n) -> p b n", b=2)

        def tok(t):
            return slice(t * P, (t + 1) * P)

        def counts(p, c, total=CH):
            last = p["K"] - 1 - (CH - total)
            return total - last if c == last else 1

        def prev_k(p):
            return passes[p["i"] - 1]["K"] if p["i"] else 2

        def summed(p, t):
            return TILES * (p + 1) + t + 1

        def evicted(p, t):
            return TILES * (p + 1) + t + 1

        Z_BANK = [3, 4, 5, 0]
        S_BANK = [4, 5]
        T_BANK = [1, 2]
        O_BANK = [6, 7]

        def prep_bank(pr, b):
            return (1, 2)[b] if pr["kind"] == "stick" else (0, 3)[b]

        stick = []
        soft = []
        groups = []
        preps = []

        def new_group(dst, bank_cols=HALF):
            groups.append({"i": len(groups), "dst": dst, "n": bank_cols})
            return groups[-1]

        mixers = [st for st in stages if st["kind"] in ("ab", "mla")]
        for st in mixers:
            st["soft0"], st["stick0"] = len(soft), len(stick)
            st["before"] = mixers.index(st)
            st["rot0"] = 2 * TILES if st["before"] else 0
            if st["kind"] == "ab":
                for h in range(SB_HEADS):
                    if h % 2 == 0:
                        g = new_group(OT[:, h // 2, 0:PROMPT])
                    for kb in reversed(range(PT)):
                        N = PROMPT - kb * P
                        r = slice(HD * (h % 2), HD * (h % 2) + HD)
                        off = [0, 512, 896, 1152]
                        stick.append({
                            "g": g, "N": N, "sp": sp_buf[:, h % 2, off[kb]:off[kb] + N], "prep": None,
                            "z": [(slice(0, N), QKV["sb_k"][r, h // 2, kb * P:kb * P + P],
                                   QKV["sb_q"][r, h // 2, kb * P:PROMPT])],
                            "later": [(slice((k2 - kb) * P, N), sp_buf[:, h % 2, off[k2]:off[k2] + PROMPT - k2 * P])
                                      for k2 in range(kb + 1, PT)],
                            "mask": (slice(0, P), None, "diag"),
                            "pv": [(r, slice(kb * P, PROMPT), QKV["sb_v"][:, kb, h * HD:h * HD + HD], slice(0, N),
                                    kb == PT - 1)],
                            "first": h % 2 == 0 and kb == PT - 1, "last": h % 2 == 1 and kb == 0})
                gs = new_group(OT[:, 0:4, PROMPT:TOK])
                for b in range(DEC_B):
                    preps.append({"i": len(preps), "k": io["cache_sb_k"][0, b], "v": io["cache_sb_v"][0, b],
                                  "kind": "stick", "unit": len(stick), "last": len(stick)})
                    pr = preps[-1]
                    par = pr["i"] % 2
                    z, pv = [], []
                    for fb in range(SB_HEADS // 2):
                        for kb in range(3):
                            c0 = kb * P + fb * 2 * DEC_T
                            key = kt[:, par, fb, kb * P:kb * P + P] if kb < 2 else QKV["sb_k"][:, fb, PROMPT:TOK]
                            z.append((slice(c0, c0 + 2 * DEC_T), key, qbd["sb_q"][:, fb, b].rearrange("p c t -> p (c t)")))
                    for h in range(SB_HEADS):
                        r = slice(HD * (h % 2), HD * (h % 2) + HD)
                        for kb in range(3):
                            c0 = kb * P + h * DEC_T
                            val = (v_raw[:, par, kb, :] if kb < 2 else QKV["sb_v"][:, PT, :])[:, h * HD:h * HD + HD]
                            pv.append((r, slice((h // 2) * P + b * DEC_T, (h // 2) * P + (b + 1) * DEC_T), val,
                                       slice(c0, c0 + DEC_T), kb == 0))
                    sp = sp_buf[:, b % 2, 0:3 * P]
                    stick.append({"g": gs, "N": 3 * P, "sp": sp, "prep": pr, "z": z, "pv": pv,
                                  "later": [(slice(0, P), sp[:, P:2 * P]), (slice(0, P), sp[:, 2 * P:3 * P]),
                                            (slice(P, 2 * P), sp[:, 2 * P:3 * P])],
                                  "mask": (slice(2 * P, 3 * P), b, "batch"),
                                  "first": b == 0, "last": b == DEC_B - 1})
                for h in range(DF_HEADS):
                    g = new_group(OT[:, 4 + h, 0:PROMPT])
                    for qb in range(PT):
                        for c in range(2):
                            r = slice(HD * c, HD * c + HD)
                            N = (qb + 1) * P
                            soft.append({
                                "g": g, "N": N, "prep": None, "coef": "neg_lam" if c else None,
                                "s": [(slice(0, P), slice(0, N), QKV["df_q"][r, h, qb * P:qb * P + P],
                                       QKV["df_k"][r, h, 0:N], True),
                                      (slice(0, P), slice(qb * P, N), const("row_mask", 1), const("col_mask", 1), False)],
                                "pv": [(slice(0, P), slice(qb * P, N), QKV["df_v"][:, j, h * P:h * P + P],
                                        (j * P, P), c == 0 and j == 0) for j in range(qb + 1)],
                                "first": qb == 0 and c == 0, "last": qb == PT - 1 and c == 1})
                gs = new_group(OT[:, 4:8, PROMPT:TOK])
                for b in range(DEC_B):
                    preps.append({"i": len(preps), "k": io["cache_df_k"][0, b], "v": io["cache_df_v"][0, b],
                                  "kind": "soft", "unit": len(soft), "last": len(soft)})
                    pr = preps[-1]
                    par = pr["i"] % 2
                    s_list, pv = [], []
                    for h in range(DF_HEADS):
                        ro = slice(32 * h, 32 * h + 32)
                        q = qbd["df_q"][:, h, b].rearrange("p c t -> p (c t)")
                        s_list.append((ro, slice(0, PAST), q, kt[:, par, h, :], True))
                        s_list.append((ro, slice(PAST, PAST + P), q, QKV["df_k"][:, h, PROMPT:TOK], False))
                        for j in range(3):
                            val = (v_raw[:, par, j, :] if j < 2 else QKV["df_v"][:, PT, :])[:, h * P:h * P + P]
                            pv.append((slice(0, P), slice(h * P + b * DEC_T, h * P + (b + 1) * DEC_T), val,
                                       (j * DF_HEADS * DEC_T + h * DEC_T, DEC_T), j == 0))
                    s_list.append((slice(0, P), slice(PAST, PAST + P), ident[0:DEC_B, b:b + 1].to_broadcast([DEC_B, P]),
                                   const("batch_mask", DEC_B), False))
                    soft.append({"g": gs, "N": PAST + P, "prep": pr, "coef": "c_rows", "s": s_list, "pv": pv,
                                 "first": b == 0, "last": b == DEC_B - 1})
            else:
                st["prep0"] = len(preps)
                for h in range(MLA_HEADS):
                    if h % 2 == 0:
                        g = new_group(OT[:, h // 2, 0:PROMPT])
                    preps.append({"i": len(preps), "kind": "head", "h": h, "unit": len(soft), "last": len(soft) + PT - 1})
                    for qb in range(PT):
                        N = (qb + 1) * P
                        r = slice(VD * (h % 2), VD * (h % 2) + VD)
                        soft.append({
                            "g": g, "N": N, "prep": preps[-1] if qb == 0 else None, "coef": None,
                            "s": [(slice(0, P), slice(0, N), q_t[0:QD, h, qb * P:qb * P + P], k_t[0:QD, h % 2, 0:N], True),
                                  (slice(0, P), slice(qb * P, N), mconst("row_mask", 1), mconst("col_mask", 1), False)],
                            "pv": [(r, slice(qb * P, N), V[:, j, h * VD:h * VD + VD], (j * P, P), j == 0)
                                   for j in range(qb + 1)],
                            "first": h % 2 == 0 and qb == 0, "last": h % 2 == 1 and qb == PT - 1})
                st["sample0"] = len(soft)
                for b in range(DEC_B):
                    g = new_group(OLT[:, b].rearrange("p a c n -> p (a c n)"))
                    preps.append({"i": len(preps), "kind": "latent", "b": b, "unit": len(soft), "last": len(soft) + 1})
                    for hh in range(2):
                        hs = slice(8 * hh, 8 * hh + 8)
                        ops = [(q_lat_t[:, c, b, hs, :].rearrange("p h t -> p (h t)"), lat_bt[:, b % 2, c, :],
                                lat_t[:, c, PROMPT:TOK]) for c in range(2)]
                        ops += [(qr_t[0:ROPE, b, hs, :].rearrange("p h t -> p (h t)"), kr_bt[0:ROPE, b % 2, :],
                                 kr_t[0:ROPE, PROMPT:TOK])]
                        s_list = []
                        for j, (q, old, new) in enumerate(ops):
                            s_list.append((slice(0, P), slice(0, PAST), q, old, j == 0))
                            s_list.append((slice(0, P), slice(PAST, PAST + P), q, new, False))
                        s_list.append((slice(0, P), slice(PAST, PAST + P), ident[0:DEC_B, b:b + 1].to_broadcast([DEC_B, P]),
                                       mconst("batch_mask", DEC_B), False))
                        pv = [(slice(0, P), slice(hh * 2 * P + c * P, hh * 2 * P + (c + 1) * P),
                               (lat_raw[:, b % 3, j, :] if j < 2 else lat_new[:])[:, c * P:(c + 1) * P], (j * P, P), j == 0)
                              for c in range(2) for j in range(3)]
                        soft.append({"g": g, "N": PAST + P, "prep": preps[-1] if hh == 0 else None, "coef": None,
                                     "s": s_list, "pv": pv, "first": hh == 0, "last": hh == 1})
            st["soft1"], st["stick1"], st["groups1"] = len(soft), len(stick), len(groups)
        for lst, kind in ((stick, "stick"), (soft, "soft")):
            for n, u in enumerate(lst):
                u["i"] = n
                u["w"] = DF_HEADS * DEC_T if u["prep"] and u["prep"]["kind"] == "soft" else P
                if u["last"]:
                    u["g"]["end"] = (kind, n)

        def flat(a):
            names = " ".join("abcd"[:len(a.shape) - 1])
            return a.rearrange(f"r {names} -> r ({names})") if len(a.shape) > 2 else a

        def groups_end(st):
            return st["groups1"]

        def mixed_done(st):
            return (sub_ok, DF_HEADS) if st["kind"] == "ab" else (uo_ok, 2)

        def keys_done(pr):
            return (sb_z if pr["kind"] == "stick" else at_s), pr["last"] + 1

        def unit_done(pr):
            return (sb_pv if pr["kind"] == "stick" else at_pv), pr["last"] + 1

        block = ctx.enter_context(nc.Block())

        @block.sync
        def _(sp):
            def load_gu(st, g):
                w = st["gu"].rearrange("(k p) n -> p k n", p=P)
                for s in range(GU_PIECES):
                    blk = g + st["n"] * 2 * FB
                    if s % 2 == 0:
                        sp.wait_ge(gu_used, blk * 2 + s // 2 + 1)
                    else:
                        sp.wait_ge(gate_mm if s == 1 else up_mm, blk * 2 + 2)
                    q, kh = s // 2, s % 2
                    sp.dma_start(gu_raw[:, s], w[:, kh * 4:kh * 4 + 4, bass.ds(g * P + q * D_FF, P)]
                                 ).then_inc(gu_landed[s], 16)

            def load_chunk(p, prev_k, c, src, n=HALF):
                if c < prev_k - 1:
                    sp.wait_ge(ch_used, p * (CH - 1) + c + 1)
                else:
                    sp.wait_ge(y_mm, p * TILES + TILES)
                sp.dma_start(ch_raw[:, c, 0:n], src).then_inc(ch_landed[c], 16)

            def load_preps(st):
                mine = [q for q in preps if q["kind"] in ("stick", "soft")]
                for n in range(len(mine) + 1):
                    if n < len(mine):
                        i, par = mine[n]["i"], mine[n]["i"] % 2
                        if i >= 2:
                            sp.wait_ge(kt_tr, 2 * (i - 1))
                        sp.dma_start(k_raw[:, par], flat(mine[n]["k"]).rearrange("(b p) n -> p b n", p=P)
                                     ).then_inc(kraw_in[par], 16)
                    if n > 0:
                        i, par = mine[n - 1]["i"], mine[n - 1]["i"] % 2
                        if i >= 2:
                            sp.wait_ge(*unit_done(preps[i - 2]))
                        sp.dma_start(v_raw[:, par], flat(mine[n - 1]["v"]).rearrange("(b p) n -> p b n", p=P)
                                     ).then_inc(vraw_in[par], 16)

            def load_pass(p):
                for c in range(p["K"]):
                    load_chunk(p["i"], prev_k(p), c, p["src"][c * P:(c + 1) * P, :], p["n"])

            def rows_out(name, src, done, n):
                sp.wait_ge(done, n)
                dst = io[name + "_out"]
                sp.dma_start(dst[0], src[:, 0:PT, :]).then_inc(st_out[name], 16)
                sp.dma_start(dst[1], src[:, PT, :]).then_inc(st_out[name], 16)

            for t in range(TILES):
                sp.dma_start(X[:, t, :], io["x_tiles"][t]).then_inc(x_in[t], 16)
            for st in stages:
                if st["kind"] == "ffn":
                    rows = st["dn"].rearrange("(f p) n -> p f n", p=P)
                    p0 = st["passes"][0]["i"]
                    with sp.Fori(0, 2) as fh:
                        load_gu(st, fh * FB)
                        for c in range(FB):
                            load_chunk(fh * 2 + p0, KD, c, rows[:, bass.ds(fh * FB + c, 1), 0:HALF].rearrange("p a n -> p (a n)"))
                            if c < FB - 1:
                                load_gu(st, fh * FB + c + 1)
                        for c in range(FB):
                            load_chunk(fh * 2 + p0 + 1, FB, c,
                                       rows[:, bass.ds(fh * FB + c, 1), HALF:D].rearrange("p a n -> p (a n)"))
                elif st["kind"] == "ab":
                    load_pass(st["passes"][0])
                    sp.wait_ge(y_mm, st["passes"][0]["i"] * TILES + TILES)
                    sp.dma_start(consts[:], io["consts"]).then_inc(consts_in, 16)
                    for q in range(1, 6):
                        load_pass(st["passes"][q])
                        p = st["passes"][q - 1]["i"]
                        if q == 2:
                            rows_out("sb_k", rows_in, y_out, evicted(p, TILES - 1))
                        if q == 3:
                            rows_out("sb_v", QKV["sb_v"], y_out, evicted(p, TILES - 1))
                        if q == 5:
                            rows_out("df_k", rows_in, rope_ok, 2 * 2 * TILES)
                    rows_out("df_v", QKV["df_v"], y_out, evicted(st["passes"][5]["i"], TILES - 1))
                    load_preps(st)
                    for q in (6, 7):
                        load_pass(st["passes"][q])
                elif st["kind"] == "mla":
                    ps = st["passes"]
                    w_uv = io["mla_uv"][0].rearrange("(k p) n -> p k n", p=P)
                    load_pass(ps[0])
                    sp.wait_ge(y_mm, ps[0]["i"] * TILES + TILES)
                    sp.dma_start(m_consts[:], io["consts"][:, m_first:m_end]).then_inc(mg_in, 16)
                    sp.wait_ge(xn_ok, TILES * st["k"])
                    sp.dma_start(mg_q[:], io["mla_q_norm"][0].partition_broadcast(P)).then_inc(mg_in, 16)
                    sp.dma_start(mg_kv[:], io["mla_kv_norm"][0].partition_broadcast(P)).then_inc(mg_in, 16)
                    load_pass(ps[1])
                    sp.dma_start(W_uv[0][:], w_uv).then_inc(muv_in[0], 16)
                    sp.dma_start(W_uk[:], io["mla_uk"][0].rearrange("(k p) n -> p k n", p=P)).then_inc(mw_in, 16)
                    load_pass(ps[2])
                    rows_out("lat", c_in[:, :, Q_LORA:Q_LORA + KV_LORA], mc_n, 2 * TILES)
                    rows_out("kr", c_in[:, :, Q_LORA + KV_LORA:MLA_IN], rope_ok, 2 * (st["rot0"] + TILES))
                    for p in ps[3:6]:
                        load_pass(p)
                    sp.wait_ge(at_s, st["sample0"])
                    lat, kr = (io["cache_mla_" + n][0].rearrange("b (k p) n -> b p k n", p=P) for n in ("latent", "krope"))
                    for b in range(DEC_B):
                        if b == 3:
                            sp.dma_start(W_uv[1][:], w_uv).then_inc(muv_in[1], 16)
                        if b >= 3:
                            sp.wait_ge(at_pv, st["sample0"] + 2 * (b - 2))
                        sp.dma_start(lat_raw[:, b % 3], lat[b]).then_inc(lat_in[b % 3], 16)
                        sp.dma_start(kr_raw[:, b % 3], kr[b]).then_inc(lat_in[b % 3], 16)
                    for p in ps[6:8]:
                        load_pass(p)
                elif st["kind"] == "ple":
                    for p in st["passes"]:
                        load_pass(p)
            for t in range(TILES):
                sp.wait_ge(x_ok, TILES * (len(stages) - 2) + t + 1)
                sp.dma_start(io["y_tiles"][t], X[:, t, :]).then_inc(out_done, 16)
            sp.wait_ge(out_done, 16 * TILES)
            for name in st_out:
                if any(st["kind"] == ("mla" if name in ("lat", "kr") else "ab") for st in stages):
                    sp.wait_ge(st_out[name], 2 * 16)

        @block.scalar
        def _(act):
            def hi_gu(blk):
                for s in range(GU_PIECES):
                    act.wait_ge(gu_landed[s], (blk + 1) * 16)
                    act.activation(gu_hi[:, s], gu_raw[:, s], ACT.Copy).then_inc(gu_hi_ok, 1)

            def hi_chunk(p, c, uses):
                act.wait_ge(ch_landed[c], (uses + 1) * 16)
                act.activation(ch_hi[:, c, 0:p["n"]], ch_raw[:, c, 0:p["n"]], ACT.Copy).then_inc(ch_hi_ok, counts(p, c))

            def silu(blk):
                for b, bank, cols in ((0, GATE_A, slice(0, GA)), (1, GATE_B, slice(GA, TOK))):
                    act.wait_ge(gate_mm, blk * 2 + b + 3)
                    act.wait_ge(sg_free, blk * 2 + b + 1)
                    act.activation(SG[:, cols], PS[:, bank, 0:cols.stop - cols.start], ACT.Silu).then_inc(silu_ok, 1)

            def load_gains(st):
                if st["k"] > 0:
                    act.wait_ge(xn_ok, TILES * st["k"])
                    act.dma_start(g_post[:], st["post"].partition_broadcast(P)).then_inc(gains_in, 16)
                if st["pre"] is not None:
                    act.dma_start(g_pre[:], st["pre"].partition_broadcast(P)).then_inc(gains_in, 16)

            def tail(st, ahead):
                k = st["k"]

                def squares(src, scale, t, first, own, own_n, before, before_n):
                    for h in range(2):
                        if h == 0 and before_n:
                            act.wait_ge(before, before_n)
                        if h == 1:
                            act.wait_ge(own, own_n + 1)
                        act.activation(SG[:, 0:HALF], src[:, t, h * HALF:(h + 1) * HALF], ACT.Square, scale=scale,
                                       accum_out=ssq[:, t, first + h:first + h + 1]).then_inc(own, 1)

                def sq1(t):
                    if ahead:
                        ahead(t)
                    act.wait_ge(y_out, evicted(st["last"], t))
                    n1, n2 = 2 * (TILES * (k - 1) + t), 2 * (TILES * k + t)
                    if st["pre"] is None and t > 0:
                        squares(Y, 1.0 / (math.sqrt(D) * st["c"]), t, 0, ss1_ok, n1, ss1_ok, n1)
                    else:
                        squares(Y, 1.0 / (math.sqrt(D) * st["c"]), t, 0, ss1_ok, n1, ss2_ok, n2)

                def sq2(t):
                    n1, n2 = 2 * (TILES * (k - 1) + t) + 2, 2 * (TILES * k + t)
                    if k > 0:
                        act.wait_ge(x_ok, TILES * (k - 1) + t + 1)
                        squares(X, 1.0 / math.sqrt(D), t, 2, ss2_ok, n2, ss1_ok, n1)
                    else:
                        act.wait_ge(x_in[t], 16)
                        squares(X, 1.0 / math.sqrt(D), t, 2, ss2_ok, n2, ss2_ok, n2)

                def hi(t):
                    for b in range(2):
                        act.wait_ge(tr_ok, 2 * (TILES * k + t) + b + 1)
                        act.activation(XT[0][:, 4 * b:4 * b + 4, tok(t)], PS[:, TR_BANK[t % 2][b], :], ACT.Copy
                                       ).then_inc(xt_hi_ok, 1)

                if k > 0 and st["kind"] == "ffn":
                    act.wait_ge(sg_free, 2 * 2 * FB * (st["n"] + 1) + 2)
                for t in range(TILES - 1):
                    if k > 0:
                        sq1(t)
                    if st["pre"] is not None:
                        sq2(t)
                if k > 0:
                    sq1(TILES - 1)
                if st["pre"] is not None:
                    hi(0)
                    hi(1)
                    sq2(TILES - 1)
                    for t in range(2, TILES):
                        hi(t)

            def copy_kt(pr):
                i, par = pr["i"], pr["i"] % 2
                if i >= 2:
                    act.wait_ge(*keys_done(preps[i - 2]))
                for b in range(2):
                    act.wait_ge(kt_tr, 2 * i + b + 1)
                    if pr["kind"] == "head":
                        dst, src = k_t[0:NOPE, pr["h"] % 2, b * 256:(b + 1) * 256], PS[0:NOPE, prep_bank(pr, b), 0:256]
                    elif pr["kind"] == "latent" and b == 0:
                        dst, src = lat_bt[:, pr["b"] % 2, :, :], PS[:, prep_bank(pr, 0), :]
                    elif pr["kind"] == "latent":
                        dst, src = kr_bt[0:ROPE, pr["b"] % 2, :], PS[0:ROPE, prep_bank(pr, 1), 0:PAST]
                    else:
                        dst, src = kt[:, par, 2 * b:2 * b + 2, :], PS[:, prep_bank(pr, b), :]
                    act.activation(dst, src, ACT.Copy).then_inc(kt_ok, 1)

            def stick_act(units):
                L = len(units)
                for n in range(L + 1):
                    if n < L:
                        u = units[n]
                        i, a = u["i"], e_buf[:, u["i"] % 2, 0:u["N"]]
                        act.wait_ge(sb_min, i + 1)
                        act.activation(a, a, ACT.Exp).then_inc(sb_exp, 1)
                        act.wait_ge(sb_exp, i + 1)
                        act.activation(a, a, ACT.Ln, bias=one[:]).then_inc(sb_ln, 1)
                    if n > 0:
                        u = units[n - 1]
                        i = u["i"]
                        act.wait_ge(sb_acc, i + 1)
                        if i >= 2:
                            act.wait_ge(sb_pv, i - 1)
                        act.activation(w_buf[:, i % 2, 0:u["N"]], PS[:, Z_BANK[i % 4], 0:u["N"]], ACT.Exp).then_inc(sb_w, 1)
                    if n + 2 < L and units[n + 2]["prep"]:
                        copy_kt(units[n + 2]["prep"])

            def soft_act(units):
                if units[0]["prep"]:
                    copy_kt(units[0]["prep"])
                for n in range(len(units) + 1):
                    if n < len(units):
                        u = units[n]
                        i = u["i"]
                        act.wait_ge(at_max, i + 1)
                        if i >= 2:
                            act.wait_ge(at_t, i - 1)
                        act.activation(p_buf[:, i % 2, 0:u["N"]], PS[:, S_BANK[i % 2], 0:u["N"]], ACT.Exp,
                                       bias=at_cols[:, i % 4, 0:1], accum_out=at_cols[:, i % 4, 1:2]).then_inc(at_exp, 1)
                    if n + 1 < len(units) and units[n + 1]["prep"]:
                        copy_kt(units[n + 1]["prep"])
                    if n > 0:
                        u = units[n - 1]
                        i = u["i"]
                        act.wait_ge(at_t, i + 1)
                        if i >= 2:
                            act.wait_ge(at_pv, i - 1)
                        n_t = u["N"] // P * u["w"]
                        act.activation(pt_buf[:, i % 2, 0:n_t], PS[:, T_BANK[i % 2], 0:n_t], ACT.Copy).then_inc(at_pt, 1)

            def split_mixed(st):
                for t in range(TILES):
                    act.wait_ge(*mixed_done(st))
                    act.activation(XT[0][:, :, tok(t)], OT[:, :, tok(t)], ACT.Copy).then_inc(ot_hi, 1)

            for st in stages:
                if st["kind"] not in ("ab", "mla"):
                    load_gains(st)
                ahead = None
                if st["kind"] == "ffn":
                    b0 = st["n"] * 2 * FB
                    pa, pb = st["passes"][0], st["passes"][1]
                    with act.Fori(0, 2) as fh:
                        hi_gu(fh * FB + b0)
                        for j in range(FB):
                            hi_chunk(pa, j, fh * 2 + pa["uses"][j])
                            silu(fh * FB + b0 + j)
                            if j < FB - 1:
                                hi_gu(fh * FB + b0 + j + 1)
                        for c in range(FB):
                            hi_chunk(pb, c, fh * 2 + pb["uses"][c])
                elif st["kind"] == "ple":
                    for b in range(3):
                        act.wait_ge(ple["tr"], 3 * st["n"] + b + 1)
                        act.activation(*ple_evict(b, 0), ACT.Copy).then_inc(ple["hi"], 1)
                    for p in st["passes"][0:2]:
                        for c in range(p["K"]):
                            hi_chunk(p, c, p["uses"][c])
                    p0, p1 = st["passes"][2:4]
                    for c in range(KD):
                        hi_chunk(p0, c, p0["uses"][c])

                    def sigmoid(q, t, p):
                        act.wait_ge(y_mm, summed(p["i"], t))
                        if q * TILES + t >= 2:
                            act.wait_ge(y_out, evicted(p["i"], t) - 2)
                        act.activation(GT[:, (q * TILES + t) % 2, :], PS[:, Y_BANK[t], :], ACT.Sigmoid
                                       ).then_inc(ple["gate"], 1)

                    for t in range(TILES):
                        sigmoid(0, t, p0)
                    for c in range(KD):
                        hi_chunk(p1, c, p1["uses"][c])
                    ahead = lambda t: sigmoid(1, t, p1)
                elif st["kind"] == "ab":
                    ps = st["passes"]
                    staged = 0
                    for q in range(6):
                        for c in range(KD):
                            hi_chunk(ps[q], c, ps[q]["uses"][c])
                        for t in range(TILES):
                            act.wait_ge(y_mm, summed(ps[q]["i"], t))
                            if q in (1, 4):
                                act.wait_ge(st_tr, TILES * (staged - 1) + t + 1)
                            if q == 3:
                                act.wait_ge(st_tr, TILES * 2)
                                act.wait_ge(st_out["sb_k"], 2 * 16)
                            name = ("sb_q", "sb_k", "sb_v", "df_q", "df_k", "df_v")[q]
                            dst = QKV[name] if name[3] == "v" else rows_in
                            act.activation(dst[:, t, :], PS[:, Y_BANK[t], :], ACT.Copy,
                                           scale=HD ** -0.5 if name[3] == "q" else 1.0).then_inc(y_out, 1)
                        staged += q in (0, 1, 3, 4)
                    act.wait_ge(lam_step, 2)
                    act.activation(lam_cols[:, 2:4], lam_cols[:, 0:2], ACT.Exp).then_inc(lam_step, 1)
                    stick_act(stick[st["stick0"]:st["stick1"]])
                    soft_act(soft[st["soft0"]:st["soft1"]])
                    for h in range(DF_HEADS):
                        act.wait_ge(o_out, groups_end(st))
                        if h > 0:
                            act.wait_ge(sub_mm, 2 * h)
                        act.activation(subln_tmp[:, 0, :], OT[:, 4 + h, :], ACT.Square).then_inc(sub_sq, 1)
                        if h > 0:
                            act.wait_ge(sub_ok, h)
                        for b, cols in ((0, slice(0, PROMPT)), (1, slice(PROMPT, TOK))):
                            act.wait_ge(sub_mm, 2 * h + b + 1)
                            act.activation(subln_tmp[:, 1, cols], PS[:, S_BANK[b], 0:cols.stop - cols.start], ACT.Ln,
                                           scale=-1.0 / (2 * HD), bias=eps_col[:]).then_inc(sub_ln, 1)
                        act.wait_ge(sub_ln, 2 * h + 2)
                        act.activation(subln_tmp[:, 1, :], subln_tmp[:, 1, :], ACT.Exp, scale=-0.5).then_inc(sub_rs, 1)
                    split_mixed(st)
                    for q in (6, 7):
                        for c in range(KD):
                            hi_chunk(ps[q], c, ps[q]["uses"][c])
                    load_gains(st)
                elif st["kind"] == "mla":
                    ps = st["passes"]
                    for q, (a, b, s0, s1) in enumerate(((0, HALF, 0, Q_LORA), (HALF, MLA_IN, Q_LORA, Q_LORA + KV_LORA))):
                        for c in range(KD):
                            hi_chunk(ps[q], c, ps[q]["uses"][c])
                        for t in range(TILES):
                            act.wait_ge(y_mm, summed(ps[q]["i"], t))
                            act.activation(c_in[:, t, a:b], PS[:, Y_BANK[t], 0:b - a], ACT.Copy).then_inc(y_out, 1)
                            act.wait_ge(y_out, evicted(ps[q]["i"], t))
                            if t > 0:
                                act.wait_ge(mc_ss, q * TILES + t)
                            act.activation(sq_tmp[:, q, 0:s1 - s0], c_in[:, t, s0:s1], ACT.Square,
                                           scale=(s1 - s0) ** -0.5, accum_out=mc[:, 0, t, q:q + 1]).then_inc(mc_ss, 1)
                    for c in range(ps[2]["K"]):
                        hi_chunk(ps[2], c, ps[2]["uses"][c])
                    for t in range(TILES):
                        act.wait_ge(mc_tr, t + 1)
                        act.activation(CQT[0][:, :, tok(t)], PS[:, TR_BANK[t % 2][0], 0:Q_LORA], ACT.Copy).then_inc(mc_hi, 1)
                    for name in ("lat", "kr"):
                        act.wait_ge(st_out[name], 2 * 16)
                    act.wait_ge(new_cp, 1)
                    for n in range(2 * PT):
                        act.wait_ge(v_mm, n + 1)
                        act.activation(V[:, n // 2, (n % 2) * HALF:(n % 2 + 1) * HALF], PS[:, S_BANK[n % 2], :], ACT.Copy
                                       ).then_inc(v_ok, 1)
                    for g in range(4):
                        p = ps[2 + g]
                        if g > 0:
                            for c in range(p["K"]):
                                hi_chunk(p, c, p["uses"][c])
                        for t in range(TILES):
                            act.wait_ge(y_mm, summed(p["i"], t))
                            if g > 0:
                                act.wait_ge(mq_tr, (g - 1) * TILES + t + 1)
                            act.activation(q_rows[:, t, :], PS[:, Y_BANK[t], 0:4 * QD], ACT.Copy, scale=QD ** -0.5
                                           ).then_inc(y_out, 1)
                    for h in range(MLA_HEADS):
                        act.wait_ge(wt_tr, h + 1)
                        if h >= 2:
                            act.wait_ge(ql_mm, h - 1)
                        act.activation(w_ukt[0:NOPE, h % 2, :], PS[0:NOPE, T_BANK[h % 2], 0:2 * P], ACT.Copy).then_inc(wt_cp, 1)
                    soft_act(soft[st["soft0"]:st["soft1"]])
                    split_mixed(st)
                    for q in (6, 7):
                        for c in range(KD):
                            hi_chunk(ps[q], c, ps[q]["uses"][c])
                    load_gains(st)
                tail(st, ahead)

        @block.gpsimd
        def _(pool):
            pool.memset(ident[:], 0.0).then_inc(const_ok, 1)
            pool.memset(minus_half[:], -0.5).then_inc(const_ok, 1)
            pool.memset(one[:], 1.0).then_inc(const_ok, 1)
            pool.memset(eps_col[:], EPS).then_inc(const_ok, 1)
            pool.wait_ge(const_ok, 4)
            pool.affine_select(out=ident[:], in_=ident[:], compare_op=ALU.not_equal, fill=1.0, base=0,
                               pattern=[[-1, P]], channel_multiplier=1).then_inc(const_ok, 1)

            def lo_gu(blk):
                for s in range(GU_PIECES):
                    pool.wait_ge(gu_hi_ok, blk * GU_PIECES + s + 1)
                    pool.tensor_tensor(gu_lo[:, s], gu_raw[:, s], gu_hi[:, s].bitcast(F32), ALU.subtract
                                       ).then_inc(gu_lo_ok, 1)

            def lo_chunk(p, i, c):
                pool.wait_ge(ch_hi_ok, i * CH + c + 1)
                pool.tensor_tensor(ch_lo[:, c, 0:p["n"]], ch_raw[:, c, 0:p["n"]], ch_hi[:, c, 0:p["n"]].bitcast(F32),
                                   ALU.subtract).then_inc(ch_lo_ok, counts(p, c))

            def tail(st):
                k = st["k"]

                def root(t, which, ss, n, eps, eps_n, done):
                    pool.wait_ge(ss, n)
                    pool.tensor_scalar(rs[:, t, which:which + 1], ssq[:, t, 2 * which:2 * which + 1],
                                       ssq[:, t, 2 * which + 1:2 * which + 2], eps, ALU.add, ALU.add).then_inc(eps_ok, 1)
                    pool.wait_ge(eps_ok, eps_n)
                    pool.tensor_tensor(rs[:, t, which:which + 1], rs[:, t, which:which + 1], minus_half[:], ALU.pow
                                       ).then_inc(done, 1)

                n = roots[0]
                for t in range(TILES):
                    if k > 0:
                        roots[0] += 1
                        root(t, 0, ss1_ok, 2 * (TILES * (k - 1) + t) + 2, EPS / st["c"] ** 2, roots[0], rs1_ok)
                    if st["pre"] is not None:
                        roots[0] += 1
                        root(t, 1, ss2_ok, 2 * (TILES * k + t) + 2, EPS, roots[0], rs2_ok)
                if st["zero_y"]:
                    for t in range(TILES):
                        pool.wait_ge(tr_ok, 2 * (TILES * k + t) + 2)
                        pool.memset(Y[:, t, :], 0.0).then_inc(y_zero, 1)

            roots = [0]
            for st in stages:
                if st["kind"] == "ffn":
                    pa, pb = st["passes"][0], st["passes"][1]
                    b0 = st["n"] * 2 * FB
                    with pool.Fori(0, 2) as fh:
                        lo_gu(fh * FB + b0)
                        for j in range(FB):
                            lo_chunk(pa, fh * 2 + pa["i"], j)
                            if j < FB - 1:
                                lo_gu(fh * FB + b0 + j + 1)
                        for c in range(FB):
                            lo_chunk(pb, fh * 2 + pb["i"], c)
                elif st["kind"] == "ple":
                    pool.wait_ge(y_mm, summed(st["passes"][0]["i"] - 1, TILES - 1))
                    pool.dma_start(p_raw[:, 0:PT, :], io["p_prompt"][st["layer"]]).then_inc(ple["in"], 16)
                    pool.dma_start(p_raw[:, PT, :], io["p_sample"][st["layer"]]).then_inc(ple["in"], 16)
                    for p in st["passes"]:
                        for c in range(p["K"]):
                            lo_chunk(p, p["i"], c)
                elif st["kind"] == "ab":
                    for q, p in enumerate(st["passes"]):
                        if q == 6:
                            pool.wait_ge(y_mm, summed(p["i"] - 1, TILES - 1))
                            pool.dma_start(lam_rows[:], io["df_lambda"][0].rearrange("a d -> (a d)").partition_broadcast(P)
                                           .rearrange("p (a d) -> p a d", a=4)).then_inc(lam_in, 16)
                            pool.dma_start(lam_cols[:, 6:7], io["df_subln"][0].rearrange("(e a) -> e a", a=1)
                                           ).then_inc(lam_in, 16)
                        for c in range(p["K"]):
                            lo_chunk(p, p["i"], c)
                elif st["kind"] == "mla":
                    ps = st["passes"]
                    for p in ps[0:2]:
                        for c in range(p["K"]):
                            lo_chunk(p, p["i"], c)
                    for q in range(2):
                        for t in range(TILES):
                            n = q * TILES + t
                            pool.wait_ge(mc_ss, n + 1)
                            pool.tensor_scalar(mc[:, 1, t, q:q + 1], mc[:, 0, t, q:q + 1], EPS, None, ALU.add
                                               ).then_inc(mc_eps, 1)
                            pool.wait_ge(mc_eps, n + 1)
                            pool.tensor_tensor(mc[:, 1, t, q:q + 1], mc[:, 1, t, q:q + 1], minus_half[:], ALU.pow
                                               ).then_inc(mc_rs, 1)
                    for p in ps[2:]:
                        for c in range(p["K"]):
                            lo_chunk(p, p["i"], c)
                tail(st)

        @block.vector
        def _(dve):
            for free, n in ((sg_free, 2), (y_out, TILES), (silu_ok, 2), (h_mul, 2), (gate_mm, 2), (up_mm, 2),
                            (gu_used, 2), (ch_used, CH - 1), (y_mm, TILES)):
                dve.sem_inc(free, n)

            def gated(blk):
                for b, bank, cols in ((0, UP_A, slice(0, GA)), (1, UP_B, slice(GA, TOK))):
                    dve.wait_ge(silu_ok, blk * 2 + b + 3)
                    dve.wait_ge(up_mm, blk * 2 + b + 3)
                    dve.tensor_tensor(SG[:, cols], SG[:, cols], PS[:, bank, 0:cols.stop - cols.start], ALU.mult
                                      ).then_inc(h_mul, 1)

            def split_h(blk, slot):
                for b, cols in ((0, slice(0, GA)), (1, slice(GA, TOK))):
                    dve.wait_ge(h_mul, blk * 2 + b + 3)
                    dve.tensor_copy(HT[0][:, bass.ds(slot, 1), cols].rearrange("p a n -> p (a n)"), SG[:, cols]
                                    ).then_inc(h_hi_ok, 1)
                    dve.wait_ge(h_hi_ok, blk * 2 + b + 1)
                    dve.tensor_tensor(HT[1][:, bass.ds(slot, 1), cols].rearrange("p a n -> p (a n)"), SG[:, cols],
                                      HT[0][:, bass.ds(slot, 1), cols].rearrange("p a n -> p (a n)").bitcast(F32),
                                      ALU.subtract).then_inc(sg_free, 1)

            def add_y(i, t, half):
                dve.wait_ge(y_mm, summed(i, t))
                dve.wait_ge(y_out, evicted(i, t) - 1)
                yt = Y[:, t, half * HALF:(half + 1) * HALF]
                dve.tensor_tensor(yt, yt, PS[:, Y_BANK[t], :], ALU.add).then_inc(y_out, 1)

            def tail(st, take):
                k = st["k"]

                def post(t):
                    n = TILES * (k - 1) + t
                    dve.wait_ge(rs1_ok, n + 1)
                    dve.scalar_tensor_tensor(Y[:, t, :], Y[:, t, :], rs[:, t, 0:1], g_post[:], ALU.mult, ALU.mult
                                             ).then_inc(post_ok, 1)
                    dve.wait_ge(post_ok, n + 1)
                    dve.tensor_tensor(X[:, t, :], X[:, t, :], Y[:, t, :], ALU.add).then_inc(x_ok, 1)

                def xn(t):
                    if k > 0:
                        dve.wait_ge(x_ok, TILES * (k - 1) + t + 1)
                    dve.wait_ge(rs2_ok, TILES * k + t + 1)
                    dve.scalar_tensor_tensor(Y[:, t, :], X[:, t, :], rs[:, t, 1:2], g_pre[:], ALU.mult, ALU.mult
                                             ).then_inc(xn_ok, 1)

                def lo(t):
                    for b in range(2):
                        dve.wait_ge(xt_hi_ok, 2 * (TILES * k + t) + b + 1)
                        dve.tensor_tensor(XT[1][:, 4 * b:4 * b + 4, tok(t)], PS[:, TR_BANK[t % 2][b], :],
                                          XT[0][:, 4 * b:4 * b + 4, tok(t)].bitcast(F32), ALU.subtract
                                          ).then_inc(xt_lo_ok, 1)

                gains[0] += 16 * ((k > 0) + (st["pre"] is not None))
                dve.wait_ge(gains_in, gains[0])
                for t in range(TILES):
                    if k > 0:
                        take(t)
                    if st["pre"] is not None and t > 0:
                        xn(t - 1)
                    if k > 0:
                        post(t)
                if st["pre"] is not None:
                    lo(0)
                    lo(1)
                    xn(TILES - 1)
                    for t in range(2, TILES):
                        lo(t)

            def rotate(x1, x2, cos, sin, n):
                G, half = x1.shape[1], x1.shape[2]
                tmp = [rope_tmp[:, j, 0:G * half].rearrange("p (g d) -> p g d", g=G) for j in range(4)]
                cs, sn = (a.unsqueeze(1).to_broadcast([P, G, half]) for a in (cos, sin))
                if n:
                    dve.wait_ge(rope_ok, 2 * n)
                for j, (x, f) in enumerate(((x1, cs), (x2, sn), (x2, cs), (x1, sn))):
                    dve.tensor_tensor(tmp[j], x, f, ALU.mult).then_inc(rope_part, 1)
                dve.wait_ge(rope_part, 4 * n + 4)
                dve.tensor_tensor(x1, tmp[0], tmp[1], ALU.subtract).then_inc(rope_ok, 1)
                dve.tensor_tensor(x2, tmp[2], tmp[3], ALU.add).then_inc(rope_ok, 1)

            def evict_group(u):
                g = u["g"]
                dst = g["dst"]
                src = PS[:, O_BANK[g["i"] % 2], 0:HALF]
                if len(dst.shape) == 3:
                    src = src.rearrange("p (a n) -> p a n", a=dst.shape[1])
                dve.tensor_copy(dst, src).then_inc(o_out, 1)

            def stick_dve(units):
                L = len(units)

                def masked(x, u):
                    cols, b, kind = u["mask"]
                    if kind == "diag":
                        return x[:, cols], const("diag")
                    m = const("batch_tri")[:, b * DEC_T:(b + 1) * DEC_T]
                    return (x[:, cols].rearrange("p (h t) -> p h t", h=SB_HEADS),
                            m.unsqueeze(1).to_broadcast([P, SB_HEADS, DEC_T]))

                for n in range(L + 3):
                    if n < L:
                        u = units[n]
                        i, z = u["i"], PS[:, Z_BANK[u["i"] % 4], 0:u["N"]]
                        dve.wait_ge(sb_z, i + 1)
                        if i >= 2:
                            dve.wait_ge(sb_sp, i - 1)
                        dve.tensor_scalar(e_buf[:, i % 2, 0:u["N"]], z, Z_MOST, None, ALU.min).then_inc(sb_min, 1)
                    if 1 <= n <= L:
                        u = units[n - 1]
                        i = u["i"]
                        dve.wait_ge(sb_ln, i + 1)
                        if i >= 4:
                            dve.wait_ge(sb_acc, i - 3 if u["prep"] is None else i - 1)
                        dve.tensor_tensor(u["sp"], PS[:, Z_BANK[i % 4], 0:u["N"]], e_buf[:, i % 2, 0:u["N"]], ALU.max
                                          ).then_inc(sb_sp, 1)
                        dve.wait_ge(sb_sp, i + 1)
                        x, m = masked(u["sp"], u)
                        dve.tensor_tensor(x, x, m, ALU.mult).then_inc(sb_spm, 1)
                    if 2 <= n <= L + 1:
                        u = units[n - 2]
                        i = u["i"]
                        dve.wait_ge(sb_w, i + 1)
                        x, m = masked(w_buf[:, i % 2, 0:u["N"]], u)
                        dve.scalar_tensor_tensor(x, x, 2.0, m, ALU.min, ALU.mult).then_inc(sb_wm, 1)
                    if n >= 3 and units[n - 3]["last"]:
                        dve.wait_ge(sb_pv, units[n - 3]["i"] + 1)
                        evict_group(units[n - 3])

            def soft_dve(units):
                L = len(units)
                for n in range(L + 3):
                    if 1 <= n <= L:
                        u = units[n - 1]
                        i = u["i"]
                        dve.wait_ge(at_exp, i + 1)
                        dve.reciprocal(at_cols[:, i % 4, 2:3], at_cols[:, i % 4, 1:2]).then_inc(at_r, 1)
                        dve.wait_ge(at_r, i + 1)
                        pr = p_buf[:, i % 2, 0:u["N"]]
                        if u["coef"]:
                            col = lam_cols[:, 4:5] if u["coef"] == "neg_lam" else lam_cols[:, 5:6]
                            dve.tensor_scalar(pr, pr, at_cols[:, i % 4, 2:3], col, ALU.mult, ALU.mult).then_inc(at_p, 1)
                        else:
                            dve.tensor_scalar(pr, pr, at_cols[:, i % 4, 2:3], None, ALU.mult).then_inc(at_p, 1)
                    if n < L:
                        u = units[n]
                        i = u["i"]
                        dve.wait_ge(at_s, i + 1)
                        dve.tensor_reduce(at_cols[:, i % 4, 0:1], PS[:, S_BANK[i % 2], 0:u["N"]], AX_X, ALU.max,
                                          negate=True).then_inc(at_max, 1)
                    if n >= 3 and units[n - 3]["last"]:
                        dve.wait_ge(at_pv, units[n - 3]["i"] + 1)
                        evict_group(units[n - 3])

            def split_mixed(st, before):
                for t in range(TILES):
                    dve.wait_ge(ot_hi, before + t + 1)
                    dve.tensor_tensor(XT[1][:, :, tok(t)], OT[:, :, tok(t)], XT[0][:, :, tok(t)].bitcast(F32),
                                      ALU.subtract).then_inc(ot_lo, 1)

            def out_rows(i, t, half):
                dve.wait_ge(y_mm, summed(i, t))
                dve.tensor_copy(Y[:, t, half * HALF:(half + 1) * HALF], PS[:, Y_BANK[t], :]).then_inc(y_out, 1)

            gains = [0]
            zeroed = [0]
            for st in stages:
                take = None
                if st["k"] > 0 and stages[st["k"] - 1]["zero_y"]:
                    zeroed[0] += TILES
                    dve.wait_ge(y_zero, zeroed[0])
                if st["kind"] == "ffn":
                    b0 = st["n"] * 2 * FB
                    i0 = st["passes"][0]["i"]
                    for fh in range(2):
                        with dve.Fori(0, FB) as fb:
                            gated(fb + (b0 + fh * FB))
                            split_h(fb + (b0 + fh * FB), fb)
                        for nh in range(2 - fh):
                            for t in range(TILES):
                                add_y(i0 + 2 * fh + nh, t, nh)
                    take = lambda t, i=i0 + 3: add_y(i, t, 1)
                elif st["kind"] == "ple":
                    for b in range(3):
                        dve.wait_ge(ple["hi"], 3 * st["n"] + b + 1)
                        dst, src = ple_evict(b, 1)
                        hi_part, _ = ple_evict(b, 0)
                        dve.tensor_tensor(dst, src, hi_part.bitcast(F32), ALU.subtract).then_inc(ple["lo"], 1)
                    for q in range(2):
                        for t in range(TILES):
                            add_y(st["passes"][q]["i"], t, q)

                    def times_gate(q, t, st=st):
                        p = st["passes"][2 + q]["i"]
                        dve.wait_ge(ple["gate"], 2 * TILES * st["n"] + q * TILES + t + 1)
                        dve.wait_ge(y_out, evicted(p, t) - 1)
                        yt = Y[:, t, q * HALF:(q + 1) * HALF]
                        dve.tensor_tensor(yt, yt, GT[:, (q * TILES + t) % 2, :], ALU.mult).then_inc(y_out, 1)

                    for t in range(TILES):
                        times_gate(0, t)
                    take = lambda t: times_gate(1, t)
                elif st["kind"] == "ab":
                    ps = st["passes"]
                    names = ["sb_q", "sb_k", "df_q", "df_k"]

                    def copy_staged(sgd, t):
                        dve.wait_ge(st_tr, TILES * sgd + t + 1)
                        dve.tensor_copy(QKV[names[sgd]][:, :, tok(t)],
                                        PS[:, T_BANK[(TILES * sgd + t) % 2], :].rearrange("p (a n) -> p a n", a=4)).then_inc(st_cp, 1)

                    dve.wait_ge(consts_in, 16)
                    for t in range(TILES):
                        copy_staged(0, t)
                    for t in range(TILES):
                        copy_staged(1, t)
                    for sgd in (2, 3):
                        for t in range(TILES):
                            dve.wait_ge(y_out, evicted(ps[sgd + 1]["i"], t))
                            g = rows_in[:, t, :].rearrange("p (g d) -> p g d", d=HD)
                            h = DF_ROT // 2
                            rotate(g[:, :, 0:h], g[:, :, h:2 * h], const("cos_d")[:, t * h:(t + 1) * h],
                                   const("sin_d")[:, t * h:(t + 1) * h], TILES * (sgd - 2) + t)
                            if sgd == 3:
                                copy_staged(2, t)
                    for t in range(TILES):
                        copy_staged(3, t)
                    lam_init = 0.8 - 0.6 * math.exp(-0.3 * st["layer"])
                    dve.wait_ge(lam_in, 32)
                    dve.tensor_tensor(lam_rows[:, 0:3:2, :], lam_rows[:, 0:3:2, :], lam_rows[:, 1:4:2, :], ALU.mult
                                      ).then_inc(lam_step, 1)
                    dve.wait_ge(lam_step, 1)
                    dve.tensor_reduce(lam_cols[:, 0:2], lam_rows[:, 0:3:2, :], AX_X, ALU.add).then_inc(lam_step, 1)
                    dve.wait_ge(lam_step, 3)
                    dve.tensor_scalar(lam_cols[:, 4:5], lam_cols[:, 3:4], lam_cols[:, 2:3], -lam_init,
                                      ALU.subtract, ALU.add).then_inc(lam_step, 1)
                    dve.wait_ge(lam_step, 4)
                    dve.tensor_scalar(lam_cols[:, 5:6], lam_cols[:, 4:5], const("comp1"), const("comp0"),
                                      ALU.mult, ALU.add).then_inc(lam_step, 1)
                    dve.tensor_scalar(lam_cols[:, 6:7], lam_cols[:, 6:7], 1.0 - lam_init, None, ALU.mult
                                      ).then_inc(lam_step, 1)
                    dve.wait_ge(st_out["df_k"], 2 * 16)
                    for name in qbd:
                        dve.memset(qbd[name][:], 0.0).then_inc(qbd_ok, 1)
                    dve.wait_ge(qbd_ok, 2)
                    for name in qbd:
                        for c in range(2):
                            r = slice(HD * c, HD * c + HD)
                            dve.tensor_copy(qbd[name][r, :, :, c, :], QKV[name][r, :, PROMPT:TOK].rearrange(
                                "p h (b t) -> p h b t", b=DEC_B)).then_inc(qbd_ok, 1)
                    stick_dve(stick[st["stick0"]:st["stick1"]])
                    dve.wait_ge(lam_step, 6)
                    soft_dve(soft[st["soft0"]:st["soft1"]])
                    for h in range(DF_HEADS):
                        dve.wait_ge(sub_rs, h + 1)
                        dve.scalar_tensor_tensor(OT[:, 4 + h, :], OT[:, 4 + h, :], lam_cols[:, 6:7],
                                                 subln_tmp[:, 1, :], ALU.mult, ALU.mult).then_inc(sub_ok, 1)
                    split_mixed(st, st["before"] * TILES)
                    for t in range(TILES):
                        out_rows(ps[6]["i"], t, 0)
                    take = lambda t, i=ps[7]["i"]: out_rows(i, t, 1)
                elif st["kind"] == "mla":
                    ps = st["passes"]
                    dve.wait_ge(mg_in, 3 * 16)
                    for q, (a, b, g) in enumerate(((0, Q_LORA, mg_q), (Q_LORA, Q_LORA + KV_LORA, mg_kv))):
                        for t in range(TILES):
                            dve.wait_ge(mc_rs, q * TILES + t + 1)
                            dve.scalar_tensor_tensor(c_in[:, t, a:b], c_in[:, t, a:b], mc[:, 1, t, q:q + 1], g[:],
                                                     ALU.mult, ALU.mult).then_inc(mc_n, 1)
                            if q == 1:
                                x = c_in[:, t, b:MLA_IN].unsqueeze(1)
                                h = ROPE // 2
                                rotate(x[:, :, 0:h], x[:, :, h:2 * h], mconst("cos_m")[:, t * h:(t + 1) * h],
                                       mconst("sin_m")[:, t * h:(t + 1) * h], st["rot0"] + t)
                    dve.wait_ge(mc_n, 2 * TILES)
                    dve.tensor_copy(lat_new[:], c_in[:, PT, Q_LORA:Q_LORA + KV_LORA]).then_inc(new_cp, 1)
                    for t in range(TILES):
                        dve.wait_ge(mc_tr, t + 1)
                        bank = TR_BANK[t % 2][1]
                        dve.tensor_copy(lat_t[:, :, tok(t)], PS[:, bank, 0:2 * P].rearrange("p (k n) -> p k n", k=2)
                                        ).then_inc(mc_lat, 1)
                        dve.tensor_copy(kr_t[NOPE:QD, tok(t)], PS[NOPE:QD, bank, 2 * P:3 * P]).then_inc(mc_lat, 1)
                        if t == PT:
                            dve.tensor_copy(kr_t[0:ROPE, tok(t)], PS[0:ROPE, bank, 3 * P:4 * P]).then_inc(mc_lat, 1)
                        dve.wait_ge(mc_hi, t + 1)
                        dve.tensor_tensor(CQT[1][:, :, tok(t)], PS[:, TR_BANK[t % 2][0], 0:Q_LORA].rearrange(
                            "p (k n) -> p k n", k=3), CQT[0][:, :, tok(t)].bitcast(F32), ALU.subtract).then_inc(mc_lo, 1)
                    dve.wait_ge(mc_lat, 2 * TILES)
                    for par in range(2):
                        dve.tensor_copy(k_t[NOPE:QD, par, :], kr_t[NOPE:QD, 0:PROMPT]).then_inc(krt_cp, 1)

                    def copy_q(g, t):
                        dve.wait_ge(mq_tr, g * TILES + t + 1)
                        dve.tensor_copy(q_t[0:QD, 4 * g:4 * g + 4, tok(t)],
                                        PS[0:QD, T_BANK[(g * TILES + t) % 2], :].rearrange("p (h n) -> p h n", h=4)
                                        ).then_inc(mq_cp, 1)
                        if t == PT:
                            for j in range(4):
                                dve.tensor_copy(qr_t[0:ROPE, :, 4 * g + j, :], PS[0:ROPE, 3, j * P:(j + 1) * P].rearrange(
                                    "p (b t) -> p b t", b=DEC_B)).then_inc(qr_cp, 1)

                    for g in range(4):
                        for t in range(TILES):
                            if g > 0:
                                copy_q(g - 1, t)
                            dve.wait_ge(y_out, evicted(ps[2 + g]["i"], t))
                            x = q_rows[:, t, :].rearrange("p (h d) -> p h d", h=4)
                            h = ROPE // 2
                            rotate(x[:, :, NOPE:NOPE + h], x[:, :, NOPE + h:QD], mconst("cos_m")[:, t * h:(t + 1) * h],
                                   mconst("sin_m")[:, t * h:(t + 1) * h], st["rot0"] + (g + 1) * TILES + t)
                    for t in range(TILES):
                        copy_q(3, t)
                    for h in range(MLA_HEADS):
                        dve.wait_ge(ql_mm, h + 1)
                        for c in range(2):
                            dve.tensor_copy(q_lat_t[:, c, :, h, :], PS[:, S_BANK[h % 2], c * P:(c + 1) * P].rearrange(
                                "p (b t) -> p b t", b=DEC_B)).then_inc(ql_cp, 1)
                    soft_dve(soft[st["soft0"]:st["soft1"]])
                    for b in range(2):
                        dve.wait_ge(uo_mm, b + 1)
                        dve.tensor_copy(OT[:, 4 * b:4 * b + 4, PROMPT:TOK], PS[:, S_BANK[b], :].rearrange(
                            "p (a n) -> p a n", a=4)).then_inc(uo_ok, 1)
                    split_mixed(st, st["before"] * TILES)
                    for t in range(TILES):
                        out_rows(ps[6]["i"], t, 0)
                    take = lambda t, i=ps[7]["i"]: out_rows(i, t, 1)
                tail(st, take)

        @block.tensor
        def _(pe):
            def product(out, a, b, start, stop):
                pe.matmul(out, a[0], b[0], start=start, stop=False)
                pe.matmul(out, a[0], b[1], start=False, stop=False)
                return pe.matmul(out, a[1], b[0], start=False, stop=stop)

            def gate_up(blk, lo_ready, banks_free):
                for q, banks, done in ((0, (GATE_A, GATE_B), gate_mm), (1, (UP_A, UP_B), up_mm)):
                    pe.wait_ge((silu_ok, h_mul)[q], blk * 2 + 2)
                    pe.wait_ge(y_out, banks_free)
                    for b, cols in ((0, slice(0, GA)), (1, slice(GA, TOK))):
                        pe.wait_ge(xt_lo_ok, lo_ready + 2 * (TILES if b else GA // P))
                        for k in range(KD):
                            s, kk = 2 * q + k // 4, k % 4
                            if b == 0 and kk == 0:
                                pe.wait_ge(gu_lo_ok, blk * GU_PIECES + s + 1)
                            mm = product(PS[:, banks[b], 0:cols.stop - cols.start], (gu_hi[:, s, kk, :], gu_lo[:, s, kk, :]),
                                         (XT[0][:, k, cols], XT[1][:, k, cols]), k == 0, k == KD - 1)
                            if b == 1 and k == 3:
                                mm.then_inc(gu_used, 1)
                        mm.then_inc(done, 1)

            def column_pass(p, i, src, head, before=None):
                K, n = p["K"], p["n"]
                order = [(c, t) for c in range(head) for t in range(TILES)]
                order += [(c, t) for t in range(TILES) for c in range(head, K)]
                for c, t in order:
                    if t == 0:
                        pe.wait_ge(ch_lo_ok, i * CH + c + 1)
                    if c == 0:
                        pe.wait_ge(y_out, i * TILES + t + 1)
                    if before:
                        before(t, c)
                    mm = product(PS[:, Y_BANK[t], 0:n], (src[0][:, c, tok(t)], src[1][:, c, tok(t)]),
                                 (ch_hi[:, c, 0:n], ch_lo[:, c, 0:n]), c == 0, c == K - 1)
                    if c == K - 1:
                        mm.then_inc(y_mm, 1)
                    elif t == TILES - 1:
                        mm.then_inc(ch_used, counts(p, c, CH - 1))

            def transpose_keys(pr):
                i, par, kind = pr["i"], pr["i"] % 2, pr["kind"]
                if kind in ("stick", "soft"):
                    pe.wait_ge(kraw_in[par], 16 * (i // 2 + 1))
                elif kind == "latent":
                    pe.wait_ge(lat_in[pr["b"] % 3], 32 * (pr["b"] // 3 + 1))
                for b in range(2):
                    if i >= 1:
                        pe.wait_ge(kt_ok, 2 * (i - 1) + b + 1)
                    if kind == "head":
                        for c in range(2):
                            mm = pe.matmul(PS[0:NOPE, prep_bank(pr, b), 0:256], W_uk[:, c, pr["h"] * NOPE:(pr["h"] + 1) * NOPE],
                                           lat_t[:, c, b * 256:(b + 1) * 256], start=c == 0, stop=c == 1)
                    elif kind == "latent" and b == 0:
                        for j in range(4):
                            mm = pe.transpose(PS[:, prep_bank(pr, 0), j * P:(j + 1) * P],
                                              lat_raw[:, pr["b"] % 3, j % 2, (j // 2) * P:(j // 2 + 1) * P], ident[:])
                    elif kind == "latent":
                        for j in range(2):
                            mm = pe.transpose(PS[0:ROPE, prep_bank(pr, 1), j * P:(j + 1) * P], kr_raw[:, pr["b"] % 3, j, :],
                                              ident[:])
                    else:
                        for j in range(4):
                            fb, kb = 2 * b + j // 2, j % 2
                            mm = pe.transpose(PS[:, prep_bank(pr, b), j * P:(j + 1) * P],
                                              k_raw[:, par, kb, fb * P:(fb + 1) * P], ident[:])
                    mm.then_inc(kt_tr, 1)

            def bank_of(u):
                g = u["g"]
                if u["first"] and g["i"] >= 2:
                    pe.wait_ge(o_out, g["i"] - 1)
                return PS[:, O_BANK[g["i"] % 2], :]

            def stick_pe(units):
                L = len(units)

                def scores(u):
                    i = u["i"]
                    if u["prep"]:
                        pe.wait_ge(kt_ok, 2 * u["prep"]["i"] + 2)
                    if i >= 4:
                        pe.wait_ge(sb_w, i - 3)
                    for j, (cols, key, q) in enumerate(u["z"]):
                        mm = pe.matmul(PS[:, Z_BANK[i % 4], cols], key, q, start=j == 0, stop=True, skip_group_check=True)
                    mm.then_inc(sb_z, 1)

                scores(units[0])
                for n in range(L + 2):
                    if 1 <= n <= L:
                        u = units[n - 1]
                        i = u["i"]
                        bank = PS[:, Z_BANK[i % 4], :]
                        pe.wait_ge(sb_spm, i + 1)
                        mm = pe.matmul(bank[:, 0:u["N"]], const("neg_tri"), u["sp"], start=False, stop=True,
                                       skip_group_check=True)
                        for cols, sp_later in u["later"]:
                            mm = pe.matmul(bank[:, cols], const("neg_ones"), sp_later, start=False, stop=True,
                                           skip_group_check=True)
                        mm.then_inc(sb_acc, 1)
                    if n + 1 < L:
                        scores(units[n + 1])
                    if n >= 2:
                        u = units[n - 2]
                        i = u["i"]
                        out = bank_of(u)
                        pe.wait_ge(sb_wm, i + 1)
                        if u["prep"]:
                            pe.wait_ge(vraw_in[u["prep"]["i"] % 2], 16 * (u["prep"]["i"] // 2 + 1))
                        for rows, cols, val, wc, start in u["pv"]:
                            mm = pe.matmul(out[rows, cols], val, w_buf[:, i % 2, wc], start=start, stop=True,
                                           skip_group_check=True)
                        mm.then_inc(sb_pv, 1)
                    if n + 2 < L and units[n + 2]["prep"]:
                        transpose_keys(units[n + 2]["prep"])

            def soft_pe(units):
                L = len(units)
                if units[0]["prep"]:
                    transpose_keys(units[0]["prep"])
                for n in range(L + 2):
                    if n < L:
                        u = units[n]
                        i = u["i"]
                        if u["prep"]:
                            pe.wait_ge(kt_ok, 2 * u["prep"]["i"] + 2)
                        if i >= 2:
                            pe.wait_ge(at_exp, i - 1)
                        for rows, cols, q, key, start in u["s"]:
                            mm = pe.matmul(PS[rows, S_BANK[i % 2], cols], q, key, start=start, stop=True,
                                           skip_group_check=True)
                        mm.then_inc(at_s, 1)
                    if n + 1 < L and units[n + 1]["prep"]:
                        transpose_keys(units[n + 1]["prep"])
                    if 1 <= n <= L:
                        u = units[n - 1]
                        i = u["i"]
                        pe.wait_ge(at_p, i + 1)
                        if i >= 2:
                            pe.wait_ge(at_pt, i - 1)
                        for j in range(u["N"] // P):
                            out, w = PS[:, T_BANK[i % 2], j * u["w"]:(j + 1) * u["w"]], p_buf[:, i % 2, j * P:(j + 1) * P]
                            if u["w"] == P:
                                mm = pe.transpose(out, w, ident[:])
                            else:
                                mm = pe.matmul(out, w, const("merge"), start=j == 0, stop=True, skip_group_check=True)
                        mm.then_inc(at_t, 1)
                    if n >= 2:
                        u = units[n - 2]
                        i = u["i"]
                        out = bank_of(u)
                        pe.wait_ge(at_pt, i + 1)
                        if u["prep"] and u["prep"]["kind"] == "soft":
                            pe.wait_ge(vraw_in[u["prep"]["i"] % 2], 16 * (u["prep"]["i"] // 2 + 1))
                        for rows, cols, val, (c0, w), start in u["pv"]:
                            mm = pe.matmul(out[rows, cols], val, pt_buf[:, i % 2, c0:c0 + w], start=start, stop=True,
                                           skip_group_check=True)
                        mm.then_inc(at_pv, 1)

            def tail(st):
                k = st["k"]
                if st["pre"] is None:
                    return
                for t in range(TILES):
                    pe.wait_ge(xn_ok, TILES * k + t + 1)
                    if t == 1 and k > 0:
                        pe.wait_ge(y_out, evicted(st["last"], TILES - 1))
                    if t > 1:
                        pe.wait_ge(xt_lo_ok, 2 * (TILES * k + t - 1))
                    for b in range(2):
                        for j in range(4):
                            mm = pe.transpose(PS[:, TR_BANK[t % 2][b], j * P:(j + 1) * P],
                                              Y[:, t, (4 * b + j) * P:(4 * b + j + 1) * P], ident[:])
                        mm.then_inc(tr_ok, 1)

            def mixed_out(st):
                n = st["before"] * TILES
                for p in st["passes"][6:8]:
                    column_pass(p, p["i"], XT, 0, lambda t, c: pe.wait_ge(ot_lo, n + t + 1) if c == 0 else None)

            pe.wait_ge(const_ok, 5)
            for st in stages:
                xt_ready = 2 * TILES * (st["k"] - 1)
                if st["kind"] == "ffn":
                    b0, i0 = st["n"] * 2 * FB, st["passes"][0]["i"]
                    with pe.Fori(0, 2) as fh:
                        with pe.Fori(0, FB) as fb:
                            gate_up(fb + fh * FB + b0, xt_ready, (fh * 2 + i0) * TILES + TILES)
                        done = (fh * FB + b0 + FB) * 2

                        def hidden(t, c):
                            if c == 0 and t == 0:
                                pe.wait_ge(sg_free, done)
                            if c == 0 and t == 1:
                                pe.wait_ge(silu_ok, done + 2)
                            if c == 0 and t == 3:
                                pe.wait_ge(h_mul, done + 2)
                            if c == FB - 1 and t == 0:
                                pe.wait_ge(sg_free, done + 2)

                        with pe.Fori(0, 2) as nh:
                            column_pass(st["passes"][0], nh + fh * 2 + i0, HT, 3, hidden)
                elif st["kind"] == "ple":
                    pe.wait_ge(ple["in"], 32 * (st["n"] + 1))
                    for b in range(3):
                        pe.wait_ge(y_out, TILES * (st["passes"][0]["i"] + 1))
                        if b == 2:
                            pe.wait_ge(xt_lo_ok, xt_ready + 2 * 4)
                        for j in range(4 if b < 2 else 2):
                            t, kb = (j, b) if b < 2 else (PT, j)
                            mm = pe.transpose(PS[:, 5 + b, j * P:(j + 1) * P], p_raw[:, t, kb * P:(kb + 1) * P], ident[:])
                        mm.then_inc(ple["tr"], 1)
                    pe.wait_ge(ple["lo"], 3 * (st["n"] + 1))
                    for p in st["passes"][0:2]:
                        column_pass(p, p["i"], PTT, 0)
                    for q, p in enumerate(st["passes"][2:4]):
                        column_pass(p, p["i"], XT, 0 if q == 0 else 2,
                                    lambda t, c: pe.wait_ge(xt_lo_ok, xt_ready + 2 * (t + 1)) if c == 0 else None)
                elif st["kind"] == "ab":
                    ps = st["passes"]
                    stage_of = {1: 0, 2: 1, 4: 2, 5: 3}

                    def staged(q):
                        def before(t, c):
                            if c:
                                return
                            if q == 0:
                                pe.wait_ge(xt_lo_ok, xt_ready + 2 * (t + 1))
                            if q in stage_of:
                                n = stage_of[q] * TILES + t
                                if stage_of[q] < 2:
                                    pe.wait_ge(y_out, evicted(ps[q - 1]["i"], t))
                                else:
                                    pe.wait_ge(rope_ok, 2 * (n - 2 * TILES) + 2)
                                if n >= 2:
                                    pe.wait_ge(st_cp, n - 1)
                                for j in range(4):
                                    mm = pe.transpose(PS[:, T_BANK[n % 2], j * P:(j + 1) * P],
                                                      rows_in[:, t, j * P:(j + 1) * P], ident[:])
                                mm.then_inc(st_tr, 1)
                        return before

                    for q in range(6):
                        column_pass(ps[q], ps[q]["i"], XT, 0, staged(q))
                    pe.wait_ge(st_cp, 4 * TILES)
                    pe.wait_ge(qbd_ok, 6)
                    pe.wait_ge(y_out, evicted(ps[5]["i"], TILES - 1))
                    stick_pe(stick[st["stick0"]:st["stick1"]])
                    soft_pe(soft[st["soft0"]:st["soft1"]])
                    for h in range(DF_HEADS):
                        pe.wait_ge(sub_sq, h + 1)
                        for b, cols in ((0, slice(0, PROMPT)), (1, slice(PROMPT, TOK))):
                            if h > 0:
                                pe.wait_ge(sub_ln, 2 * h - 1 + b)
                            pe.matmul(PS[:, S_BANK[b], 0:cols.stop - cols.start], const("neg_ones"),
                                      subln_tmp[:, 0, cols], start=True, stop=True).then_inc(sub_mm, 1)
                    mixed_out(st)
                elif st["kind"] == "mla":
                    ps = st["passes"]
                    for q in range(2):
                        column_pass(ps[q], ps[q]["i"], XT, 0, lambda t, c: pe.wait_ge(xt_lo_ok, xt_ready + 2 * (t + 1))
                                    if c == 0 and q == 0 else None)
                    pe.wait_ge(y_out, evicted(ps[1]["i"], TILES - 1))
                    for t in range(TILES):
                        pe.wait_ge(mc_n, TILES + t + 1)
                        pe.wait_ge(rope_ok, 2 * (st["rot0"] + t) + 2)
                        if t >= 2:
                            pe.wait_ge(mc_lo, t - 1)
                            pe.wait_ge(mc_lat, 2 * (t - 1))
                        b0, b1 = TR_BANK[t % 2]
                        for j in range(3):
                            pe.transpose(PS[:, b0, j * P:(j + 1) * P], c_in[:, t, j * P:(j + 1) * P], ident[:])
                        for j in range(2):
                            pe.transpose(PS[:, b1, j * P:(j + 1) * P], c_in[:, t, Q_LORA + j * P:Q_LORA + (j + 1) * P],
                                         ident[:])
                        mm = pe.transpose(PS[0:QD, b1, 2 * P:3 * P], c_in[:, t, MLA_IN - QD:MLA_IN], ident[:])
                        if t == PT:
                            mm = pe.transpose(PS[0:ROPE, b1, 3 * P:4 * P], c_in[:, t, MLA_IN - ROPE:MLA_IN], ident[:])
                        mm.then_inc(mc_tr, 1)
                    pe.wait_ge(muv_in[0], 16)
                    for n in range(2 * PT):
                        if n % 2 == 0:
                            pe.wait_ge(mc_lat, n + 2)
                        if n >= 2:
                            pe.wait_ge(v_ok, n - 1)
                        for c in range(2):
                            mm = pe.matmul(PS[:, S_BANK[n % 2], :], lat_t[:, c, tok(n // 2)],
                                           W_uv[0][:, c, (n % 2) * HALF:(n % 2 + 1) * HALF], start=c == 0, stop=c == 1)
                        mm.then_inc(v_mm, 1)

                    def heads_t(g, t):
                        n = g * TILES + t
                        pe.wait_ge(rope_ok, 2 * (st["rot0"] + TILES + n) + 2)
                        if n >= 2:
                            pe.wait_ge(mq_cp, n - 1)
                        for j in range(4):
                            mm = pe.transpose(PS[0:QD, T_BANK[n % 2], j * P:(j + 1) * P],
                                              q_rows[:, t, j * QD:(j + 1) * QD], ident[:])
                        if t == PT:
                            if g > 0:
                                pe.wait_ge(qr_cp, 4 * g)
                            for j in range(4):
                                mm = pe.transpose(PS[0:ROPE, 3, j * P:(j + 1) * P],
                                                  q_rows[:, t, j * QD + NOPE:(j + 1) * QD], ident[:])
                        mm.then_inc(mq_tr, 1)

                    for g in range(4):
                        def before(t, c, g=g):
                            if c == 0 and g > 0:
                                heads_t(g - 1, t)
                            if c == 0 and g == 0:
                                pe.wait_ge(mc_lo, t + 1)
                                if t == 0:
                                    pe.wait_ge(v_ok, 2 * PT)
                        column_pass(ps[2 + g], ps[2 + g]["i"], CQT, 0, before)
                    for t in range(TILES):
                        heads_t(3, t)
                    pe.wait_ge(mq_cp, 4 * TILES)
                    pe.wait_ge(qr_cp, 4 * 4)
                    pe.wait_ge(mw_in, 16)
                    for n in range(MLA_HEADS + 1):
                        if n < MLA_HEADS:
                            if n >= 2:
                                pe.wait_ge(wt_cp, n - 1)
                            for c in range(2):
                                mm = pe.transpose(PS[0:NOPE, T_BANK[n % 2], c * P:(c + 1) * P],
                                                  W_uk[:, c, n * NOPE:(n + 1) * NOPE], ident[:])
                            mm.then_inc(wt_tr, 1)
                        if n >= 1:
                            h = n - 1
                            pe.wait_ge(wt_cp, h + 1)
                            if h >= 2:
                                pe.wait_ge(ql_cp, 2 * (h - 1))
                            for c in range(2):
                                mm = pe.matmul(PS[:, S_BANK[h % 2], c * P:(c + 1) * P], w_ukt[0:NOPE, h % 2, c * P:(c + 1) * P],
                                               q_t[0:NOPE, h, PROMPT:TOK], start=c == 0, stop=True, skip_group_check=True)
                            mm.then_inc(ql_mm, 1)
                    pe.wait_ge(ql_cp, 2 * MLA_HEADS)
                    pe.wait_ge(krt_cp, 2)
                    soft_pe(soft[st["soft0"]:st["soft1"]])
                    pe.wait_ge(muv_in[1], 16)
                    pe.wait_ge(o_out, groups_end(st))
                    for h in range(MLA_HEADS):
                        out = PS[VD * (h % 2):VD * (h % 2) + VD, S_BANK[h // 8], (h // 2 % 4) * P:(h // 2 % 4 + 1) * P]
                        for c in range(2):
                            mm = pe.matmul(out, W_uv[1][:, c, h * VD:(h + 1) * VD],
                                           OLT[:, :, h // 8, c, (h % 8) * DEC_T:(h % 8 + 1) * DEC_T],
                                           start=c == 0, stop=c == 1, skip_group_check=True)
                        if h % 8 == 7:
                            mm.then_inc(uo_mm, 1)
                    mixed_out(st)
                tail(st)


_INS = ["x_prompt", "x_sample", "p_prompt", "p_sample", "cache_sb_k", "cache_sb_v", "cache_df_k", "cache_df_v",
        "cache_mla_latent", "cache_mla_krope", "norms", "ffn1_gu", "ffn1_dn", "ffn2_gu", "ffn2_dn", "ple_in",
        "ple_gate", "ab_in", "ab_out", "df_lambda", "df_subln", "mla_in", "mla_q_norm", "mla_kv_norm", "mla_uq",
        "mla_uk", "mla_uv", "mla_out"]


_NEW_ROWS = {"sb_k": (SB_HEADS, HD), "sb_v": (SB_HEADS, HD), "df_k": (DF_HEADS, 2, HD), "df_v": (DF_HEADS, 2 * HD),
             "lat": (KV_LORA,), "kr": (ROPE,)}


def build(nc, io, outs, plan):
    io = dict(io, plan=plan)
    xp, xs = io["x_prompt"][0].rearrange("(t p) d -> t p d", p=P), io["x_sample"].rearrange("b t d -> (b t) d")
    yp, ys = outs[0][0].rearrange("(t p) d -> t p d", p=P), outs[1].rearrange("b t d -> (b t) d")
    io["x_tiles"] = [xp[t] for t in range(PT)] + [xs]
    io["y_tiles"] = [yp[t] for t in range(PT)] + [ys]
    io["p_prompt"] = [io["p_prompt"][l, 0].rearrange("(t p) d -> p t d", p=P) for l in range(DEPTH)]
    io["p_sample"] = [io["p_sample"][l].rearrange("b t d -> (b t) d") for l in range(DEPTH)]
    n = len(_NEW_ROWS)
    for i, name in enumerate(_NEW_ROWS):
        pr, sa = outs[2 + i][0, 0], outs[2 + n + i][0]
        f = " ".join("xyz"[:len(pr.shape) - 1])
        io[name + "_out"] = (pr.rearrange(f"(t p) {f} -> p t ({f})", p=P), sa.rearrange(f"b t {f} -> (b t) ({f})"))
    encoder(nc, io)
PLAN = [("ffn", 0, 1), ("ab", 0, 0), ("ffn", 0, 2), ("ple", 0, 0), ("ffn", 1, 1), ("mla", 1, 0), ("ffn", 1, 2), ("ple", 1, 0)]
_OUTS = [((1, PROMPT, D), "float32"), ((DEC_B, DEC_T, D), "float32")]
_OUTS += [(lead + row, "float32") for lead in ((1, 1, PROMPT), (1, DEC_B, DEC_T)) for row in _NEW_ROWS.values()]


def kernel(**inputs):
    import numpy as _np
    import concourse.bacc as _bacc
    from concourse import mybir as _mybir
    from concourse.bass_utils import run_bass_kernel_spmd as _run

    nc = _bacc.Bacc("TRN2", target_bir_lowering=False, num_devices=1)
    arrays, io, outs = {}, {}, []
    for name in _INS:
        a = _np.ascontiguousarray(inputs[name])
        arrays[f"in_{name}"] = a
        io[name] = nc.dram_tensor(f"in_{name}", a.shape, _mybir.dt.from_np(a.dtype), kind="ExternalInput").ap()
    arrays["in_consts"] = const_table()
    io["consts"] = nc.dram_tensor("in_consts", arrays["in_consts"].shape, _mybir.dt.float32, kind="ExternalInput").ap()
    for i, (shape, dtype) in enumerate(_OUTS):
        outs.append(nc.dram_tensor(f"out_{i}", shape, _mybir.dt.from_np(_np.dtype(dtype)), kind="ExternalOutput").ap())
    build(nc, io, outs, PLAN)
    r = _run(nc, [arrays], core_ids=[0])
    return tuple(r.results[0][f"out_{i}"] for i in range(len(_OUTS)))
```

```python
from contextlib import ExitStack
import math

import numpy as np

import concourse.bass as bass
from concourse import mybir

F32 = mybir.dt.float32
F32R = mybir.dt.float32r
ALU = mybir.AluOpType
ACT = mybir.ActivationFunctionType
AX_X = mybir.AxisListType.X

P = 128
D = 1024
KD = D // P
PROMPT = 512
DEC_B, DEC_T = 8, 16
PAST = 256
TILES = PROMPT // P + DEC_B * DEC_T // P
PT = PROMPT // P
TOK = TILES * P
DEPTH = 2
D_FF = 2816
D_PLE = 256
EPS = 1e-6
HEAD = 3
HALF = 512

FB = D_FF // P // 2
GA = 3 * P
GU_PIECES = 4
CH = FB

SB_HEADS, HD = 8, 64
DF_HEADS = 4
DF_ROT = HD // 4
ROPE_THETA = 500000.0
MLA_HEADS, NOPE, ROPE, VD = 16, 64, 32, 64
QD = NOPE + ROPE
Q_LORA, KV_LORA = 384, 256
MLA_THETA = 10000.0
MLA_IN = Q_LORA + KV_LORA + ROPE
Z_MOST = 20.0
BIG = float(2.0 ** 100)


def const_map():
    widths = [("neg_tri", P), ("neg_ones", P), ("diag", P), ("batch_tri", P), ("cos_d", TILES * DF_ROT // 2),
              ("sin_d", TILES * DF_ROT // 2), ("comp0", 1), ("comp1", 1), ("merge", DF_HEADS * DEC_T), ("row_mask", P), ("col_mask", P),
              ("batch_mask", P), ("cos_m", TILES * ROPE // 2), ("sin_m", TILES * ROPE // 2)]
    out, n = {}, 0
    for name, w in widths:
        out[name] = (n, w)
        n += w
    out["end"] = n
    return out


CONSTS = const_map()


def positions():
    return np.concatenate([np.arange(PROMPT), np.tile(PAST + np.arange(DEC_T), DEC_B)]).astype(np.float32)


def rope_table(rot, theta):
    half = rot // 2
    inv = np.float32(theta) ** (-(np.arange(half, dtype=np.float32) * np.float32(2.0 / rot)))
    ang = positions()[:, None] * inv.astype(np.float32)[None, :]
    lay = lambda a: a.reshape(TILES, P, half).transpose(1, 0, 2).reshape(P, TILES * half).astype(np.float32)
    return lay(np.cos(ang)), lay(np.sin(ang))


def const_table():
    t = np.zeros((P, CONSTS["end"]), np.float32)

    def put(name, value, rows=P):
        a, n = CONSTS[name]
        t[0:rows, a:a + n] = value

    k, q = np.arange(P)[:, None], np.arange(P)[None, :]
    put("neg_tri", -(k >= q).astype(np.float32))
    put("neg_ones", -1.0)
    put("diag", k < q)
    put("batch_tri", (k // DEC_T == q // DEC_T) & (k % DEC_T < q % DEC_T))
    cos, sin = rope_table(DF_ROT, ROPE_THETA)
    put("cos_d", cos)
    put("sin_d", sin)
    cos, sin = rope_table(ROPE, MLA_THETA)
    put("cos_m", cos)
    put("sin_m", sin)
    put("comp0", (k // DEC_T) % 2 == 0)
    put("comp1", (k // DEC_T) % 2 == 1)
    ht = np.arange(DF_HEADS * DEC_T)[None, :]
    put("merge", (k // (2 * DEC_T) == ht // DEC_T) & (k % DEC_T == ht % DEC_T))
    put("row_mask", np.where(q < P // 2, -BIG, 0.0), 1)
    put("col_mask", q >= P // 2, 1)
    put("batch_mask", np.where(np.arange(DEC_B)[:, None] == q // DEC_T, 0.0, -BIG), DEC_B)
    return t


def encoder(nc, io):
    ctx = ExitStack()
    with ctx:
        def sem(name):
            return ctx.enter_context(nc.semaphore(name))

        base0 = (nc.sbuf_base + 31) // 32 * 32
        cursor = [base0]

        def region(nbytes):
            start = cursor[0]
            cursor[0] += (nbytes + 31) // 32 * 32
            return start

        def place(name, shape, dt, offset):
            return nc.alloc_sbuf_tensor_at(name, shape, dt, offset=offset)

        X = place("x_rows", [P, TILES, D], F32, region(TILES * D * 4))
        r_xt = region(2 * KD * TOK * 4)
        XT = [place("xt_hi", [P, KD, TOK], F32R, r_xt), place("xt_lo", [P, KD, TOK], F32R, r_xt + KD * TOK * 4)]
        r_y = region(TILES * D * 4)
        Y = place("y_rows", [P, TILES, D], F32, r_y)
        r_h = region(2 * FB * TOK * 4)
        HT = [place("ht_hi", [P, FB, TOK], F32R, r_h), place("ht_lo", [P, FB, TOK], F32R, r_h + FB * TOK * 4)]
        r_gu = region(2 * GU_PIECES * HALF * 4)
        gu_raw = place("gu_raw", [P, GU_PIECES, 4, P], F32, r_gu)
        gu_lo = place("gu_lo", [P, GU_PIECES, 4, P], F32R, r_gu)
        gu_hi = place("gu_hi", [P, GU_PIECES, 4, P], F32R, r_gu + GU_PIECES * HALF * 4)
        r_ch = region(2 * CH * HALF * 4)
        ch_raw = place("ch_raw", [P, CH, HALF], F32, r_ch)
        ch_lo = place("ch_lo", [P, CH, HALF], F32R, r_ch)
        ch_hi = place("ch_hi", [P, CH, HALF], F32R, r_ch + CH * HALF * 4)
        g_post = place("g_post", [P, D], F32, region(D * 4))
        g_pre = place("g_pre", [P, D], F32, region(D * 4))
        SG = place("silu_gate", [P, TOK], F32, region(TOK * 4))
        ident = place("ident", [P, P], F32, region(P * 4))
        ssq = place("ssq", [P, TILES, 4], F32, region(TILES * 4 * 4))
        rs = place("rs", [P, TILES, 2], F32, region(TILES * 2 * 4))
        minus_half = place("minus_half", [P, 1], F32, region(4))
        one = place("one", [P, 1], F32, region(4))
        eps_col = place("eps_col", [P, 1], F32, region(4))
        exact_r = place("exact_masks", [P, 3 * P], F32R, region(3 * P * 4))
        exact_id = place("exact_id", [P, DEC_B], F32R, region(DEC_B * 4))
        at_cols = place("at_cols", [P, 4, 4], F32, region(64))
        assert cursor[0] <= nc.sbuf_usable_end, (cursor[0], nc.sbuf_usable_end)

        exact_raw = place("exact_raw", [P, 3 * P], F32, r_h)

        p_raw = place("p_raw", [P, TILES, D_PLE], F32, r_gu)
        PTT = [place(f"pt_{w}", [P, D_PLE // P, TOK], F32R, r_gu + 5120 * (i + 1)) for i, w in enumerate(("hi", "lo"))]
        GT = place("gate", [P, 2, HALF], F32, r_h)

        def at_y(name, shape, offset):
            return place(name, shape, F32, r_y + offset)

        OT = place("mixed", [P, KD, TOK], F32, r_xt + KD * TOK * 4)
        rows_in = at_y("rows_in", [P, TILES, HALF], 0)
        QKV = {n: at_y(n, [P, 4, TOK] if n[3] != "v" else [P, TILES, HALF], 10240 * (i + 1))
               for i, n in enumerate(("sb_q", "sb_k", "sb_v", "df_q", "df_k", "df_v"))}
        k_raw = at_y("k_raw", [P, 2, 2, HALF], 71680)
        v_raw = at_y("v_raw", [P, 2, 2, HALF], 79872)
        consts = at_y("consts", [P, CONSTS["end"]], 88064)
        assert 88064 + 4 * CONSTS["end"] <= r_ch - r_y
        kt = place("kt", [P, 2, 4, PAST], F32, g_post.manual_sbuf_range[0])
        rope_tmp = place("rope_tmp", [P, 4, 64], F32, SG.manual_sbuf_range[0])
        sp_buf = place("sp_buf", [P, 2, 1280], F32, r_xt)
        e_buf = place("e_buf", [P, 4, HALF], F32, r_xt + 10240)
        w_buf = place("w_buf", [P, 2, HALF], F32, r_ch + KD * HALF * 4)
        p_buf = place("p_buf", [P, 2, HALF], F32, r_xt)
        pt_buf = place("pt_buf", [P, 2, HALF], F32, r_xt + 4096)
        qbd = {n: at_y("qbd_" + n, [P, 4, DEC_B, 2, DEC_T], 4096 * i) for i, n in enumerate(("sb_q", "df_q"))}
        lam_rows = place("lam_rows", [P, 4, HD], F32, SG.manual_sbuf_range[0] + 1024)
        lam_cols = place("lam_cols", [P, 8], F32, SG.manual_sbuf_range[0] + 2048)
        sub_sq_buf = at_y("sub_sq_buf", [P, DF_HEADS, TOK], 10240)
        sub_rs_buf = at_y("sub_rs_buf", [P, DF_HEADS, TOK], 20480)

        c_in = at_y("c_in", [P, TILES, MLA_IN], 0)
        V = at_y("mla_v", [P, PT, MLA_HEADS * VD], 0)
        OLT = at_y("out_latent_t", [P, DEC_B, 2, 2, P], 0)
        CQT = [place(f"cq_t_{w}", [P, Q_LORA // P, TOK], F32R, r_y + 16384 + 7680 * i) for i, w in enumerate(("hi", "lo"))]
        q_lat_t = at_y("q_latent_t", [P, 2, DEC_B, MLA_HEADS, DEC_T], 16384)
        lat_t = at_y("latent_t", [P, 2, TOK], 32768)
        kr_t = at_y("krope_t", [P, TOK], 37888)
        lat_new = at_y("latent_new", [P, KV_LORA], 40448)
        W_uk = at_y("w_uk", [P, 2, MLA_HEADS * NOPE], 41472)
        at_q = 49664
        q_t = at_y("q_t", [P, MLA_HEADS, TOK], at_q)
        W_uv = [at_y(f"w_uv{i}", [P, 2, MLA_HEADS * VD], at_q) for i in range(2)]
        sq_tmp = at_y("sq_tmp", [P, 2, Q_LORA], at_q + 8192)
        lat_raw = at_y("lat_raw", [P, 3, 2, KV_LORA], at_q + 8192)
        kr_raw = at_y("kr_raw", [P, 3, 2, ROPE], at_q + 14336)
        lat_bt = at_y("lat_bt", [P, 2, 2, PAST], at_q + 15360)
        kr_bt = at_y("kr_bt", [P, 2, PAST], at_q + 19456)
        m_first, m_end = CONSTS["row_mask"][0], CONSTS["end"]
        m_consts = at_y("m_consts", [P, m_end - m_first], 90624)
        assert at_q + 4 * MLA_HEADS * TOK <= 90624 and 90624 + 4 * (m_end - m_first) <= r_ch - r_y
        q_rows = place("q_rows", [P, TILES, 4 * QD], F32, r_xt)
        k_t = place("k_t", [P, 2, PROMPT], F32, r_xt + 8192)
        qr_t = place("q_rope_t", [P, DEC_B, MLA_HEADS, DEC_T], F32, r_xt + 12288)
        g0 = g_post.manual_sbuf_range[0]
        mg_q = place("mg_q", [P, Q_LORA], F32, g0)
        mg_kv = place("mg_kv", [P, KV_LORA], F32, g0 + 4 * Q_LORA)
        w_ukt = place("w_ukt", [P, 2, 2 * P], F32, g0 + 2560)
        mc = place("mc_cols", [P, 2, TILES, 2], F32, g0 + 4608)

        def const(name, rows=P):
            a, n = CONSTS[name]
            return consts[0:rows, a:a + n]

        def mconst(name, rows=P):
            a, n = CONSTS[name]
            return m_consts[0:rows, a - m_first:a - m_first + n]

        def exact(name, rows):
            a = CONSTS[name][0] - m_first
            return exact_r[0:rows, a:a + P]

        PS = ctx.enter_context(nc.psum_tensor("ps", [P, 8, HALF], F32))
        Y_BANK = [0, 4, 5, 6, 7]
        TR_BANK = [(1, 2), (3, 0), (1, 2), (3, 7), (1, 2)]
        GATE_A, GATE_B, UP_A, UP_B = 4, 5, 6, 7

        x_in = [sem(f"x_in{t}") for t in range(TILES)]
        gains_in = sem("gains_in")
        const_ok = sem("const_ok")
        gu_landed = [sem(f"gu_landed{s}") for s in range(GU_PIECES)]
        gu_hi_ok, gu_lo_ok, gu_used = sem("gu_hi_ok"), sem("gu_lo_ok"), sem("gu_used")
        ch_landed = [sem(f"ch_landed{c}") for c in range(CH)]
        ch_hi_ok, ch_lo_ok, ch_used = sem("ch_hi_ok"), sem("ch_lo_ok"), sem("ch_used")
        y_mm, y_out = sem("y_mm"), sem("y_out")
        gate_mm, up_mm = sem("gate_mm"), sem("up_mm")
        silu_ok, h_mul, h_hi_ok, sg_free = sem("silu_ok"), sem("h_mul"), sem("h_hi_ok"), sem("sg_free")
        ss1_ok, ss2_ok = sem("ss1_ok"), sem("ss2_ok")
        eps_ok, rs1_ok, rs2_ok = sem("eps_ok"), sem("rs1_ok"), sem("rs2_ok")
        post_ok, x_ok, xn_ok = sem("post_ok"), sem("x_ok"), sem("xn_ok")
        tr_ok, xt_hi_ok, xt_lo_ok = sem("tr_ok"), sem("xt_hi_ok"), sem("xt_lo_ok")
        ple = {k: sem(f"ple_{k}") for k in ("in", "tr", "hi", "lo", "gate", "pin")}
        out_done = sem("out_done")
        consts_in = sem("consts_in")
        exact_in, exact_ok = sem("exact_in"), sem("exact_ok")
        rope_part, rope_ok, st_tr, st_cp = (sem(n) for n in ("rope_part", "rope_ok", "st_tr", "st_cp"))
        st_out = {n: sem("st_out_" + n) for n in ("sb_k", "sb_v", "df_k", "df_v", "lat", "kr")}
        kraw_in = [sem(f"kraw_in{b}") for b in range(2)]
        vraw_in = [sem(f"vraw_in{b}") for b in range(2)]
        kt_tr, kt_ok = sem("kt_tr"), sem("kt_ok")
        sb_z, sb_min, sb_exp, sb_ln, sb_sp, sb_spm, sb_acc, sb_w, sb_wm, sb_pv = (
            sem("sb_" + n) for n in ("z", "min", "exp", "ln", "sp", "spm", "acc", "w", "wm", "pv"))
        at_s, at_max, at_exp, at_r, at_p, at_t, at_pt, at_pv, o_out = (
            sem(n) for n in ("at_s", "at_max", "at_exp", "at_r", "at_p", "at_t", "at_pt", "at_pv", "o_out"))
        lam_in, lam_step, qbd_ok = sem("lam_in"), sem("lam_step"), sem("qbd_ok")
        sub_sq, sub_mm, sub_ln, sub_rs, sub_ok = (sem("sub_" + n) for n in ("sq", "mm", "ln", "rs", "ok"))
        ot_hi, ot_lo = sem("ot_hi"), sem("ot_lo")
        mg_in, mw_in, muv_in = sem("mg_in"), sem("mw_in"), [sem(f"muv_in{i}") for i in range(2)]
        mc_ss, mc_eps, mc_rs, mc_n, mc_tr, mc_hi, mc_lo, mc_lat = (
            sem("mc_" + n) for n in ("ss", "eps", "rs", "n", "tr", "hi", "lo", "lat"))
        v_mm, v_ok, mq_tr, mq_cp, qr_cp, krt_cp, wt_tr, wt_cp, ql_mm, ql_cp, uo_mm, uo_ok, new_cp = (
            sem(n) for n in ("v_mm", "v_ok", "mq_tr", "mq_cp", "qr_cp", "krt_cp", "wt_tr", "wt_cp", "ql_mm", "ql_cp",
                             "uo_mm", "uo_ok", "new_cp"))
        lat_in = [sem(f"lat_in{b}") for b in range(3)]

        passes = []

        def new_pass(K, src):
            passes.append({"i": len(passes), "K": K, "n": src.shape[1] if src is not None else HALF, "src": src,
                           "uses": [sum(q["K"] > c for q in passes) for c in range(CH)]})
            return passes[-1]

        def col_half(w, h):
            return w[:, h * HALF:(h + 1) * HALF]

        stages = [{"kind": "start", "passes": []}]
        for kind, layer, which in io["plan"]:
            st = {"kind": kind, "layer": layer}
            if kind == "ffn":
                st["n"] = sum(q["kind"] == "ffn" for q in stages)
                st["gu"], st["dn"] = io[f"ffn{which}_gu"][layer], io[f"ffn{which}_dn"][layer]
                st["passes"] = [new_pass(FB, None) for _ in range(4)]
                st["g"], st["c"] = (1 if which == 1 else 5), 0.5
            elif kind == "ple":
                st["n"] = sum(q["kind"] == "ple" for q in stages)
                st["passes"] = [new_pass(D_PLE // P, col_half(io["ple_in"][layer], h)) for h in range(2)]
                st["passes"] += [new_pass(KD, col_half(io["ple_gate"][layer], h)) for h in range(2)]
                st["g"], st["c"] = 7, 1.0
            elif kind == "ab":
                st["passes"] = [new_pass(KD, col_half(io["ab_in"][0], h)) for h in range(6)]
                st["passes"] += [new_pass(KD, col_half(io["ab_out"][0], h)) for h in range(2)]
                st["g"], st["c"] = 3, 1.0
            elif kind == "mla":
                w = io["mla_in"][0]
                st["passes"] = [new_pass(KD, w[:, 0:HALF]), new_pass(KD, w[:, HALF:MLA_IN])]
                st["passes"] += [new_pass(Q_LORA // P, io["mla_uq"][0][:, g * 4 * QD:(g + 1) * 4 * QD])
                                 for g in range(MLA_HEADS // 4)]
                st["passes"] += [new_pass(KD, col_half(io["mla_out"][0], h)) for h in range(2)]
                st["g"], st["c"] = 3, 1.0
            stages.append(st)
        for prev, st in zip(stages, stages[1:]):
            assert st["kind"] != "ple" or prev["kind"] == "ffn"

        for k, st in enumerate(stages):
            st["k"] = k
            if k > 0:
                st["post"] = io["norms"][st["layer"], st["g"]]
                nxt = (st["layer"], st["g"] + 1) if st["g"] < 7 else (st["layer"] + 1, 0)
            else:
                nxt = (io["plan"][0][1], {"ffn": 0, "ple": 6, "ab": 2, "mla": 2}[io["plan"][0][0]])
                if io["plan"][0][0] == "ffn" and io["plan"][0][2] == 2:
                    nxt = (nxt[0], 4)
            st["pre"] = None if k == len(stages) - 1 else io["norms"][nxt[0], nxt[1]]
            st["last"] = st["passes"][-1]["i"] if st["passes"] else None
            st["next"] = stages[k + 1] if k + 1 < len(stages) else None
            st["early"] = st["next"] is not None and st["next"]["kind"] == "ffn"
            st["to_ple"] = st["next"] is not None and st["next"]["kind"] == "ple"
            st["tr_bank"] = [(1, 2), (3, 0), (1, 2), (1, 2), (1, 2)] if st["to_ple"] else TR_BANK

        def ple_evict(b, part):
            if b < 2:
                return PTT[part][:, b, 0:PROMPT], PS[:, 1 + b, :]
            return PTT[part][:, :, PROMPT:TOK], PS[:, 3, 0:2 * P].rearrange("p (b n) -> p b n", b=2)

        def tok(t):
            return slice(t * P, (t + 1) * P)

        def counts(p, c, total=CH):
            last = p["K"] - 1 - (CH - total)
            return total - last if c == last else 1

        def prev_k(p):
            return passes[p["i"] - 1]["K"] if p["i"] else 2

        def summed(p, t):
            return TILES * (p + 1) + t + 1

        def evicted(p, t):
            return TILES * (p + 1) + t + 1

        S_BANK = [4, 5]
        T_BANK = [1, 2]
        O_BANK = [6, 7]

        def prep_bank(pr, b):
            return (1, 2)[b] if pr["kind"] == "stick" else (0, 3)[b]

        stick = []
        soft = []
        groups = []
        preps = []

        def new_group(dst, bank_cols=HALF):
            groups.append({"i": len(groups), "dst": dst, "n": bank_cols})
            return groups[-1]

        mixers = [st for st in stages if st["kind"] in ("ab", "mla")]
        for st in mixers:
            st["soft0"], st["stick0"] = len(soft), len(stick)
            st["before"] = mixers.index(st)
            st["rot0"] = 2 * TILES if st["before"] else 0
            if st["kind"] == "ab":
                for h in range(SB_HEADS):
                    if h % 2 == 0:
                        g = new_group(OT[:, h // 2, 0:PROMPT])
                    for kb in reversed(range(PT)):
                        N = PROMPT - kb * P
                        r = slice(HD * (h % 2), HD * (h % 2) + HD)
                        off = [0, 512, 896, 1152]
                        stick.append({
                            "g": g, "N": N, "sp": sp_buf[:, h % 2, off[kb]:off[kb] + N], "prep": None,
                            "z": [(slice(0, N), QKV["sb_k"][r, h // 2, kb * P:kb * P + P],
                                   QKV["sb_q"][r, h // 2, kb * P:PROMPT])],
                            "later": [(slice((k2 - kb) * P, N), sp_buf[:, h % 2, off[k2]:off[k2] + PROMPT - k2 * P])
                                      for k2 in range(kb + 1, PT)],
                            "mask": (slice(0, P), None, "diag"),
                            "pv": [(r, slice(kb * P, PROMPT), QKV["sb_v"][:, kb, h * HD:h * HD + HD], slice(0, N),
                                    kb == PT - 1)],
                            "first": h % 2 == 0 and kb == PT - 1, "last": h % 2 == 1 and kb == 0})
                gs = new_group(OT[:, 0:4, PROMPT:TOK])
                for b in range(DEC_B):
                    preps.append({"i": len(preps), "k": io["cache_sb_k"][0, b], "v": io["cache_sb_v"][0, b],
                                  "kind": "stick", "unit": len(stick), "last": len(stick)})
                    pr = preps[-1]
                    par = pr["i"] % 2
                    z, pv = [], []
                    for fb in range(SB_HEADS // 2):
                        for kb in range(3):
                            c0 = kb * P + fb * 2 * DEC_T
                            key = kt[:, par, fb, kb * P:kb * P + P] if kb < 2 else QKV["sb_k"][:, fb, PROMPT:TOK]
                            z.append((slice(c0, c0 + 2 * DEC_T), key, qbd["sb_q"][:, fb, b].rearrange("p c t -> p (c t)")))
                    for h in range(SB_HEADS):
                        r = slice(HD * (h % 2), HD * (h % 2) + HD)
                        for kb in range(3):
                            c0 = kb * P + h * DEC_T
                            val = (v_raw[:, par, kb, :] if kb < 2 else QKV["sb_v"][:, PT, :])[:, h * HD:h * HD + HD]
                            pv.append((r, slice((h // 2) * P + b * DEC_T, (h // 2) * P + (b + 1) * DEC_T), val,
                                       slice(c0, c0 + DEC_T), kb == 0))
                    sp = sp_buf[:, b % 2, 0:3 * P]
                    stick.append({"g": gs, "N": 3 * P, "sp": sp, "prep": pr, "z": z, "pv": pv,
                                  "later": [(slice(0, P), sp[:, P:2 * P]), (slice(0, P), sp[:, 2 * P:3 * P]),
                                            (slice(P, 2 * P), sp[:, 2 * P:3 * P])],
                                  "mask": (slice(2 * P, 3 * P), b, "batch"),
                                  "first": b == 0, "last": b == DEC_B - 1})
                for h in range(DF_HEADS):
                    g = new_group(OT[:, 4 + h, 0:PROMPT])
                    for qb in range(PT):
                        for c in range(2):
                            r = slice(HD * c, HD * c + HD)
                            N = (qb + 1) * P
                            soft.append({
                                "g": g, "N": N, "prep": None, "coef": "neg_lam" if c else None,
                                "s": [(slice(0, P), slice(0, N), QKV["df_q"][r, h, qb * P:qb * P + P],
                                       QKV["df_k"][r, h, 0:N], True),
                                      (slice(0, P), slice(qb * P, N), exact("row_mask", 1), exact("col_mask", 1), False)],
                                "pv": [(slice(0, P), slice(qb * P, N), QKV["df_v"][:, j, h * P:h * P + P],
                                        (j * P, P), c == 0 and j == 0) for j in range(qb + 1)],
                                "first": qb == 0 and c == 0, "last": qb == PT - 1 and c == 1})
                gs = new_group(OT[:, 4:8, PROMPT:TOK])
                for b in range(DEC_B):
                    preps.append({"i": len(preps), "k": io["cache_df_k"][0, b], "v": io["cache_df_v"][0, b],
                                  "kind": "soft", "unit": len(soft), "last": len(soft)})
                    pr = preps[-1]
                    par = pr["i"] % 2
                    s_list, pv = [], []
                    for h in range(DF_HEADS):
                        ro = slice(32 * h, 32 * h + 32)
                        q = qbd["df_q"][:, h, b].rearrange("p c t -> p (c t)")
                        s_list.append((ro, slice(0, PAST), q, kt[:, par, h, :], True))
                        s_list.append((ro, slice(PAST, PAST + P), q, QKV["df_k"][:, h, PROMPT:TOK], False))
                        for j in range(3):
                            val = (v_raw[:, par, j, :] if j < 2 else QKV["df_v"][:, PT, :])[:, h * P:h * P + P]
                            pv.append((slice(0, P), slice(h * P + b * DEC_T, h * P + (b + 1) * DEC_T), val,
                                       (j * DF_HEADS * DEC_T + h * DEC_T, DEC_T), j == 0))
                    s_list.append((slice(0, P), slice(PAST, PAST + P), exact_id[0:DEC_B, b:b + 1].to_broadcast([DEC_B, P]),
                                   exact("batch_mask", DEC_B), False))
                    soft.append({"g": gs, "N": PAST + P, "prep": pr, "coef": "c_rows", "s": s_list, "pv": pv,
                                 "first": b == 0, "last": b == DEC_B - 1})
            else:
                st["prep0"] = len(preps)
                for h in range(MLA_HEADS):
                    if h % 2 == 0:
                        g = new_group(OT[:, h // 2, 0:PROMPT])
                    preps.append({"i": len(preps), "kind": "head", "h": h, "unit": len(soft), "last": len(soft) + PT - 1})
                    for qb in range(PT):
                        N = (qb + 1) * P
                        r = slice(VD * (h % 2), VD * (h % 2) + VD)
                        soft.append({
                            "g": g, "N": N, "prep": preps[-1] if qb == 0 else None, "coef": None,
                            "s": [(slice(0, P), slice(0, N), q_t[0:QD, h, qb * P:qb * P + P], k_t[0:QD, h % 2, 0:N], True),
                                  (slice(0, P), slice(qb * P, N), exact("row_mask", 1), exact("col_mask", 1), False)],
                            "pv": [(r, slice(qb * P, N), V[:, j, h * VD:h * VD + VD], (j * P, P), j == 0)
                                   for j in range(qb + 1)],
                            "first": h % 2 == 0 and qb == 0, "last": h % 2 == 1 and qb == PT - 1})
                st["sample0"] = len(soft)
                for b in range(DEC_B):
                    g = new_group(OLT[:, b].rearrange("p a c n -> p (a c n)"))
                    preps.append({"i": len(preps), "kind": "latent", "b": b, "unit": len(soft), "last": len(soft) + 1})
                    for hh in range(2):
                        hs = slice(8 * hh, 8 * hh + 8)
                        ops = [(q_lat_t[:, c, b, hs, :].rearrange("p h t -> p (h t)"), lat_bt[:, b % 2, c, :],
                                lat_t[:, c, PROMPT:TOK]) for c in range(2)]
                        ops += [(qr_t[0:ROPE, b, hs, :].rearrange("p h t -> p (h t)"), kr_bt[0:ROPE, b % 2, :],
                                 kr_t[0:ROPE, PROMPT:TOK])]
                        s_list = []
                        for j, (q, old, new) in enumerate(ops):
                            s_list.append((slice(0, P), slice(0, PAST), q, old, j == 0))
                            s_list.append((slice(0, P), slice(PAST, PAST + P), q, new, False))
                        s_list.append((slice(0, P), slice(PAST, PAST + P), exact_id[0:DEC_B, b:b + 1].to_broadcast([DEC_B, P]),
                                       exact("batch_mask", DEC_B), False))
                        pv = [(slice(0, P), slice(hh * 2 * P + c * P, hh * 2 * P + (c + 1) * P),
                               (lat_raw[:, b % 3, j, :] if j < 2 else lat_new[:])[:, c * P:(c + 1) * P], (j * P, P), j == 0)
                              for c in range(2) for j in range(3)]
                        soft.append({"g": g, "N": PAST + P, "prep": preps[-1] if hh == 0 else None, "coef": None,
                                     "s": s_list, "pv": pv, "first": hh == 0, "last": hh == 1})
            st["soft1"], st["stick1"], st["groups1"] = len(soft), len(stick), len(groups)
        six_banks_for = 4 * 6
        bank_user = {}
        for n, u in enumerate(stick):
            u["bank"] = [3, 4, 5, 0, 1, 2][n % 6] if n < six_banks_for else [3, 4, 5, 0][n % 4]
            u["bank_before"] = bank_user.get(u["bank"])
            bank_user[u["bank"]] = n
        for lst, kind in ((stick, "stick"), (soft, "soft")):
            for n, u in enumerate(lst):
                u["i"] = n
                u["w"] = DF_HEADS * DEC_T if u["prep"] and u["prep"]["kind"] == "soft" else P
                if u["last"]:
                    u["g"]["end"] = (kind, n)

        def flat(a):
            names = " ".join("abcd"[:len(a.shape) - 1])
            return a.rearrange(f"r {names} -> r ({names})") if len(a.shape) > 2 else a

        def sub_part(buf, h):
            if h < DF_HEADS:
                return buf[:, h, 0:PROMPT], PS[:, h, :]
            return buf[:, :, PROMPT:TOK], PS[:, h, :].rearrange("p (h n) -> p h n", h=DF_HEADS)

        def groups_end(st):
            return st["groups1"]

        def mixed_done(st):
            return (sub_ok, DF_HEADS) if st["kind"] == "ab" else (uo_ok, 2)

        def keys_done(pr):
            return (sb_z if pr["kind"] == "stick" else at_s), pr["last"] + 1

        def unit_done(pr):
            return (sb_pv if pr["kind"] == "stick" else at_pv), pr["last"] + 1

        block = ctx.enter_context(nc.Block())

        @block.sync
        def _(sp):
            def load_gu(st, g):
                w = st["gu"].rearrange("(k p) n -> p k n", p=P)
                for s in range(GU_PIECES):
                    blk = g + st["n"] * 2 * FB
                    if s % 2 == 0:
                        sp.wait_ge(gu_used, blk * 2 + s // 2 + 1)
                    else:
                        sp.wait_ge(gate_mm if s == 1 else up_mm, blk * 2 + 2)
                    q, kh = s // 2, s % 2
                    sp.dma_start(gu_raw[:, s], w[:, kh * 4:kh * 4 + 4, bass.ds(g * P + q * D_FF, P)]
                                 ).then_inc(gu_landed[s], 16)

            def load_chunk(p, prev_k, c, src, n=HALF):
                if c < prev_k - 1:
                    sp.wait_ge(ch_used, p * (CH - 1) + c + 1)
                else:
                    sp.wait_ge(y_mm, p * TILES + TILES)
                sp.dma_start(ch_raw[:, c, 0:n], src).then_inc(ch_landed[c], 16)

            def load_preps(kind):
                mine = [q for q in preps if q["kind"] == kind]
                lag = 4 if kind == "stick" else 3
                for n in range(len(mine) + lag):
                    if n < len(mine):
                        i, par = mine[n]["i"], mine[n]["i"] % 2
                        if i >= 2:
                            sp.wait_ge(kt_tr, 2 * (i - 1))
                        sp.dma_start(k_raw[:, par], flat(mine[n]["k"]).rearrange("(b p) n -> p b n", p=P)
                                     ).then_inc(kraw_in[par], 16)
                    if n >= lag:
                        i, par = mine[n - lag]["i"], mine[n - lag]["i"] % 2
                        if i >= 2:
                            sp.wait_ge(*unit_done(preps[i - 2]))
                        sp.dma_start(v_raw[:, par], flat(mine[n - lag]["v"]).rearrange("(b p) n -> p b n", p=P)
                                     ).then_inc(vraw_in[par], 16)

            def load_pass(p):
                for c in range(p["K"]):
                    load_chunk(p["i"], prev_k(p), c, p["src"][c * P:(c + 1) * P, :], p["n"])

            def rows_out(name, src, done, n):
                sp.wait_ge(done, n)
                dst = io[name + "_out"]
                sp.dma_start(dst[0], src[:, 0:PT, :]).then_inc(st_out[name], 16)
                sp.dma_start(dst[1], src[:, PT, :]).then_inc(st_out[name], 16)

            for t in range(TILES):
                sp.dma_start(X[:, t, :], io["x_tiles"][t]).then_inc(x_in[t], 16)
            for st in stages:
                if st["kind"] == "ffn":
                    rows = st["dn"].rearrange("(f p) n -> p f n", p=P)
                    p0 = st["passes"][0]["i"]
                    with sp.Fori(0, 2) as fh:
                        load_gu(st, fh * FB)
                        for c in range(FB):
                            load_chunk(fh * 2 + p0, KD, c, rows[:, bass.ds(fh * FB + c, 1), 0:HALF].rearrange("p a n -> p (a n)"))
                            if c < FB - 1:
                                load_gu(st, fh * FB + c + 1)
                        for c in range(FB):
                            load_chunk(fh * 2 + p0 + 1, FB, c,
                                       rows[:, bass.ds(fh * FB + c, 1), HALF:D].rearrange("p a n -> p (a n)"))
                elif st["kind"] == "ab":
                    load_pass(st["passes"][0])
                    sp.wait_ge(y_mm, st["passes"][0]["i"] * TILES + TILES)
                    sp.dma_start(consts[:], io["consts"]).then_inc(consts_in, 16)
                    for q in range(1, 6):
                        load_pass(st["passes"][q])
                        p = st["passes"][q - 1]["i"]
                        if q == 2:
                            rows_out("sb_k", rows_in, y_out, evicted(p, TILES - 1))
                        if q == 3:
                            rows_out("sb_v", QKV["sb_v"], y_out, evicted(p, TILES - 1))
                        if q == 5:
                            rows_out("df_k", rows_in, rope_ok, 2 * 2 * TILES)
                    load_pass(st["passes"][6])
                    rows_out("df_v", QKV["df_v"], y_out, evicted(st["passes"][5]["i"], TILES - 1))
                    load_preps("stick")
                    load_preps("soft")
                    load_pass(st["passes"][7])
                elif st["kind"] == "mla":
                    ps = st["passes"]
                    w_uv = io["mla_uv"][0].rearrange("(k p) n -> p k n", p=P)
                    load_pass(ps[0])
                    sp.wait_ge(y_mm, ps[0]["i"] * TILES + TILES)
                    sp.dma_start(m_consts[:], io["consts"][:, m_first:m_end]).then_inc(mg_in, 16)
                    sp.wait_ge(xn_ok, 2 * TILES * st["k"])
                    sp.dma_start(mg_q[:], io["mla_q_norm"][0].partition_broadcast(P)).then_inc(mg_in, 16)
                    sp.dma_start(mg_kv[:], io["mla_kv_norm"][0].partition_broadcast(P)).then_inc(mg_in, 16)
                    load_pass(ps[1])
                    sp.dma_start(W_uv[0][:], w_uv).then_inc(muv_in[0], 16)
                    sp.dma_start(W_uk[:], io["mla_uk"][0].rearrange("(k p) n -> p k n", p=P)).then_inc(mw_in, 16)
                    load_pass(ps[2])
                    rows_out("lat", c_in[:, :, Q_LORA:Q_LORA + KV_LORA], mc_n, 2 * TILES)
                    rows_out("kr", c_in[:, :, Q_LORA + KV_LORA:MLA_IN], rope_ok, 2 * (st["rot0"] + TILES))
                    for p in ps[3:7]:
                        load_pass(p)
                    sp.wait_ge(at_s, st["sample0"])
                    lat, kr = (io["cache_mla_" + n][0].rearrange("b (k p) n -> b p k n", p=P) for n in ("latent", "krope"))
                    for b in range(DEC_B):
                        if b == 3:
                            sp.dma_start(W_uv[1][:], w_uv).then_inc(muv_in[1], 16)
                        if b >= 3:
                            sp.wait_ge(at_pv, st["sample0"] + 2 * (b - 2))
                        sp.dma_start(lat_raw[:, b % 3], lat[b]).then_inc(lat_in[b % 3], 16)
                        sp.dma_start(kr_raw[:, b % 3], kr[b]).then_inc(lat_in[b % 3], 16)
                    load_pass(ps[7])
                elif st["kind"] == "ple":
                    for p in st["passes"]:
                        load_pass(p)
            for t in range(TILES):
                sp.wait_ge(x_ok, 2 * (TILES * (len(stages) - 2) + t) + 2)
                sp.dma_start(io["y_tiles"][t], X[:, t, :]).then_inc(out_done, 16)
            sp.wait_ge(out_done, 16 * TILES)
            for name in st_out:
                if any(st["kind"] == ("mla" if name in ("lat", "kr") else "ab") for st in stages):
                    sp.wait_ge(st_out[name], 2 * 16)

        @block.scalar
        def _(act):
            def hi_gu(blk):
                for s in range(GU_PIECES):
                    act.wait_ge(gu_landed[s], (blk + 1) * 16)
                    act.activation(gu_hi[:, s], gu_raw[:, s], ACT.Copy).then_inc(gu_hi_ok, 1)

            def hi_chunk(p, c, uses):
                act.wait_ge(ch_landed[c], (uses + 1) * 16)
                act.activation(ch_hi[:, c, 0:p["n"]], ch_raw[:, c, 0:p["n"]], ACT.Copy).then_inc(ch_hi_ok, counts(p, c))

            def hi_chunks(p, a, b):
                for c in range(a, min(b, p["K"])):
                    hi_chunk(p, c, p["uses"][c])

            def silu(blk):
                for b, bank, cols in ((0, GATE_A, slice(0, GA)), (1, GATE_B, slice(GA, TOK))):
                    act.wait_ge(gate_mm, blk * 2 + b + 3)
                    act.wait_ge(sg_free, blk * 2 + b + 1)
                    act.activation(SG[:, cols], PS[:, bank, 0:cols.stop - cols.start], ACT.Silu).then_inc(silu_ok, 1)

            def load_gains(st):
                if st["k"] > 0:
                    act.wait_ge(xn_ok, 2 * TILES * st["k"])
                    act.dma_start(g_post[:], st["post"].partition_broadcast(P)).then_inc(gains_in, 16)
                if st["pre"] is not None:
                    act.dma_start(g_pre[:], st["pre"].partition_broadcast(P)).then_inc(gains_in, 16)

            junk = [None, 0]

            def first_gu(st):
                if st["early"]:
                    hi_gu(st["next"]["n"] * 2 * FB)

            def tail(st, ahead):
                k = st["k"]

                def square(src, scale, t, which, h, done, n):
                    if junk[0] is not None:
                        act.wait_ge(junk[0], junk[1])
                    act.activation(SG[:, 0:HALF], src[:, t, h * HALF:(h + 1) * HALF], ACT.Square, scale=scale,
                                   accum_out=ssq[:, t, 2 * which + h:2 * which + h + 1]).then_inc(done, 1)
                    junk[:] = [done, n + 2 * t + h + 1]

                def sq1(t, h):
                    if h == 1 and ahead:
                        ahead(t)
                    act.wait_ge(y_out, evicted(st["last"] - (h == 0), t))
                    square(Y, 1.0 / (math.sqrt(D) * st["c"]), t, 0, h, ss1_ok, 2 * TILES * (k - 1))

                def sq2(t):
                    for h in range(2):
                        if k > 0:
                            act.wait_ge(x_ok, 2 * (TILES * (k - 1) + t) + h + 1)
                        else:
                            act.wait_ge(x_in[t], 16)
                        square(X, 1.0 / math.sqrt(D), t, 1, h, ss2_ok, 2 * TILES * k)

                def hi(t):
                    for b in range(2):
                        act.wait_ge(tr_ok, 2 * (TILES * k + t) + b + 1)
                        act.activation(XT[0][:, 4 * b:4 * b + 4, tok(t)], PS[:, st["tr_bank"][t][b], :], ACT.Copy
                                       ).then_inc(xt_hi_ok, 1)

                if k > 0 and st["kind"] == "ffn":
                    act.wait_ge(sg_free, 2 * 2 * FB * (st["n"] + 1) + 2)
                if k > 0:
                    sq1(0, 0)
                    sq1(0, 1)
                for t in range(TILES):
                    if t == TILES - 1 and st["pre"] is not None:
                        hi(2)
                    if k > 0 and t < TILES - 1:
                        sq1(t + 1, 0)
                    if st["pre"] is not None:
                        sq2(t)
                    if t == TILES - 2:
                        if k == 0:
                            first_gu(st)
                        if st["pre"] is not None:
                            hi(0)
                            hi(1)
                    if k > 0 and t < TILES - 1:
                        sq1(t + 1, 1)
                if st["pre"] is not None:
                    hi(3)
                    hi(4)

            def copy_kt(pr):
                i, par = pr["i"], pr["i"] % 2
                if i >= 2:
                    act.wait_ge(*keys_done(preps[i - 2]))
                for b in range(2):
                    act.wait_ge(kt_tr, 2 * i + b + 1)
                    if pr["kind"] == "head":
                        dst, src = k_t[0:NOPE, pr["h"] % 2, b * 256:(b + 1) * 256], PS[0:NOPE, prep_bank(pr, b), 0:256]
                    elif pr["kind"] == "latent" and b == 0:
                        dst, src = lat_bt[:, pr["b"] % 2, :, :], PS[:, prep_bank(pr, 0), :]
                    elif pr["kind"] == "latent":
                        dst, src = kr_bt[0:ROPE, pr["b"] % 2, :], PS[0:ROPE, prep_bank(pr, 1), 0:PAST]
                    else:
                        dst, src = kt[:, par, 2 * b:2 * b + 2, :], PS[:, prep_bank(pr, b), :]
                    act.activation(dst, src, ACT.Copy).then_inc(kt_ok, 1)

            def stick_act(units):
                L = len(units)
                for m in range(0, L + 2, 2):
                    pair, pair_before = units[m:m + 2], units[max(m - 2, 0):m]
                    for u in pair:
                        i, a = u["i"], e_buf[:, u["i"] % 4, 0:u["N"]]
                        act.wait_ge(sb_min, i + 1)
                        act.activation(a, a, ACT.Exp).then_inc(sb_exp, 1)
                    for u in pair:
                        i, a = u["i"], e_buf[:, u["i"] % 4, 0:u["N"]]
                        act.wait_ge(sb_exp, i + 1)
                        act.activation(a, a, ACT.Ln, bias=one[:]).then_inc(sb_ln, 1)
                    for u in units[m + 3:m + 4]:
                        if u["prep"]:
                            copy_kt(u["prep"])
                    for u in pair_before:
                        i = u["i"]
                        act.wait_ge(sb_acc, i + 1)
                        if i >= 2:
                            act.wait_ge(sb_pv, i - 1)
                        act.activation(w_buf[:, i % 2, 0:u["N"]], PS[:, u["bank"], 0:u["N"]], ACT.Exp).then_inc(sb_w, 1)
                    for u in units[m + 4:m + 5]:
                        if u["prep"]:
                            copy_kt(u["prep"])

            def soft_act(units):
                if units[0]["prep"]:
                    copy_kt(units[0]["prep"])
                for n in range(len(units) + 1):
                    if n < len(units):
                        u = units[n]
                        i = u["i"]
                        act.wait_ge(at_max, i + 1)
                        if i >= 2:
                            act.wait_ge(at_t, i - 1)
                        act.activation(p_buf[:, i % 2, 0:u["N"]], PS[:, S_BANK[i % 2], 0:u["N"]], ACT.Exp,
                                       bias=at_cols[:, i % 4, 0:1], accum_out=at_cols[:, i % 4, 1:2]).then_inc(at_exp, 1)
                    if n + 1 < len(units) and units[n + 1]["prep"]:
                        copy_kt(units[n + 1]["prep"])
                    if n > 0:
                        u = units[n - 1]
                        i = u["i"]
                        act.wait_ge(at_t, i + 1)
                        if i >= 2:
                            act.wait_ge(at_pv, i - 1)
                        n_t = u["N"] // P * u["w"]
                        act.activation(pt_buf[:, i % 2, 0:n_t], PS[:, T_BANK[i % 2], 0:n_t], ACT.Copy).then_inc(at_pt, 1)

            def split_mixed(st):
                for t in range(TILES):
                    act.wait_ge(*mixed_done(st))
                    act.activation(XT[0][:, :, tok(t)], OT[:, :, tok(t)], ACT.Copy).then_inc(ot_hi, 1)

            for st in stages:
                if st["kind"] not in ("ab", "mla"):
                    load_gains(st)
                ahead = None
                if st["kind"] == "ffn":
                    b0 = st["n"] * 2 * FB
                    pa, pb = st["passes"][0], st["passes"][1]
                    for fh in range(2):
                        if fh > 0:
                            hi_gu(fh * FB + b0)
                        for j in range(FB):
                            hi_chunk(pa, j, fh * 2 + pa["uses"][j])
                            silu(fh * FB + b0 + j)
                            if j < FB - 1:
                                hi_gu(fh * FB + b0 + j + 1)
                        for c in range(FB):
                            hi_chunk(pb, c, fh * 2 + pb["uses"][c])
                elif st["kind"] == "ple":
                    hi_chunks(st["passes"][1], 0, KD)
                    p0, p1 = st["passes"][2:4]
                    for c in range(KD):
                        hi_chunk(p0, c, p0["uses"][c])

                    def sigmoid(q, t, p):
                        act.wait_ge(y_mm, summed(p["i"], t))
                        if q * TILES + t >= 2:
                            act.wait_ge(y_out, evicted(p["i"], t) - 2)
                        act.activation(GT[:, (q * TILES + t) % 2, :], PS[:, Y_BANK[t], :], ACT.Sigmoid
                                       ).then_inc(ple["gate"], 1)

                    hi_chunks(p1, 0, HEAD)
                    for t in range(TILES):
                        sigmoid(0, t, p0)
                    hi_chunks(p1, HEAD, KD)
                    ahead = lambda t: sigmoid(1, t, p1)
                elif st["kind"] == "ab":
                    ps = st["passes"]
                    staged = 0
                    hi_chunks(ps[0], 0, KD)
                    for q in range(6):
                        hi_chunks(ps[q + 1], 0, HEAD)
                        for t in range(TILES):
                            act.wait_ge(y_mm, summed(ps[q]["i"], t))
                            if q in (1, 4):
                                act.wait_ge(st_tr, TILES * (staged - 1) + t + 1)
                            if q == 3:
                                act.wait_ge(st_tr, TILES * 2)
                                act.wait_ge(st_out["sb_k"], 2 * 16)
                            name = ("sb_q", "sb_k", "sb_v", "df_q", "df_k", "df_v")[q]
                            dst = QKV[name] if name[3] == "v" else rows_in
                            act.activation(dst[:, t, :], PS[:, Y_BANK[t], :], ACT.Copy,
                                           scale=HD ** -0.5 if name[3] == "q" else 1.0).then_inc(y_out, 1)
                        staged += q in (0, 1, 3, 4)
                        hi_chunks(ps[q + 1], HEAD, KD)
                    act.wait_ge(lam_step, 2)
                    act.activation(lam_cols[:, 2:4], lam_cols[:, 0:2], ACT.Exp).then_inc(lam_step, 1)
                    stick_act(stick[st["stick0"]:st["stick1"]])
                    soft_act(soft[st["soft0"]:st["soft1"]])
                    act.wait_ge(o_out, groups_end(st))
                    for h in range(DF_HEADS):
                        act.activation(sub_sq_buf[:, h, :], OT[:, 4 + h, :], ACT.Square).then_inc(sub_sq, 1)
                    for h in range(DF_HEADS + 1):
                        act.wait_ge(sub_mm, h + 1)
                        dst, src = sub_part(sub_rs_buf, h)
                        act.activation(dst, src, ACT.Ln, scale=-1.0 / (2 * HD), bias=eps_col[:]).then_inc(sub_ln, 1)
                    act.wait_ge(sub_ln, DF_HEADS + 1)
                    for h in range(DF_HEADS):
                        act.activation(sub_rs_buf[:, h, :], sub_rs_buf[:, h, :], ACT.Exp, scale=-0.5).then_inc(sub_rs, 1)
                    split_mixed(st)
                    hi_chunks(ps[7], 0, KD)
                    load_gains(st)
                elif st["kind"] == "mla":
                    ps = st["passes"]
                    hi_chunks(ps[0], 0, KD)
                    for q, (a, b, s0, s1) in enumerate(((0, HALF, 0, Q_LORA), (HALF, MLA_IN, Q_LORA, Q_LORA + KV_LORA))):
                        hi_chunks(ps[q + 1], 0, HEAD)
                        for t in range(TILES):
                            act.wait_ge(y_mm, summed(ps[q]["i"], t))
                            act.activation(c_in[:, t, a:b], PS[:, Y_BANK[t], 0:b - a], ACT.Copy).then_inc(y_out, 1)
                            act.wait_ge(y_out, evicted(ps[q]["i"], t))
                            if t > 0:
                                act.wait_ge(mc_ss, q * TILES + t)
                            act.activation(sq_tmp[:, q, 0:s1 - s0], c_in[:, t, s0:s1], ACT.Square,
                                           scale=(s1 - s0) ** -0.5, accum_out=mc[:, 0, t, q:q + 1]).then_inc(mc_ss, 1)
                        hi_chunks(ps[q + 1], HEAD, KD)
                    for t in range(TILES):
                        act.wait_ge(mc_tr, t + 1)
                        act.activation(CQT[0][:, :, tok(t)], PS[:, TR_BANK[t][0], 0:Q_LORA], ACT.Copy).then_inc(mc_hi, 1)
                    for name in ("lat", "kr"):
                        act.wait_ge(st_out[name], 2 * 16)
                    act.wait_ge(new_cp, 1)
                    for n in range(2 * PT):
                        act.wait_ge(v_mm, n + 1)
                        act.activation(V[:, n // 2, (n % 2) * HALF:(n % 2 + 1) * HALF], PS[:, S_BANK[n % 2], :], ACT.Copy
                                       ).then_inc(v_ok, 1)
                    def copy_q(g, t):
                        act.wait_ge(mq_tr, g * TILES + t + 1)
                        act.activation(q_t[0:QD, 4 * g:4 * g + 4, tok(t)],
                                       PS[0:QD, T_BANK[(g * TILES + t) % 2], :].rearrange("p (h n) -> p h n", h=4),
                                       ACT.Copy).then_inc(mq_cp, 1)
                        if t == PT:
                            for j in range(4):
                                act.activation(qr_t[0:ROPE, :, 4 * g + j, :], PS[0:ROPE, 3, j * P:(j + 1) * P].rearrange(
                                    "p (b t) -> p b t", b=DEC_B), ACT.Copy).then_inc(qr_cp, 1)

                    for g in range(4):
                        p = ps[2 + g]
                        if g > 0:
                            for t in range(TILES):
                                copy_q(g - 1, t)
                        hi_chunks(ps[3 + g], 0, 2)
                        for t in range(TILES):
                            act.wait_ge(y_mm, summed(p["i"], t))
                            if g > 0:
                                act.wait_ge(mq_tr, (g - 1) * TILES + t + 1)
                            act.activation(q_rows[:, t, :], PS[:, Y_BANK[t], 0:4 * QD], ACT.Copy, scale=QD ** -0.5
                                           ).then_inc(y_out, 1)
                        hi_chunks(ps[3 + g], 2, KD)
                    for t in range(TILES):
                        copy_q(3, t)
                    for h in range(MLA_HEADS):
                        act.wait_ge(wt_tr, h + 1)
                        if h >= 2:
                            act.wait_ge(ql_mm, h - 1)
                        act.activation(w_ukt[0:NOPE, h % 2, :], PS[0:NOPE, T_BANK[h % 2], 0:2 * P], ACT.Copy).then_inc(wt_cp, 1)
                    soft_act(soft[st["soft0"]:st["soft1"]])
                    split_mixed(st)
                    hi_chunks(ps[7], 0, KD)
                    load_gains(st)
                if st["k"] > 0:
                    first_gu(st)
                if st["to_ple"]:
                    for b in range(3):
                        act.wait_ge(ple["tr"], 3 * st["next"]["n"] + b + 1)
                        act.activation(*ple_evict(b, 0), ACT.Copy).then_inc(ple["hi"], 1)
                    hi_chunks(st["next"]["passes"][0], 0, KD)
                tail(st, ahead)

        @block.gpsimd
        def _(pool):
            pool.memset(ident[:], 0.0).then_inc(const_ok, 1)
            pool.memset(minus_half[:], -0.5).then_inc(const_ok, 1)
            pool.memset(one[:], 1.0).then_inc(const_ok, 1)
            pool.memset(eps_col[:], EPS).then_inc(const_ok, 1)
            pool.wait_ge(const_ok, 4)
            pool.affine_select(out=ident[:], in_=ident[:], compare_op=ALU.not_equal, fill=1.0, base=0,
                               pattern=[[-1, P]], channel_multiplier=1).then_inc(const_ok, 1)

            pool.dma_start(exact_raw[0:DEC_B, :], io["consts"][0:DEC_B, m_first:m_first + 3 * P]).then_inc(exact_in, 16)

            def lo_gu(blk):
                for s in range(GU_PIECES):
                    pool.wait_ge(gu_hi_ok, blk * GU_PIECES + s + 1)
                    pool.tensor_tensor(gu_lo[:, s], gu_raw[:, s], gu_hi[:, s].bitcast(F32), ALU.subtract
                                       ).then_inc(gu_lo_ok, 1)

            def lo_chunk(p, i, c):
                pool.wait_ge(ch_hi_ok, i * CH + c + 1)
                pool.tensor_tensor(ch_lo[:, c, 0:p["n"]], ch_raw[:, c, 0:p["n"]], ch_hi[:, c, 0:p["n"]].bitcast(F32),
                                   ALU.subtract).then_inc(ch_lo_ok, counts(p, c))

            def tail(st):
                k = st["k"]
                if st["early"] and k > 0:
                    lo_gu(st["next"]["n"] * 2 * FB)

                def root(t, which, ss, n, eps, eps_n, done):
                    pool.wait_ge(ss, n)
                    pool.tensor_scalar(rs[:, t, which:which + 1], ssq[:, t, 2 * which:2 * which + 1],
                                       ssq[:, t, 2 * which + 1:2 * which + 2], eps, ALU.add, ALU.add).then_inc(eps_ok, 1)
                    pool.wait_ge(eps_ok, eps_n)
                    pool.tensor_tensor(rs[:, t, which:which + 1], rs[:, t, which:which + 1], minus_half[:], ALU.pow
                                       ).then_inc(done, 1)

                n = roots[0]
                for t in range(TILES):
                    if k > 0:
                        roots[0] += 1
                        root(t, 0, ss1_ok, 2 * (TILES * (k - 1) + t) + 2, EPS / st["c"] ** 2, roots[0], rs1_ok)
                    if st["pre"] is not None:
                        roots[0] += 1
                        root(t, 1, ss2_ok, 2 * (TILES * k + t) + 2, EPS, roots[0], rs2_ok)
                    if st["early"] and k == 0 and t == 2:
                        lo_gu(st["next"]["n"] * 2 * FB)

            roots = [0]
            for st in stages:
                if st["kind"] == "ffn":
                    pa, pb = st["passes"][0], st["passes"][1]
                    b0 = st["n"] * 2 * FB
                    for fh in range(2):
                        if fh > 0:
                            lo_gu(fh * FB + b0)
                        for j in range(FB):
                            lo_chunk(pa, fh * 2 + pa["i"], j)
                            if j < FB - 1:
                                lo_gu(fh * FB + b0 + j + 1)
                        if fh == 1 and st["to_ple"]:
                            nxt = st["next"]
                            pool.wait_ge(up_mm, 2 + 2 * (b0 + 2 * FB))
                            pool.dma_start(p_raw[:, 0:PT, :], io["p_prompt"][nxt["layer"]]).then_inc(ple["in"], 16)
                            pool.dma_start(p_raw[:, PT, :], io["p_sample"][nxt["layer"]]).then_inc(ple["in"], 16)
                        for c in range(FB):
                            lo_chunk(pb, fh * 2 + pb["i"], c)
                    if st["to_ple"]:
                        p = st["next"]["passes"][0]
                        for c in range(p["K"]):
                            lo_chunk(p, p["i"], c)
                elif st["kind"] == "ple":
                    for p in st["passes"][1:]:
                        for c in range(p["K"]):
                            lo_chunk(p, p["i"], c)
                elif st["kind"] == "ab":
                    for q, p in enumerate(st["passes"]):
                        if q == 0:
                            pool.dma_start(lam_rows[:], io["df_lambda"][0].rearrange("a d -> (a d)").partition_broadcast(P)
                                           .rearrange("p (a d) -> p a d", a=4)).then_inc(lam_in, 16)
                            pool.dma_start(lam_cols[:, 6:7], io["df_subln"][0].rearrange("(e a) -> e a", a=1)
                                           ).then_inc(lam_in, 16)
                        for c in range(p["K"]):
                            lo_chunk(p, p["i"], c)
                        if q == 6:
                            pool.wait_ge(st_out["df_k"], 2 * 16)
                            pool.wait_ge(st_cp, 4 * TILES)
                            for name in qbd:
                                pool.memset(qbd[name][:], 0.0).then_inc(qbd_ok, 1)
                            pool.wait_ge(qbd_ok, 2)
                            for name in qbd:
                                for c in range(2):
                                    r = slice(HD * c, HD * c + HD)
                                    pool.tensor_copy(qbd[name][r, :, :, c, :], QKV[name][r, :, PROMPT:TOK].rearrange(
                                        "p h (b t) -> p h b t", b=DEC_B)).then_inc(qbd_ok, 1)
                elif st["kind"] == "mla":
                    ps = st["passes"]
                    for p in ps[0:2]:
                        for c in range(p["K"]):
                            lo_chunk(p, p["i"], c)
                    for q in range(2):
                        for t in range(TILES):
                            n = q * TILES + t
                            pool.wait_ge(mc_ss, n + 1)
                            pool.tensor_scalar(mc[:, 1, t, q:q + 1], mc[:, 0, t, q:q + 1], EPS, None, ALU.add
                                               ).then_inc(mc_eps, 1)
                            pool.wait_ge(mc_eps, n + 1)
                            pool.tensor_tensor(mc[:, 1, t, q:q + 1], mc[:, 1, t, q:q + 1], minus_half[:], ALU.pow
                                               ).then_inc(mc_rs, 1)
                    for p in ps[2:]:
                        for c in range(p["K"]):
                            lo_chunk(p, p["i"], c)
                tail(st)

        @block.vector
        def _(dve):
            for free, n in ((sg_free, 2), (y_out, TILES), (silu_ok, 2), (h_mul, 2), (gate_mm, 2), (up_mm, 2),
                            (gu_used, 2), (ch_used, CH - 1), (y_mm, TILES)):
                dve.sem_inc(free, n)

            def gated(blk):
                for b, bank, cols in ((0, UP_A, slice(0, GA)), (1, UP_B, slice(GA, TOK))):
                    dve.wait_ge(silu_ok, blk * 2 + b + 3)
                    dve.wait_ge(up_mm, blk * 2 + b + 3)
                    dve.tensor_tensor(SG[:, cols], SG[:, cols], PS[:, bank, 0:cols.stop - cols.start], ALU.mult
                                      ).then_inc(h_mul, 1)

            def split_h(blk, slot):
                for b, cols in ((0, slice(0, GA)), (1, slice(GA, TOK))):
                    dve.wait_ge(h_mul, blk * 2 + b + 3)
                    dve.tensor_copy(HT[0][:, bass.ds(slot, 1), cols].rearrange("p a n -> p (a n)"), SG[:, cols]
                                    ).then_inc(h_hi_ok, 1)
                    dve.wait_ge(h_hi_ok, blk * 2 + b + 1)
                    dve.tensor_tensor(HT[1][:, bass.ds(slot, 1), cols].rearrange("p a n -> p (a n)"), SG[:, cols],
                                      HT[0][:, bass.ds(slot, 1), cols].rearrange("p a n -> p (a n)").bitcast(F32),
                                      ALU.subtract).then_inc(sg_free, 1)

            def out_rows(i, t, half):
                dve.wait_ge(y_mm, summed(i, t))
                dve.tensor_copy(Y[:, t, half * HALF:(half + 1) * HALF], PS[:, Y_BANK[t], :]).then_inc(y_out, 1)

            def add_y(i, t, half):
                dve.wait_ge(y_mm, summed(i, t))
                dve.wait_ge(y_out, evicted(i, t) - 1)
                yt = Y[:, t, half * HALF:(half + 1) * HALF]
                dve.tensor_tensor(yt, yt, PS[:, Y_BANK[t], :], ALU.add).then_inc(y_out, 1)

            def tail(st, take):
                k = st["k"]

                def post(t):
                    n = TILES * (k - 1) + t
                    dve.wait_ge(rs1_ok, n + 1)
                    for h in range(2):
                        cols = slice(h * HALF, (h + 1) * HALF)
                        dve.scalar_tensor_tensor(Y[:, t, cols], Y[:, t, cols], rs[:, t, 0:1], g_post[:, cols],
                                                 ALU.mult, ALU.mult).then_inc(post_ok, 1)
                        dve.wait_ge(post_ok, 2 * n + h + 1)
                        dve.tensor_tensor(X[:, t, cols], X[:, t, cols], Y[:, t, cols], ALU.add).then_inc(x_ok, 1)

                def xn(t):
                    if k > 0:
                        dve.wait_ge(x_ok, 2 * (TILES * (k - 1) + t) + 2)
                    dve.wait_ge(rs2_ok, TILES * k + t + 1)
                    for h in range(2):
                        cols = slice(h * HALF, (h + 1) * HALF)
                        dve.scalar_tensor_tensor(Y[:, t, cols], X[:, t, cols], rs[:, t, 1:2], g_pre[:, cols],
                                                 ALU.mult, ALU.mult).then_inc(xn_ok, 1)

                def lo(t):
                    for b in range(2):
                        dve.wait_ge(xt_hi_ok, 2 * (TILES * k + t) + b + 1)
                        dve.tensor_tensor(XT[1][:, 4 * b:4 * b + 4, tok(t)], PS[:, st["tr_bank"][t][b], :],
                                          XT[0][:, 4 * b:4 * b + 4, tok(t)].bitcast(F32), ALU.subtract
                                          ).then_inc(xt_lo_ok, 1)

                gains[0] += 16 * ((k > 0) + (st["pre"] is not None))
                dve.wait_ge(gains_in, gains[0])
                for t in range(TILES):
                    if st["pre"] is not None and t == TILES - 1:
                        lo(0)
                        lo(1)
                    if k > 0:
                        take(t)
                    if st["pre"] is not None and t > 0:
                        xn(t - 1)
                    if st["pre"] is not None and t == TILES - 1:
                        lo(2)
                    if k > 0:
                        post(t)
                if st["pre"] is not None:
                    xn(4)
                    lo(3)
                    lo(4)

            def rotate(x1, x2, cos, sin, n):
                G, half = x1.shape[1], x1.shape[2]
                tmp = [rope_tmp[:, j, 0:G * half].rearrange("p (g d) -> p g d", g=G) for j in range(4)]
                cs, sn = (a.unsqueeze(1).to_broadcast([P, G, half]) for a in (cos, sin))
                if n:
                    dve.wait_ge(rope_ok, 2 * n)
                for j, (x, f) in enumerate(((x1, cs), (x2, sn), (x2, cs), (x1, sn))):
                    dve.tensor_tensor(tmp[j], x, f, ALU.mult).then_inc(rope_part, 1)
                dve.wait_ge(rope_part, 4 * n + 4)
                dve.tensor_tensor(x1, tmp[0], tmp[1], ALU.subtract).then_inc(rope_ok, 1)
                dve.tensor_tensor(x2, tmp[2], tmp[3], ALU.add).then_inc(rope_ok, 1)

            def evict_group(u):
                g = u["g"]
                dst = g["dst"]
                src = PS[:, O_BANK[g["i"] % 2], 0:HALF]
                if len(dst.shape) == 3:
                    src = src.rearrange("p (a n) -> p a n", a=dst.shape[1])
                dve.tensor_copy(dst, src).then_inc(o_out, 1)

            def stick_dve(units):
                L = len(units)

                def masked(x, u):
                    cols, b, kind = u["mask"]
                    if kind == "diag":
                        return x[:, cols], const("diag")
                    m = const("batch_tri")[:, b * DEC_T:(b + 1) * DEC_T]
                    return (x[:, cols].rearrange("p (h t) -> p h t", h=SB_HEADS),
                            m.unsqueeze(1).to_broadcast([P, SB_HEADS, DEC_T]))

                def clamped(u):
                    i = u["i"]
                    dve.wait_ge(sb_z, i + 1)
                    if i >= 4:
                        dve.wait_ge(sb_sp, i - 3)
                    dve.tensor_scalar(e_buf[:, i % 4, 0:u["N"]], PS[:, u["bank"], 0:u["N"]], Z_MOST, None, ALU.min
                                      ).then_inc(sb_min, 1)

                clamped(units[0])
                for n in range(L + 4):
                    if n + 1 < L:
                        clamped(units[n + 1])
                    if 1 <= n <= L:
                        u = units[n - 1]
                        i = u["i"]
                        dve.wait_ge(sb_ln, i + 1)
                        if i >= 4:
                            dve.wait_ge(sb_acc, i - 3 if u["prep"] is None else i - 1)
                        dve.tensor_tensor(u["sp"], PS[:, u["bank"], 0:u["N"]], e_buf[:, i % 4, 0:u["N"]], ALU.max
                                          ).then_inc(sb_sp, 1)
                        dve.wait_ge(sb_sp, i + 1)
                        x, m = masked(u["sp"], u)
                        dve.tensor_tensor(x, x, m, ALU.mult).then_inc(sb_spm, 1)
                    if 3 <= n <= L + 2:
                        u = units[n - 3]
                        i = u["i"]
                        dve.wait_ge(sb_w, i + 1)
                        x, m = masked(w_buf[:, i % 2, 0:u["N"]], u)
                        dve.scalar_tensor_tensor(x, x, 2.0, m, ALU.min, ALU.mult).then_inc(sb_wm, 1)
                    if n >= 4 and units[n - 4]["last"]:
                        dve.wait_ge(sb_pv, units[n - 4]["i"] + 1)
                        evict_group(units[n - 4])

            def soft_dve(units):
                L = len(units)
                for n in range(L + 3):
                    if 1 <= n <= L:
                        u = units[n - 1]
                        i = u["i"]
                        dve.wait_ge(at_exp, i + 1)
                        dve.reciprocal(at_cols[:, i % 4, 2:3], at_cols[:, i % 4, 1:2]).then_inc(at_r, 1)
                        dve.wait_ge(at_r, i + 1)
                        pr = p_buf[:, i % 2, 0:u["N"]]
                        if u["coef"]:
                            col = lam_cols[:, 4:5] if u["coef"] == "neg_lam" else lam_cols[:, 5:6]
                            dve.tensor_scalar(pr, pr, at_cols[:, i % 4, 2:3], col, ALU.mult, ALU.mult).then_inc(at_p, 1)
                        else:
                            dve.tensor_scalar(pr, pr, at_cols[:, i % 4, 2:3], None, ALU.mult).then_inc(at_p, 1)
                    if n < L:
                        u = units[n]
                        i = u["i"]
                        dve.wait_ge(at_s, i + 1)
                        dve.tensor_reduce(at_cols[:, i % 4, 0:1], PS[:, S_BANK[i % 2], 0:u["N"]], AX_X, ALU.max,
                                          negate=True).then_inc(at_max, 1)
                    if n >= 3 and units[n - 3]["last"]:
                        dve.wait_ge(at_pv, units[n - 3]["i"] + 1)
                        evict_group(units[n - 3])

            def split_mixed(st, before):
                for t in range(TILES):
                    dve.wait_ge(ot_hi, before + t + 1)
                    dve.tensor_tensor(XT[1][:, :, tok(t)], OT[:, :, tok(t)], XT[0][:, :, tok(t)].bitcast(F32),
                                      ALU.subtract).then_inc(ot_lo, 1)

            gains = [0]
            for st in stages:
                take = None

                if st["k"] == 1:
                    dve.wait_ge(const_ok, 5)
                    dve.tensor_copy(exact_id[0:DEC_B, :], ident[0:DEC_B, 0:DEC_B]).then_inc(exact_ok, 1)
                    dve.wait_ge(exact_in, 16)
                    dve.tensor_copy(exact_r[0:DEC_B, :], exact_raw[0:DEC_B, :]).then_inc(exact_ok, 1)
                    dve.wait_ge(exact_ok, 2)

                if st["kind"] == "ffn":
                    b0 = st["n"] * 2 * FB
                    i0 = st["passes"][0]["i"]
                    for fh in range(2):
                        with dve.Fori(0, FB) as fb:
                            gated(fb + (b0 + fh * FB))
                            split_h(fb + (b0 + fh * FB), fb)
                        for nh in range(2 - fh):
                            for t in range(TILES):
                                (out_rows if fh == 0 else add_y)(i0 + 2 * fh + nh, t, nh)
                    take = lambda t, i=i0 + 3: add_y(i, t, 1)
                    if st["to_ple"]:
                        for b in range(3):
                            dve.wait_ge(ple["hi"], 3 * st["next"]["n"] + b + 1)
                            dst, src = ple_evict(b, 1)
                            hi_part, _ = ple_evict(b, 0)
                            dve.tensor_tensor(dst, src, hi_part.bitcast(F32), ALU.subtract).then_inc(ple["lo"], 1)
                elif st["kind"] == "ple":
                    for q in range(2):
                        for t in range(TILES):
                            out_rows(st["passes"][q]["i"], t, q)

                    def times_gate(q, t, st=st):
                        p = st["passes"][2 + q]["i"]
                        dve.wait_ge(ple["gate"], 2 * TILES * st["n"] + q * TILES + t + 1)
                        dve.wait_ge(y_out, evicted(p, t) - 1)
                        yt = Y[:, t, q * HALF:(q + 1) * HALF]
                        dve.tensor_tensor(yt, yt, GT[:, (q * TILES + t) % 2, :], ALU.mult).then_inc(y_out, 1)

                    for t in range(TILES):
                        times_gate(0, t)
                    take = lambda t: times_gate(1, t)
                elif st["kind"] == "ab":
                    ps = st["passes"]
                    names = ["sb_q", "sb_k", "df_q", "df_k"]

                    def copy_staged(sgd, t):
                        dve.wait_ge(st_tr, TILES * sgd + t + 1)
                        dve.tensor_copy(QKV[names[sgd]][:, :, tok(t)],
                                        PS[:, T_BANK[(TILES * sgd + t) % 2], :].rearrange("p (a n) -> p a n", a=4)).then_inc(st_cp, 1)

                    dve.wait_ge(consts_in, 16)
                    for t in range(TILES):
                        copy_staged(0, t)
                    for t in range(TILES):
                        copy_staged(1, t)
                    for sgd in (2, 3):
                        for t in range(TILES):
                            dve.wait_ge(y_out, evicted(ps[sgd + 1]["i"], t))
                            g = rows_in[:, t, :].rearrange("p (g d) -> p g d", d=HD)
                            h = DF_ROT // 2
                            rotate(g[:, :, 0:h], g[:, :, h:2 * h], const("cos_d")[:, t * h:(t + 1) * h],
                                   const("sin_d")[:, t * h:(t + 1) * h], TILES * (sgd - 2) + t)
                        for t in range(TILES):
                            copy_staged(sgd, t)
                    lam_init = 0.8 - 0.6 * math.exp(-0.3 * st["layer"])
                    dve.wait_ge(lam_in, 32)
                    dve.tensor_tensor(lam_rows[:, 0:3:2, :], lam_rows[:, 0:3:2, :], lam_rows[:, 1:4:2, :], ALU.mult
                                      ).then_inc(lam_step, 1)
                    dve.wait_ge(lam_step, 1)
                    dve.tensor_reduce(lam_cols[:, 0:2], lam_rows[:, 0:3:2, :], AX_X, ALU.add).then_inc(lam_step, 1)
                    dve.wait_ge(lam_step, 3)
                    dve.tensor_scalar(lam_cols[:, 4:5], lam_cols[:, 3:4], lam_cols[:, 2:3], -lam_init,
                                      ALU.subtract, ALU.add).then_inc(lam_step, 1)
                    dve.wait_ge(lam_step, 4)
                    dve.tensor_scalar(lam_cols[:, 5:6], lam_cols[:, 4:5], const("comp1"), const("comp0"),
                                      ALU.mult, ALU.add).then_inc(lam_step, 1)
                    dve.tensor_scalar(lam_cols[:, 6:7], lam_cols[:, 6:7], 1.0 - lam_init, None, ALU.mult
                                      ).then_inc(lam_step, 1)
                    stick_dve(stick[st["stick0"]:st["stick1"]])
                    dve.wait_ge(lam_step, 6)
                    soft_dve(soft[st["soft0"]:st["soft1"]])
                    for h in range(DF_HEADS):
                        dve.wait_ge(sub_rs, h + 1)
                        dve.scalar_tensor_tensor(OT[:, 4 + h, :], OT[:, 4 + h, :], lam_cols[:, 6:7],
                                                 sub_rs_buf[:, h, :], ALU.mult, ALU.mult).then_inc(sub_ok, 1)
                    split_mixed(st, st["before"] * TILES)
                    for t in range(TILES):
                        out_rows(ps[6]["i"], t, 0)
                    take = lambda t, i=ps[7]["i"]: out_rows(i, t, 1)
                elif st["kind"] == "mla":
                    ps = st["passes"]
                    dve.wait_ge(mg_in, 3 * 16)
                    for q, (a, b, g) in enumerate(((0, Q_LORA, mg_q), (Q_LORA, Q_LORA + KV_LORA, mg_kv))):
                        for t in range(TILES):
                            dve.wait_ge(mc_rs, q * TILES + t + 1)
                            dve.scalar_tensor_tensor(c_in[:, t, a:b], c_in[:, t, a:b], mc[:, 1, t, q:q + 1], g[:],
                                                     ALU.mult, ALU.mult).then_inc(mc_n, 1)
                            if q == 1:
                                x = c_in[:, t, b:MLA_IN].unsqueeze(1)
                                h = ROPE // 2
                                rotate(x[:, :, 0:h], x[:, :, h:2 * h], mconst("cos_m")[:, t * h:(t + 1) * h],
                                       mconst("sin_m")[:, t * h:(t + 1) * h], st["rot0"] + t)
                    dve.wait_ge(mc_n, 2 * TILES)
                    dve.tensor_copy(lat_new[:], c_in[:, PT, Q_LORA:Q_LORA + KV_LORA]).then_inc(new_cp, 1)
                    for t in range(TILES):
                        dve.wait_ge(mc_tr, t + 1)
                        bank = TR_BANK[t][1]
                        dve.tensor_copy(lat_t[:, :, tok(t)], PS[:, bank, 0:2 * P].rearrange("p (k n) -> p k n", k=2)
                                        ).then_inc(mc_lat, 1)
                        dve.tensor_copy(kr_t[NOPE:QD, tok(t)], PS[NOPE:QD, bank, 2 * P:3 * P]).then_inc(mc_lat, 1)
                        if t == PT:
                            dve.tensor_copy(kr_t[0:ROPE, tok(t)], PS[0:ROPE, bank, 3 * P:4 * P]).then_inc(mc_lat, 1)
                        dve.wait_ge(mc_hi, t + 1)
                        dve.tensor_tensor(CQT[1][:, :, tok(t)], PS[:, TR_BANK[t][0], 0:Q_LORA].rearrange(
                            "p (k n) -> p k n", k=3), CQT[0][:, :, tok(t)].bitcast(F32), ALU.subtract).then_inc(mc_lo, 1)
                    dve.wait_ge(mc_lat, 2 * TILES)
                    for par in range(2):
                        dve.tensor_copy(k_t[NOPE:QD, par, :], kr_t[NOPE:QD, 0:PROMPT]).then_inc(krt_cp, 1)

                    for g in range(4):
                        for t in range(TILES):
                            dve.wait_ge(y_out, evicted(ps[2 + g]["i"], t))
                            x = q_rows[:, t, :].rearrange("p (h d) -> p h d", h=4)
                            h = ROPE // 2
                            rotate(x[:, :, NOPE:NOPE + h], x[:, :, NOPE + h:QD], mconst("cos_m")[:, t * h:(t + 1) * h],
                                   mconst("sin_m")[:, t * h:(t + 1) * h], st["rot0"] + (g + 1) * TILES + t)
                    for h in range(MLA_HEADS):
                        dve.wait_ge(ql_mm, h + 1)
                        for c in range(2):
                            dve.tensor_copy(q_lat_t[:, c, :, h, :], PS[:, S_BANK[h % 2], c * P:(c + 1) * P].rearrange(
                                "p (b t) -> p b t", b=DEC_B)).then_inc(ql_cp, 1)
                    soft_dve(soft[st["soft0"]:st["soft1"]])
                    for b in range(2):
                        dve.wait_ge(uo_mm, b + 1)
                        dve.tensor_copy(OT[:, 4 * b:4 * b + 4, PROMPT:TOK], PS[:, S_BANK[b], :].rearrange(
                            "p (a n) -> p a n", a=4)).then_inc(uo_ok, 1)
                    split_mixed(st, st["before"] * TILES)
                    for t in range(TILES):
                        out_rows(ps[6]["i"], t, 0)
                    take = lambda t, i=ps[7]["i"]: out_rows(i, t, 1)
                tail(st, take)

        @block.tensor
        def _(pe):
            def product(out, a, b, start, stop):
                pe.matmul(out, a[0], b[0], start=start, stop=False)
                pe.matmul(out, a[0], b[1], start=False, stop=False)
                return pe.matmul(out, a[1], b[0], start=False, stop=stop)

            def gate_up(blk, lo_ready, banks_free, between=None):
                halves = [(0, 0), (0, 1), (1, 0), (1, 1)]
                for q, b in sorted(halves, key=lambda qb: qb[1]) if between else halves:
                    banks, done = (((GATE_A, GATE_B), gate_mm), ((UP_A, UP_B), up_mm))[q]
                    if b == 0:
                        pe.wait_ge((silu_ok, h_mul)[q], blk * 2 + 2)
                        pe.wait_ge(y_out, banks_free)
                    elif between and q == 0:
                        between()
                    for cols in ((slice(0, GA), slice(GA, TOK))[b],):
                        pe.wait_ge(xt_lo_ok, lo_ready + 2 * (TILES if b else GA // P))
                        for k in range(KD):
                            s, kk = 2 * q + k // 4, k % 4
                            if b == 0 and kk == 0:
                                pe.wait_ge(gu_lo_ok, blk * GU_PIECES + s + 1)
                            mm = product(PS[:, banks[b], 0:cols.stop - cols.start], (gu_hi[:, s, kk, :], gu_lo[:, s, kk, :]),
                                         (XT[0][:, k, cols], XT[1][:, k, cols]), k == 0, k == KD - 1)
                            if b == 1 and k == 3:
                                mm.then_inc(gu_used, 1)
                        mm.then_inc(done, 1)

            def column_pass(p, i, src, head, before=None):
                K, n = p["K"], p["n"]
                order = [(c, t) for c in range(head) for t in range(TILES)]
                order += [(c, t) for t in range(TILES) for c in range(head, K)]
                for c, t in order:
                    if t == 0:
                        pe.wait_ge(ch_lo_ok, i * CH + c + 1)
                    if c == 0:
                        pe.wait_ge(y_out, i * TILES + t + 1)
                    if before:
                        before(t, c)
                    mm = product(PS[:, Y_BANK[t], 0:n], (src[0][:, c, tok(t)], src[1][:, c, tok(t)]),
                                 (ch_hi[:, c, 0:n], ch_lo[:, c, 0:n]), c == 0, c == K - 1)
                    if c == K - 1:
                        mm.then_inc(y_mm, 1)
                    elif t == TILES - 1:
                        mm.then_inc(ch_used, counts(p, c, CH - 1))

            def transpose_keys(pr):
                i, par, kind = pr["i"], pr["i"] % 2, pr["kind"]
                if kind in ("stick", "soft"):
                    pe.wait_ge(kraw_in[par], 16 * (i // 2 + 1))
                elif kind == "latent":
                    pe.wait_ge(lat_in[pr["b"] % 3], 32 * (pr["b"] // 3 + 1))
                for b in range(2):
                    if i >= 1:
                        pe.wait_ge(kt_ok, 2 * (i - 1) + b + 1)
                    if kind == "head":
                        for c in range(2):
                            mm = pe.matmul(PS[0:NOPE, prep_bank(pr, b), 0:256], W_uk[:, c, pr["h"] * NOPE:(pr["h"] + 1) * NOPE],
                                           lat_t[:, c, b * 256:(b + 1) * 256], start=c == 0, stop=c == 1)
                    elif kind == "latent" and b == 0:
                        for j in range(4):
                            mm = pe.transpose(PS[:, prep_bank(pr, 0), j * P:(j + 1) * P],
                                              lat_raw[:, pr["b"] % 3, j % 2, (j // 2) * P:(j // 2 + 1) * P], ident[:])
                    elif kind == "latent":
                        for j in range(2):
                            mm = pe.transpose(PS[0:ROPE, prep_bank(pr, 1), j * P:(j + 1) * P], kr_raw[:, pr["b"] % 3, j, :],
                                              ident[:])
                    else:
                        for j in range(4):
                            fb, kb = 2 * b + j // 2, j % 2
                            mm = pe.transpose(PS[:, prep_bank(pr, b), j * P:(j + 1) * P],
                                              k_raw[:, par, kb, fb * P:(fb + 1) * P], ident[:])
                    mm.then_inc(kt_tr, 1)

            def bank_of(u):
                g = u["g"]
                if u["first"] and g["i"] >= 2:
                    pe.wait_ge(o_out, g["i"] - 1)
                return PS[:, O_BANK[g["i"] % 2], :]

            def stick_pe(units):
                L = len(units)

                def scores(u):
                    i = u["i"]
                    if u["prep"]:
                        pe.wait_ge(kt_ok, 2 * u["prep"]["i"] + 2)
                        pe.wait_ge(qbd_ok, 6)
                    if u["bank_before"] is not None:
                        pe.wait_ge(sb_w, u["bank_before"] + 1)
                    for j, (cols, key, q) in enumerate(u["z"]):
                        mm = pe.matmul(PS[:, u["bank"], cols], key, q, start=j == 0, stop=True, skip_group_check=True)
                    mm.then_inc(sb_z, 1)

                scores(units[0])
                scores(units[1])
                for n in range(L + 3):
                    if n + 3 < L and units[n + 3]["prep"]:
                        transpose_keys(units[n + 3]["prep"])
                    if n + 2 < L:
                        scores(units[n + 2])
                    if n >= 3:
                        u = units[n - 3]
                        i = u["i"]
                        out = bank_of(u)
                        pe.wait_ge(sb_wm, i + 1)
                        if u["prep"]:
                            pe.wait_ge(vraw_in[u["prep"]["i"] % 2], 16 * (u["prep"]["i"] // 2 + 1))
                        for rows, cols, val, wc, start in u["pv"]:
                            mm = pe.matmul(out[rows, cols], val, w_buf[:, i % 2, wc], start=start, stop=True,
                                           skip_group_check=True)
                        mm.then_inc(sb_pv, 1)
                    if 1 <= n <= L:
                        u = units[n - 1]
                        i = u["i"]
                        bank = PS[:, u["bank"], :]
                        pe.wait_ge(sb_spm, i + 1)
                        mm = pe.matmul(bank[:, 0:u["N"]], const("neg_tri"), u["sp"], start=False, stop=True,
                                       skip_group_check=True)
                        for cols, sp_later in u["later"]:
                            mm = pe.matmul(bank[:, cols], const("neg_ones"), sp_later, start=False, stop=True,
                                           skip_group_check=True)
                        mm.then_inc(sb_acc, 1)

            def soft_pe(units):
                L = len(units)
                if units[0]["prep"]:
                    transpose_keys(units[0]["prep"])
                for n in range(L + 2):
                    if n < L:
                        u = units[n]
                        i = u["i"]
                        if u["prep"]:
                            pe.wait_ge(kt_ok, 2 * u["prep"]["i"] + 2)
                        if i >= 2:
                            pe.wait_ge(at_exp, i - 1)
                        for rows, cols, q, key, start in u["s"]:
                            mm = pe.matmul(PS[rows, S_BANK[i % 2], cols], q, key, start=start, stop=True,
                                           skip_group_check=True)
                        mm.then_inc(at_s, 1)
                    if n + 1 < L and units[n + 1]["prep"]:
                        transpose_keys(units[n + 1]["prep"])
                    if 1 <= n <= L:
                        u = units[n - 1]
                        i = u["i"]
                        pe.wait_ge(at_p, i + 1)
                        if i >= 2:
                            pe.wait_ge(at_pt, i - 1)
                        for j in range(u["N"] // P):
                            out, w = PS[:, T_BANK[i % 2], j * u["w"]:(j + 1) * u["w"]], p_buf[:, i % 2, j * P:(j + 1) * P]
                            if u["w"] == P:
                                mm = pe.transpose(out, w, ident[:])
                            else:
                                mm = pe.matmul(out, w, const("merge"), start=j == 0, stop=True, skip_group_check=True)
                        mm.then_inc(at_t, 1)
                    if n >= 2:
                        u = units[n - 2]
                        i = u["i"]
                        out = bank_of(u)
                        pe.wait_ge(at_pt, i + 1)
                        if u["prep"] and u["prep"]["kind"] == "soft":
                            pe.wait_ge(vraw_in[u["prep"]["i"] % 2], 16 * (u["prep"]["i"] // 2 + 1))
                        for rows, cols, val, (c0, w), start in u["pv"]:
                            mm = pe.matmul(out[rows, cols], val, pt_buf[:, i % 2, c0:c0 + w], start=start, stop=True,
                                           skip_group_check=True)
                        mm.then_inc(at_pv, 1)

            def rows_t(st, t):
                n = TILES * st["k"]
                if t == 3 and st["k"] > 0 and not st["to_ple"]:
                    pe.wait_ge(y_out, evicted(st["last"], TILES - 1))
                if t > 1:
                    pe.wait_ge(xt_lo_ok, 2 * (n + t - (0 if st["to_ple"] and t > 2 else 1)))
                if t == 0 and st["to_ple"]:
                    pe.wait_ge(ple["lo"], 3 * (st["next"]["n"] + 1))
                for b in range(2):
                    pe.wait_ge(xn_ok, 2 * (n + t) + b + 1)
                    for j in range(4):
                        mm = pe.transpose(PS[:, st["tr_bank"][t][b], j * P:(j + 1) * P],
                                          Y[:, t, (4 * b + j) * P:(4 * b + j + 1) * P], ident[:])
                    mm.then_inc(tr_ok, 1)

            def embeddings_t(st):
                pe.wait_ge(ple["in"], 32 * (st["n"] + 1))
                for b in range(3):
                    for j in range(4 if b < 2 else 2):
                        t, kb = (j, b) if b < 2 else (PT, j)
                        mm = pe.transpose(PS[:, 1 + b, j * P:(j + 1) * P], p_raw[:, t, kb * P:(kb + 1) * P], ident[:])
                    mm.then_inc(ple["tr"], 1)

            def rows_in_pass(st):
                return 0 if st["k"] == 0 else 2

            def last_pass(st, src, head, before):
                def with_rows(t, c):
                    if st["pre"] is not None and c == head and t >= TILES - rows_in_pass(st):
                        rows_t(st, t + rows_in_pass(st) - TILES)
                    if before:
                        before(t, c)
                p = st["passes"][-1]
                column_pass(p, p["i"], src, head, with_rows)

            def tail(st):
                if st["pre"] is not None:
                    for t in range(rows_in_pass(st), 3 if st["early"] else TILES):
                        rows_t(st, t)

            def mixed_out(st):
                n = st["before"] * TILES
                split = lambda t, c: pe.wait_ge(ot_lo, n + t + 1) if c == 0 else None
                column_pass(st["passes"][6], st["passes"][6]["i"], XT, HEAD, split)
                last_pass(st, XT, 1, split)

            pe.wait_ge(const_ok, 5)
            for st in stages:
                if st["kind"] in ("ab", "mla"):
                    pe.wait_ge(exact_ok, 2)
                xt_ready = 2 * TILES * (st["k"] - 1)
                if st["kind"] == "ffn":
                    b0, i0 = st["n"] * 2 * FB, st["passes"][0]["i"]
                    prev = stages[st["k"] - 1]
                    for fh in range(2):
                        if fh == 0:
                            gate_up(b0, xt_ready, TILES * (i0 + 1), lambda: [rows_t(prev, t) for t in (3, 4)])
                        with pe.Fori(1 - fh, FB) as fb:
                            gate_up(fb + (fh * FB + b0), xt_ready, (fh * 2 + i0) * TILES + TILES)
                        done = (fh * FB + b0 + FB) * 2

                        def hidden(t, c):
                            if c == 0 and t == 0:
                                pe.wait_ge(sg_free, done)
                            if c == 0 and t == 1:
                                pe.wait_ge(silu_ok, done + 2)
                            if c == 0 and t == 3:
                                pe.wait_ge(h_mul, done + 2)
                            if c == FB - 1 and t == 0:
                                pe.wait_ge(sg_free, done + 2)

                        if fh == 0:
                            with pe.Fori(0, 2) as nh:
                                column_pass(st["passes"][0], nh + i0, HT, HEAD, hidden)
                        else:
                            column_pass(st["passes"][2], i0 + 2, HT, HEAD, hidden)
                            if st["to_ple"]:
                                embeddings_t(st["next"])
                            last_pass(st, HT, HEAD, None)
                            if st["to_ple"]:
                                p = st["next"]["passes"][0]
                                column_pass(p, p["i"], PTT, 1, lambda t, c: pe.wait_ge(
                                    xt_lo_ok, 2 * (TILES * st["k"] + 2)) if t == 0 and c == 0 else None)
                elif st["kind"] == "ple":
                    p = st["passes"][1]
                    column_pass(p, p["i"], PTT, 1)
                    p = st["passes"][2]
                    column_pass(p, p["i"], XT, HEAD, lambda t, c: pe.wait_ge(xt_lo_ok, xt_ready + 2 * (t + 1)) if c == 0 else None)
                    last_pass(st, XT, 1, None)
                elif st["kind"] == "ab":
                    ps = st["passes"]
                    stage_of = {1: 0, 2: 1, 4: 2, 5: 3}

                    def staged(q):
                        def before(t, c):
                            if c:
                                return
                            if q == 0:
                                pe.wait_ge(xt_lo_ok, xt_ready + 2 * max(t + 1, 2))
                            if q in stage_of:
                                n = stage_of[q] * TILES + t
                                if stage_of[q] < 2:
                                    pe.wait_ge(y_out, evicted(ps[q - 1]["i"], t))
                                else:
                                    pe.wait_ge(rope_ok, 2 * (n - 2 * TILES) + 2)
                                if n >= 2:
                                    pe.wait_ge(st_cp, n - 1)
                                for j in range(4):
                                    mm = pe.transpose(PS[:, T_BANK[n % 2], j * P:(j + 1) * P],
                                                      rows_in[:, t, j * P:(j + 1) * P], ident[:])
                                mm.then_inc(st_tr, 1)
                        return before

                    for q in range(6):
                        column_pass(ps[q], ps[q]["i"], XT, HEAD, staged(q))
                    pe.wait_ge(st_cp, 4 * TILES)
                    pe.wait_ge(y_out, evicted(ps[5]["i"], TILES - 1))
                    stick_pe(stick[st["stick0"]:st["stick1"]])
                    soft_pe(soft[st["soft0"]:st["soft1"]])
                    for h in range(DF_HEADS + 1):
                        pe.wait_ge(sub_sq, min(h + 1, DF_HEADS))
                        cols, _ = sub_part(sub_sq_buf, h)
                        pe.matmul(PS[:, h, :], const("neg_ones"), cols, start=True, stop=True).then_inc(sub_mm, 1)
                    mixed_out(st)
                elif st["kind"] == "mla":
                    ps = st["passes"]
                    for q in range(2):
                        column_pass(ps[q], ps[q]["i"], XT, HEAD, lambda t, c: pe.wait_ge(xt_lo_ok, xt_ready + 2 * max(t + 1, 2))
                                    if c == 0 and q == 0 else None)
                    pe.wait_ge(y_out, evicted(ps[1]["i"], TILES - 1))
                    for t in range(TILES):
                        pe.wait_ge(mc_n, TILES + t + 1)
                        pe.wait_ge(rope_ok, 2 * (st["rot0"] + t) + 2)
                        if t >= 2:
                            pe.wait_ge(mc_lo, t - 1)
                            pe.wait_ge(mc_lat, 2 * (t - 1))
                        b0, b1 = TR_BANK[t]
                        for j in range(3):
                            pe.transpose(PS[:, b0, j * P:(j + 1) * P], c_in[:, t, j * P:(j + 1) * P], ident[:])
                        for j in range(2):
                            pe.transpose(PS[:, b1, j * P:(j + 1) * P], c_in[:, t, Q_LORA + j * P:Q_LORA + (j + 1) * P],
                                         ident[:])
                        mm = pe.transpose(PS[0:QD, b1, 2 * P:3 * P], c_in[:, t, MLA_IN - QD:MLA_IN], ident[:])
                        if t == PT:
                            mm = pe.transpose(PS[0:ROPE, b1, 3 * P:4 * P], c_in[:, t, MLA_IN - ROPE:MLA_IN], ident[:])
                        mm.then_inc(mc_tr, 1)
                    pe.wait_ge(muv_in[0], 16)
                    for n in range(2 * PT):
                        if n % 2 == 0:
                            pe.wait_ge(mc_lat, n + 2)
                        if n >= 2:
                            pe.wait_ge(v_ok, n - 1)
                        for c in range(2):
                            mm = pe.matmul(PS[:, S_BANK[n % 2], :], lat_t[:, c, tok(n // 2)],
                                           W_uv[0][:, c, (n % 2) * HALF:(n % 2 + 1) * HALF], start=c == 0, stop=c == 1)
                        mm.then_inc(v_mm, 1)

                    def heads_t(g, t):
                        n = g * TILES + t
                        pe.wait_ge(rope_ok, 2 * (st["rot0"] + TILES + n) + 2)
                        if n >= 2:
                            pe.wait_ge(mq_cp, n - 1)
                        for j in range(4):
                            mm = pe.transpose(PS[0:QD, T_BANK[n % 2], j * P:(j + 1) * P],
                                              q_rows[:, t, j * QD:(j + 1) * QD], ident[:])
                        if t == PT:
                            if g > 0:
                                pe.wait_ge(qr_cp, 4 * g)
                            for j in range(4):
                                mm = pe.transpose(PS[0:ROPE, 3, j * P:(j + 1) * P],
                                                  q_rows[:, t, j * QD + NOPE:(j + 1) * QD], ident[:])
                        mm.then_inc(mq_tr, 1)

                    for g in range(4):
                        def before(t, c, g=g):
                            if c == 0 and g > 0:
                                heads_t(g - 1, t)
                            if c == 0 and g == 0:
                                pe.wait_ge(mc_lo, t + 1)
                                if t == 0:
                                    pe.wait_ge(v_ok, 2 * PT)
                        column_pass(ps[2 + g], ps[2 + g]["i"], CQT, 2, before)
                    for t in range(TILES):
                        heads_t(3, t)
                    pe.wait_ge(mq_cp, 4 * TILES)
                    pe.wait_ge(qr_cp, 4 * 4)
                    pe.wait_ge(mw_in, 16)
                    for n in range(MLA_HEADS + 1):
                        if n < MLA_HEADS:
                            if n >= 2:
                                pe.wait_ge(wt_cp, n - 1)
                            for c in range(2):
                                mm = pe.transpose(PS[0:NOPE, T_BANK[n % 2], c * P:(c + 1) * P],
                                                  W_uk[:, c, n * NOPE:(n + 1) * NOPE], ident[:])
                            mm.then_inc(wt_tr, 1)
                        if n >= 1:
                            h = n - 1
                            pe.wait_ge(wt_cp, h + 1)
                            if h >= 2:
                                pe.wait_ge(ql_cp, 2 * (h - 1))
                            for c in range(2):
                                mm = pe.matmul(PS[:, S_BANK[h % 2], c * P:(c + 1) * P], w_ukt[0:NOPE, h % 2, c * P:(c + 1) * P],
                                               q_t[0:NOPE, h, PROMPT:TOK], start=c == 0, stop=True, skip_group_check=True)
                            mm.then_inc(ql_mm, 1)
                    pe.wait_ge(ql_cp, 2 * MLA_HEADS)
                    pe.wait_ge(krt_cp, 2)
                    soft_pe(soft[st["soft0"]:st["soft1"]])
                    pe.wait_ge(muv_in[1], 16)
                    pe.wait_ge(o_out, groups_end(st))
                    for h in range(MLA_HEADS):
                        out = PS[VD * (h % 2):VD * (h % 2) + VD, S_BANK[h // 8], (h // 2 % 4) * P:(h // 2 % 4 + 1) * P]
                        for c in range(2):
                            mm = pe.matmul(out, W_uv[1][:, c, h * VD:(h + 1) * VD],
                                           OLT[:, :, h // 8, c, (h % 8) * DEC_T:(h % 8 + 1) * DEC_T],
                                           start=c == 0, stop=c == 1, skip_group_check=True)
                        if h % 8 == 7:
                            mm.then_inc(uo_mm, 1)
                    mixed_out(st)
                tail(st)


_INS = ["x_prompt", "x_sample", "p_prompt", "p_sample", "cache_sb_k", "cache_sb_v", "cache_df_k", "cache_df_v",
        "cache_mla_latent", "cache_mla_krope", "norms", "ffn1_gu", "ffn1_dn", "ffn2_gu", "ffn2_dn", "ple_in",
        "ple_gate", "ab_in", "ab_out", "df_lambda", "df_subln", "mla_in", "mla_q_norm", "mla_kv_norm", "mla_uq",
        "mla_uk", "mla_uv", "mla_out"]


_NEW_ROWS = {"sb_k": (SB_HEADS, HD), "sb_v": (SB_HEADS, HD), "df_k": (DF_HEADS, 2, HD), "df_v": (DF_HEADS, 2 * HD),
             "lat": (KV_LORA,), "kr": (ROPE,)}


def build(nc, io, outs, plan):
    io = dict(io, plan=plan)
    xp, xs = io["x_prompt"][0].rearrange("(t p) d -> t p d", p=P), io["x_sample"].rearrange("b t d -> (b t) d")
    yp, ys = outs[0][0].rearrange("(t p) d -> t p d", p=P), outs[1].rearrange("b t d -> (b t) d")
    io["x_tiles"] = [xp[t] for t in range(PT)] + [xs]
    io["y_tiles"] = [yp[t] for t in range(PT)] + [ys]
    io["p_prompt"] = [io["p_prompt"][l, 0].rearrange("(t p) d -> p t d", p=P) for l in range(DEPTH)]
    io["p_sample"] = [io["p_sample"][l].rearrange("b t d -> (b t) d") for l in range(DEPTH)]
    n = len(_NEW_ROWS)
    for i, name in enumerate(_NEW_ROWS):
        pr, sa = outs[2 + i][0, 0], outs[2 + n + i][0]
        f = " ".join("xyz"[:len(pr.shape) - 1])
        io[name + "_out"] = (pr.rearrange(f"(t p) {f} -> p t ({f})", p=P), sa.rearrange(f"b t {f} -> (b t) ({f})"))
    encoder(nc, io)
PLAN = [("ffn", 0, 1), ("ab", 0, 0), ("ffn", 0, 2), ("ple", 0, 0), ("ffn", 1, 1), ("mla", 1, 0), ("ffn", 1, 2), ("ple", 1, 0)]
_OUTS = [((1, PROMPT, D), "float32"), ((DEC_B, DEC_T, D), "float32")]
_OUTS += [(lead + row, "float32") for lead in ((1, 1, PROMPT), (1, DEC_B, DEC_T)) for row in _NEW_ROWS.values()]


def kernel(**inputs):
    import numpy as _np
    import concourse.bacc as _bacc
    from concourse import mybir as _mybir
    from concourse.bass_utils import run_bass_kernel_spmd as _run

    nc = _bacc.Bacc("TRN2", target_bir_lowering=False, num_devices=1)
    arrays, io, outs = {}, {}, []
    for name in _INS:
        a = _np.ascontiguousarray(inputs[name])
        arrays[f"in_{name}"] = a
        io[name] = nc.dram_tensor(f"in_{name}", a.shape, _mybir.dt.from_np(a.dtype), kind="ExternalInput").ap()
    arrays["in_consts"] = const_table()
    io["consts"] = nc.dram_tensor("in_consts", arrays["in_consts"].shape, _mybir.dt.float32, kind="ExternalInput").ap()
    for i, (shape, dtype) in enumerate(_OUTS):
        outs.append(nc.dram_tensor(f"out_{i}", shape, _mybir.dt.from_np(_np.dtype(dtype)), kind="ExternalOutput").ap())
    build(nc, io, outs, PLAN)
    r = _run(nc, [arrays], core_ids=[0])
    return tuple(r.results[0][f"out_{i}"] for i in range(len(_OUTS)))
```
